# Optimizing a Trainium2 kernel written in Bass

```python
import jax, jax.numpy as jnp
from jax import lax
import numpy as np

D_MODEL = 2048
BATCH = 1
SEQ = 256
DEPTH = 1

CHUNK = 64
HEAD_DIM = 128
D_MIX = D_MODEL
W_A = 6 * HEAD_DIM
W_B = 6 * HEAD_DIM
N_POOL_GROUPS = 4
POOL_WINDOWS = (2, 4, 8, 16)
G_C = HEAD_DIM
W_C = N_POOL_GROUPS * G_C
D_IN_TOT = 3 * W_A + 2 * W_B + W_C
K_SHORT = 3
K_CONFORMER = 31
K_FFN = 3
D_FF = 5632
RMS_EPS = 1e-6
LN_EPS = 1e-5


def rms_norm(x, g):
    xf = x.astype(jnp.float32)
    y = xf * lax.rsqrt(jnp.mean(xf * xf, axis=-1, keepdims=True) + RMS_EPS)
    return (y * g.astype(jnp.float32)).astype(x.dtype)

def layer_norm(x, g, b):
    xf = x.astype(jnp.float32)
    mu = jnp.mean(xf, axis=-1, keepdims=True)
    var = jnp.mean(jnp.square(xf - mu), axis=-1, keepdims=True)
    y = (xf - mu) * lax.rsqrt(var + LN_EPS)
    return (y * g.astype(jnp.float32) + b.astype(jnp.float32)).astype(x.dtype)

def causal_depthwise_conv(x, w):
    k, c = w.shape
    return lax.conv_general_dilated(
        x, w[:, None, :].astype(x.dtype),
        window_strides=(1,), padding=[(k - 1, 0)],
        dimension_numbers=("NWC", "WIO", "NWC"),
        feature_group_count=c)

def trailing_mean_minus_self(x, window):
    s = x.shape[1]
    xf = x.astype(jnp.float32)
    c = jnp.cumsum(xf, axis=1)
    c_shift = jnp.pad(c, ((0, 0), (window, 0), (0, 0)))[:, :s]
    counts = jnp.minimum(jnp.arange(1, s + 1, dtype=jnp.float32), float(window))[None, :, None]
    return ((c - c_shift) / counts - xf).astype(x.dtype)

def short_gated_conv_mixer(u_a, conv_w):
    b_gate, c_gate, v = jnp.split(u_a, 3, axis=-1)
    return b_gate * causal_depthwise_conv(c_gate * v, conv_w)

def conformer_conv_mixer(u_b, conv_w, conv_b, ln_g, ln_b):
    val, gate = jnp.split(u_b, 2, axis=-1)
    glu = val * jax.nn.sigmoid(gate)
    y = causal_depthwise_conv(glu, conv_w) + conv_b
    y = layer_norm(y, ln_g, ln_b)
    return jax.nn.silu(y)

def multiscale_pool_mixer(u_c, pool_w, pool_scale):
    bsz, s, _ = u_c.shape
    groups = u_c.reshape(bsz, s, N_POOL_GROUPS, G_C)
    pooled = jnp.stack(
        [trailing_mean_minus_self(groups[:, :, gi], w) for gi, w in enumerate(POOL_WINDOWS)],
        axis=2)
    mixed = jnp.einsum("bsgc,gcd->bsgd", pooled, pool_w)
    return mixed.reshape(bsz, s, W_C) * pool_scale

def conv_gated_mlp(h, w_up, conv_w, conv_b, w_down):
    up = h @ w_up
    up = causal_depthwise_conv(up, conv_w) + conv_b
    gate, val = jnp.split(up, 2, axis=-1)
    return (jax.nn.silu(gate) * val) @ w_down

def first_inputs(seed: int = 0) -> dict:
    key = jax.random.key(seed)
    ks = jax.random.split(key, 20)
    f32 = jnp.float32
    nrm = lambda k, shape, scale: jax.random.normal(k, shape, f32) * scale
    gain = lambda k, shape: 1.0 + 0.05 * jax.random.normal(k, shape, f32)
    return {
        "x": jax.random.normal(ks[0], (BATCH, SEQ, D_MODEL), f32),
        "norm_mix_pre": gain(ks[1], (DEPTH, D_MODEL)),
        "norm_mix_post": gain(ks[2], (DEPTH, D_MODEL)),
        "norm_ffn_pre": gain(ks[3], (DEPTH, D_MODEL)),
        "norm_ffn_post": gain(ks[4], (DEPTH, D_MODEL)),
        "w_in": nrm(ks[5], (DEPTH, D_MODEL, D_IN_TOT), D_MODEL ** -0.5),
        "conv_a_w": nrm(ks[6], (DEPTH, K_SHORT, W_A), K_SHORT ** -0.5),
        "conv_b_w": nrm(ks[7], (DEPTH, K_CONFORMER, W_B), K_CONFORMER ** -0.5),
        "conv_b_bias": nrm(ks[8], (DEPTH, W_B), 0.01),
        "ln_b_gain": gain(ks[9], (DEPTH, W_B)),
        "ln_b_bias": nrm(ks[10], (DEPTH, W_B), 0.01),
        "pool_w": nrm(ks[11], (DEPTH, N_POOL_GROUPS, G_C, G_C), G_C ** -0.5),
        "pool_scale": 1.0 + 0.1 * jax.random.normal(ks[12], (DEPTH, W_C), f32),
        "w_out": nrm(ks[13], (DEPTH, D_MIX, D_MODEL), D_MIX ** -0.5),
        "w_up": nrm(ks[14], (DEPTH, D_MODEL, 2 * D_FF), D_MODEL ** -0.5),
        "conv_ffn_w": nrm(ks[15], (DEPTH, K_FFN, 2 * D_FF), K_FFN ** -0.5),
        "conv_ffn_bias": nrm(ks[16], (DEPTH, 2 * D_FF), 0.01),
        "w_down": nrm(ks[17], (DEPTH, D_FF, D_MODEL), D_FF ** -0.5),
    }

def first_block(x, norm_mix_pre, norm_mix_post, norm_ffn_pre, norm_ffn_post,
              w_in, conv_a_w, conv_b_w, conv_b_bias, ln_b_gain, ln_b_bias,
              pool_w, pool_scale, w_out, w_up, conv_ffn_w, conv_ffn_bias, w_down):
    for l in range(DEPTH):
        h = rms_norm(x, norm_mix_pre[l])
        u = h @ w_in[l]
        u_a = u[..., :3 * W_A]
        u_b = u[..., 3 * W_A:3 * W_A + 2 * W_B]
        u_c = u[..., 3 * W_A + 2 * W_B:]
        y_a = short_gated_conv_mixer(u_a, conv_a_w[l])
        y_b = conformer_conv_mixer(u_b, conv_b_w[l], conv_b_bias[l], ln_b_gain[l], ln_b_bias[l])
        y_c = multiscale_pool_mixer(u_c, pool_w[l], pool_scale[l])
        y = jnp.concatenate([y_a, y_b, y_c], axis=-1) @ w_out[l]
        x = x + rms_norm(y, norm_mix_post[l])
        h = rms_norm(x, norm_ffn_pre[l])
        f = conv_gated_mlp(h, w_up[l], conv_ffn_w[l], conv_ffn_bias[l], w_down[l])
        x = x + rms_norm(f, norm_ffn_post[l])
    return x


M_HEADS = 4
M_HEAD_DIM = 256
M_WIDTH = M_HEADS * M_HEAD_DIM
M_CHUNK = 128
CONV_WIDTH = 4
A_HEADS = 8
A_HEAD_DIM = 128
A_WIDTH = A_HEADS * A_HEAD_DIM
MOBA_BLOCK = 256
MOBA_TOPK = 3
Q_BLOCK = 128
ROPE_THETA = 10000.0
D_FF_2 = 4 * D_MODEL
NORM_EPS = 1e-6

SPLITS = (M_WIDTH, M_WIDTH, M_WIDTH, M_WIDTH, M_HEADS, M_HEADS,
          A_WIDTH, A_WIDTH, A_WIDTH, D_MODEL, D_MODEL)
IN_COLS = 4 * M_WIDTH + 2 * M_HEADS + 3 * A_WIDTH + 2 * D_MODEL


def rmsnorm(x, w):
    xf = x.astype(jnp.float32)
    y = xf * lax.rsqrt(jnp.mean(xf * xf, axis=-1, keepdims=True) + NORM_EPS)
    return (y * w.astype(jnp.float32)).astype(x.dtype)

def split_cols(u):
    outs, start = [], 0
    for width in SPLITS:
        outs.append(u[..., start:start + width])
        start += width
    return outs

def to_heads(u, n_heads):
    B, S, C = u.shape
    return u.reshape(B, S, n_heads, C // n_heads).transpose(0, 2, 1, 3)

def causal_depthwise_conv_2(u, w, b):
    S = u.shape[1]
    up = jnp.pad(u, ((0, 0), (CONV_WIDTH - 1, 0), (0, 0)))
    out = b
    for j in range(CONV_WIDTH):
        out = out + w[j] * up[:, j:j + S]
    return out

def apply_rope(x, positions):
    D = x.shape[-1]
    inv_freq = 1.0 / (ROPE_THETA ** (jnp.arange(0, D, 2, dtype=jnp.float32) / D))
    ang = positions.astype(jnp.float32)[..., None] * inv_freq
    ang = jnp.concatenate([ang, ang], axis=-1)[:, None]
    xf = x.astype(jnp.float32)
    x1, x2 = xf[..., :D // 2], xf[..., D // 2:]
    rot = jnp.concatenate([-x2, x1], axis=-1)
    return (xf * jnp.cos(ang) + rot * jnp.sin(ang)).astype(x.dtype)

def mlstm_chunkwise(q, k, v, i_pre, f_pre):
    B, H, S, D = q.shape
    L = M_CHUNK
    NC = S // L
    f32 = jnp.float32
    q = q.astype(f32).reshape(B, H, NC, L, D)
    k = (k.astype(f32) * (D ** -0.5)).reshape(B, H, NC, L, D)
    v = v.astype(f32).reshape(B, H, NC, L, D)
    log_f = jax.nn.log_sigmoid(f_pre.astype(f32)).reshape(B, H, NC, L)
    log_i = i_pre.astype(f32).reshape(B, H, NC, L)
    b = jnp.cumsum(log_f, axis=-1)
    F = b[..., -1]

    w = F[..., None] - b + log_i
    m_loc = jnp.max(w, axis=-1)
    e = jnp.exp(w - m_loc[..., None])
    C_loc = jnp.einsum('bhclv,bhclk->bhcvk', v * e[..., None], k)
    n_loc = jnp.einsum('bhcl,bhclk->bhck', e, k)

    def step(carry, xs):
        C, n, m = carry
        Fc, Cl, nl, ml = xs
        m_new = jnp.maximum(Fc + m, ml)
        a = jnp.exp(Fc + m - m_new)
        g = jnp.exp(ml - m_new)
        C_new = a[..., None, None] * C + g[..., None, None] * Cl
        n_new = a[..., None] * n + g[..., None] * nl
        return (C_new, n_new, m_new), (C, n, m)

    init = (jnp.zeros((B, H, D, D), f32), jnp.zeros((B, H, D), f32), jnp.zeros((B, H), f32))
    xs = (jnp.moveaxis(F, 2, 0), jnp.moveaxis(C_loc, 2, 0),
          jnp.moveaxis(n_loc, 2, 0), jnp.moveaxis(m_loc, 2, 0))
    _, (C_prev, n_prev, m_prev) = lax.scan(step, init, xs)
    C_prev = jnp.moveaxis(C_prev, 0, 2)
    n_prev = jnp.moveaxis(n_prev, 0, 2)
    m_prev = jnp.moveaxis(m_prev, 0, 2)

    a_log = b + m_prev[..., None]
    d_log = b[..., :, None] - b[..., None, :] + log_i[..., None, :]
    causal = jnp.tril(jnp.ones((L, L), dtype=bool))
    d_log = jnp.where(causal, d_log, -jnp.inf)
    m_t = jnp.maximum(a_log, jnp.max(d_log, axis=-1))
    s_ts = jnp.einsum('bhctd,bhcsd->bhcts', q, k) * jnp.exp(d_log - m_t[..., None])
    inter = jnp.exp(a_log - m_t)
    num = (inter[..., None] * jnp.einsum('bhcvk,bhctk->bhctv', C_prev, q)
           + jnp.einsum('bhcts,bhcsv->bhctv', s_ts, v))
    den = inter * jnp.einsum('bhck,bhctk->bhct', n_prev, q) + jnp.sum(s_ts, axis=-1)
    h = num / jnp.maximum(jnp.abs(den), jnp.exp(-m_t))[..., None]
    return h.reshape(B, H, S, D)

def moba_attention(q, k, v):
    B, H, S, D = q.shape
    BS = MOBA_BLOCK
    NB = -(-S // BS)
    K_SEL = min(MOBA_TOPK, NB)
    pad = NB * BS - S
    kp = jnp.pad(k, ((0, 0), (0, 0), (0, pad), (0, 0))).reshape(B, H, NB, BS, D)
    vp = jnp.pad(v, ((0, 0), (0, 0), (0, pad), (0, 0))).reshape(B, H, NB, BS, D)
    k_mean = jnp.mean(kp.astype(jnp.float32), axis=3)
    scale = D ** -0.5
    NQB = S // Q_BLOCK
    blk_ids = jnp.arange(NB)
    b_idx = jnp.arange(B)[:, None, None, None]
    h_idx = jnp.arange(H)[None, :, None, None]
    n_sel = K_SEL * BS

    def one_block(qb):
        start = qb * Q_BLOCK
        qf = lax.dynamic_slice_in_dim(q, start, Q_BLOCK, axis=2).astype(jnp.float32)
        own = start // BS
        gate = jnp.einsum('bhqd,bhnd->bhqn', qf, k_mean)
        gate = jnp.where(blk_ids < own, gate, -jnp.inf)
        _, sel = lax.top_k(gate, K_SEL)
        valid = jnp.arange(K_SEL) < own
        k_sel = kp[b_idx, h_idx, sel].astype(jnp.float32)
        v_sel = vp[b_idx, h_idx, sel].astype(jnp.float32)
        s_sel = jnp.einsum('bhqd,bhqnkd->bhqnk', qf, k_sel) * scale
        s_sel = jnp.where(valid[:, None], s_sel, -jnp.inf).reshape(B, H, Q_BLOCK, n_sel)
        k_own = lax.dynamic_index_in_dim(kp, own, axis=2, keepdims=False).astype(jnp.float32)
        v_own = lax.dynamic_index_in_dim(vp, own, axis=2, keepdims=False).astype(jnp.float32)
        s_own = jnp.einsum('bhqd,bhkd->bhqk', qf, k_own) * scale
        q_pos = start + jnp.arange(Q_BLOCK)
        k_pos = own * BS + jnp.arange(BS)
        s_own = jnp.where(k_pos[None, :] <= q_pos[:, None], s_own, -jnp.inf)
        p = jax.nn.softmax(jnp.concatenate([s_sel, s_own], axis=-1), axis=-1)
        o = (jnp.einsum('bhqm,bhqmd->bhqd', p[..., :n_sel],
                        v_sel.reshape(B, H, Q_BLOCK, n_sel, D))
             + jnp.einsum('bhqk,bhkd->bhqd', p[..., n_sel:], v_own))
        return o.astype(q.dtype)

    out = lax.map(one_block, jnp.arange(NQB))
    return jnp.moveaxis(out, 0, 2).reshape(B, H, S, D)

def second_inputs(seed: int = 0) -> dict:
    key = jax.random.key(seed)
    ks = jax.random.split(key, 16)
    f32 = jnp.float32

    def gain(k, n):
        return 1.0 + 0.05 * jax.random.normal(k, (DEPTH, n), f32)

    def dense(k, fan_in, fan_out):
        return jax.random.normal(k, (DEPTH, fan_in, fan_out), f32) * (fan_in ** -0.5)

    x = jax.random.normal(ks[0], (BATCH, SEQ, D_MODEL), f32)
    positions = jnp.broadcast_to(jnp.arange(SEQ, dtype=jnp.int32), (BATCH, SEQ))
    f_bias = (jnp.linspace(3.0, 6.0, M_HEADS, dtype=f32)[None, :]
              + 0.1 * jax.random.normal(ks[6], (DEPTH, M_HEADS), f32))
    return {
        'x': x,
        'positions': positions,
        'norm_mix_pre': gain(ks[1], D_MODEL),
        'w_in': dense(ks[2], D_MODEL, IN_COLS),
        'conv_w': jax.random.normal(ks[3], (DEPTH, CONV_WIDTH, 2 * M_WIDTH), f32) * (CONV_WIDTH ** -0.5),
        'conv_b': 0.01 * jax.random.normal(ks[4], (DEPTH, 2 * M_WIDTH), f32),
        'i_bias': 0.1 * jax.random.normal(ks[5], (DEPTH, M_HEADS), f32),
        'f_bias': f_bias,
        'mlstm_norm': gain(ks[7], M_WIDTH),
        'w_branch_m': dense(ks[8], M_WIDTH, D_MODEL),
        'w_branch_a': dense(ks[9], A_WIDTH, D_MODEL),
        'w_out': dense(ks[10], D_MODEL, D_MODEL),
        'norm_mix_post': gain(ks[11], D_MODEL),
        'norm_ffn_pre': gain(ks[12], D_MODEL),
        'w_up': dense(ks[13], D_MODEL, D_FF_2),
        'w_down': dense(ks[14], D_FF_2, D_MODEL),
        'norm_ffn_post': gain(ks[15], D_MODEL),
    }

def second_block(x, positions, norm_mix_pre, w_in, conv_w, conv_b, i_bias, f_bias, mlstm_norm,
              w_branch_m, w_branch_a, w_out, norm_mix_post, norm_ffn_pre, w_up, w_down,
              norm_ffn_post):
    dt = x.dtype
    B, S, _ = x.shape
    for l in range(DEPTH):
        xn = rmsnorm(x, norm_mix_pre[l])
        proj = jnp.einsum('bsd,dc->bsc', xn, w_in[l])
        mq, mk, mv, mo, mi, mf, aq, ak, av, g_m, g_a = split_cols(proj)

        qk = jax.nn.silu(causal_depthwise_conv_2(jnp.concatenate([mq, mk], axis=-1),
                                               conv_w[l], conv_b[l]))
        mq_h = to_heads(qk[..., :M_WIDTH], M_HEADS)
        mk_h = to_heads(qk[..., M_WIDTH:], M_HEADS)
        mv_h = to_heads(mv, M_HEADS)
        i_pre = jnp.transpose(mi + i_bias[l], (0, 2, 1))
        f_pre = jnp.transpose(mf + f_bias[l], (0, 2, 1))
        h = mlstm_chunkwise(mq_h, mk_h, mv_h, i_pre, f_pre)
        h = h * lax.rsqrt(jnp.mean(h * h, axis=-1, keepdims=True) + NORM_EPS)
        h = h.transpose(0, 2, 1, 3).reshape(B, S, M_WIDTH) * mlstm_norm[l].astype(jnp.float32)
        h_m = (h * jax.nn.sigmoid(mo.astype(jnp.float32))).astype(dt)

        aq_h = apply_rope(to_heads(aq, A_HEADS), positions)
        ak_h = apply_rope(to_heads(ak, A_HEADS), positions)
        av_h = to_heads(av, A_HEADS)
        o_a = moba_attention(aq_h, ak_h, av_h)
        h_a = o_a.transpose(0, 2, 1, 3).reshape(B, S, A_WIDTH)

        y_m = jnp.einsum('bsc,cd->bsd', h_m, w_branch_m[l])
        y_a = jnp.einsum('bsc,cd->bsd', h_a, w_branch_a[l])
        merged = jax.nn.sigmoid(g_m) * y_m + jax.nn.sigmoid(g_a) * y_a
        mix_out = jnp.einsum('bsd,de->bse', merged, w_out[l])
        x = x + rmsnorm(mix_out, norm_mix_post[l])

        hn = rmsnorm(x, norm_ffn_pre[l])
        u = jnp.square(jax.nn.relu(jnp.einsum('bsd,df->bsf', hn, w_up[l])))
        y = jnp.einsum('bsf,fd->bsd', u, w_down[l])
        x = x + rmsnorm(y, norm_ffn_post[l])
    return x


def setup_inputs(seed=0):
    out = dict(first_inputs(seed))
    for name, value in second_inputs(seed + 1).items():
        if name != "x":
            out[name + "_2"] = value
    return out


def reference(
    x, norm_mix_pre, norm_mix_post, norm_ffn_pre, norm_ffn_post, w_in, conv_a_w, conv_b_w,
    conv_b_bias, ln_b_gain, ln_b_bias, pool_w, pool_scale, w_out, w_up, conv_ffn_w,
    conv_ffn_bias, w_down, positions_2, norm_mix_pre_2, w_in_2, conv_w_2, conv_b_2, i_bias_2,
    f_bias_2, mlstm_norm_2, w_branch_m_2, w_branch_a_2, w_out_2, norm_mix_post_2,
    norm_ffn_pre_2, w_up_2, w_down_2, norm_ffn_post_2,
):
    x = first_block(
        x, norm_mix_pre, norm_mix_post, norm_ffn_pre, norm_ffn_post, w_in, conv_a_w, conv_b_w,
        conv_b_bias, ln_b_gain, ln_b_bias, pool_w, pool_scale, w_out, w_up, conv_ffn_w,
        conv_ffn_bias, w_down,
    )
    return second_block(
        x, positions_2, norm_mix_pre_2, w_in_2, conv_w_2, conv_b_2, i_bias_2, f_bias_2,
        mlstm_norm_2, w_branch_m_2, w_branch_a_2, w_out_2, norm_mix_post_2, norm_ffn_pre_2,
        w_up_2, w_down_2, norm_ffn_post_2,
    )


_drawn_inputs = setup_inputs


def setup_inputs(seed=0):
    import zlib

    import numpy as np

    out = dict(_drawn_inputs(seed))
    spreads = {}
    factors = {'conv_b_bias': 3.851,
     'ln_b_bias': 8.0,
     'conv_ffn_bias': 5.149,
     'conv_b_2': 8.0,
     'i_bias_2': 64.0}
    for name, (base, spread) in spreads.items():
        noise = np.random.default_rng([zlib.crc32(name.encode()), seed]).standard_normal(out[name].shape)
        drawn = base * np.exp(spread * noise) if base else spread * noise
        out[name] = __import__('jax').numpy.asarray(drawn.astype(out[name].dtype))
    for name, factor in factors.items():
        out[name] = (out[name] * factor).astype(out[name].dtype)
    return out
```

```python
def plan(shapes):
    off, at = {}, 0
    for name, n in shapes:
        off[name] = at
        at += n
    return off, at


PARAM_COLUMNS = [
    ("norm_mix_pre", 16), ("norm_mix_post", 16), ("norm_ffn_pre", 16), ("norm_ffn_post", 16),
    ("norm_mix_pre_2", 16), ("norm_mix_post_2", 16), ("norm_ffn_pre_2", 16), ("norm_ffn_post_2", 16),
    ("conv_a_w", 3 * 6), ("conv_b_w", 31 * 6), ("conv_b_bias", 6), ("ln_b_gain", 6), ("ln_b_bias", 6),
    ("pool_scale", 4), ("conv_ffn_w", 3 * 88), ("conv_ffn_bias", 88),
    ("conv_w_2", 4 * 16), ("conv_b_2", 16), ("mlstm_norm_2", 8), ("gate_bias", 2),
    ("pool_w", 4 * 128),
]
CONST_COLUMNS = [
    ("identity", 128), ("ones", 128), ("keep", 128), ("masked", 128), ("select", 4 * 128),
    ("pool_first", 4 * 16), ("inv_freq", 1), ("epsilon", 3), ("half_pi", 1), ("sign", 1),
]


def turn_parts():
    import math

    import numpy as np

    first = 6.28125
    second = math.floor((2 * math.pi - first) * 2.0 ** 20) / 2.0 ** 20
    return first, second, float(np.float32(2 * math.pi - first - second))


class Step:

    def __init__(self, base, i=None, rate=0, terms=()):
        self.base = base
        self.terms = tuple(terms) + (() if i is None else ((i, rate),))

    def plus(self, k):
        return Step(self.base + k, terms=self.terms)

    def times(self, k):
        return Step(self.base * k, terms=tuple((i, r * k) for i, r in self.terms))

    def along(self, i, rate):
        return Step(self.base, i, rate, self.terms)

    def value(self, k=0):
        out = self.base + k
        for i, rate in self.terms:
            out = i * rate + out
        return out

    def slot(self, slots):
        assert all(rate % slots == 0 for _, rate in self.terms)
        return self.base % slots

    def turn(self, slots):
        assert all(rate % slots == 0 for _, rate in self.terms)
        return Step(self.base // slots, terms=tuple((i, rate // slots) for i, rate in self.terms))


def build(nc, xT, params, consts, positions, w_in, w_out, w_up, w_down,
          w_in_2, w_branch_m_2, w_branch_a_2, w_out_2, w_up_2, w_down_2, outT):
    import math
    from contextlib import ExitStack

    import concourse.bass as bass
    from concourse import mybir

    f32, f32r, i32 = mybir.dt.float32, mybir.dt.float32r, mybir.dt.int32
    ALU, ACT, AX = mybir.AluOpType, mybir.ActivationFunctionType, mybir.AxisListType

    T = 256
    D = 2048
    KT = D // 128
    FF1, FF2 = 5632, 8192
    RAW_SLOTS, SPLIT_SLOTS = 4, 4
    PARAM, N_PARAM = plan(PARAM_COLUMNS)
    CONST, N_CONST = plan(CONST_COLUMNS)
    LO_CREDIT = 2 * RAW_SLOTS
    USED_CREDIT = SPLIT_SLOTS
    PAIR_CREDIT = 4

    ctx = ExitStack()
    with ctx:
        top = [(nc.sbuf_base + 31) // 32 * 32]

        def place(name, shape, dtype=f32, at=None):
            size = 4 * math.prod(shape[1:])
            if at is None:
                at = top[0]
                top[0] += (size + 31) // 32 * 32
            return nc.alloc_sbuf_tensor_at(name, shape, dtype, offset=at)

        cursor = [0]

        def put(name, shape):
            at = cursor[0]
            cursor[0] += (4 * math.prod(shape[1:]) + 31) // 32 * 32
            return place(name, shape, at=at)

        def region(size):
            at = top[0]
            top[0] += size
            return at


        raw = place("raw", [128, RAW_SLOTS, 2048])
        w_hi = place("w_hi", [128, SPLIT_SLOTS, 1024], f32r)
        w_lo = place("w_lo", [128, SPLIT_SLOTS, 1024], f32r)
        x = place("x", [128, KT, T])
        h_split = place("h_split", [128, KT, 2 * T], f32r)
        ACT_SPLIT = top[0]
        act_split = place("act_split", [128, KT, 2 * T], f32r)
        par = place("par", [128, N_PARAM])
        con = place("con", [128, N_CONST])
        low = place("low", [128, 2, 2, T])
        scaled = place("scaled", [128, 2, 2, T])
        squares = place("squares", [128, 2, 2, T])
        square_sum = place("square_sum", [128, 2, T])
        gate_pair = place("gate_pair", [128, 2, 2, T])
        diag = place("diag", [128, 2, 128])
        stat = place("stat", [128, 2])
        root = place("root", [128, 2])
        pos_i = place("pos_i", [128, T], i32)
        C = region(32 * 1024)
        assert top[0] <= nc.sbuf_top, (top[0], nc.sbuf_top)

        cursor[0] = C
        glu = put("glu", [128, 6, 30 + T])
        conv_b = put("conv_b", [128, 6, T])
        val_b = put("val_b", [128, 2, T])
        tanh_b = put("tanh_b", [128, 2, T])
        b_gate = put("b_gate", [128, 2, T])
        c_gate = put("c_gate", [128, 2, T])
        cv = put("cv", [128, 2, 2 + T])
        conv_a = put("conv_a", [128, 2, T])
        pool_in = put("pool_in", [128, 2, 16 + T])
        pool_sum = put("pool_sum", [128, 2, 16 + T])
        pooled = put("pooled", [128, 2, T])
        assert cursor[0] <= C + 32 * 1024, cursor[0] - C

        ln_squares = place("ln_squares", [128, 6, T], at=C)
        y = place("y", [128, KT, T], at=C)
        cursor[0] = C + KT * T * 4
        up_in = put("up_in", [128, 2, 2 + T])
        gate_conv = put("gate_conv", [128, 4, T])
        gate_tanh = put("gate_tanh", [128, 4, T])
        val_conv = put("val_conv", [128, 2, T])
        hidden = put("hidden", [128, 2, T])
        assert cursor[0] <= C + 32 * 1024, cursor[0] - C
        cursor[0] = C
        qk_in = put("qk_in", [128, 2, 3 + T])
        q_m = put("q_m", [128, 2, T])
        k_m = put("k_m", [128, 2, T])
        v_m = put("v_m", [128, 2, T])
        o_m = put("o_m", [128, 2, T])
        v_tok = put("v_tok", [128, 2, T])
        decay = put("decay", [128, 384])
        s_ts = put("s_ts", [128, 384])
        den_m = put("den_m", [128, 2, T])
        h_m = put("h_m", [128, 2, T])
        gcol = put("gcol", [128, 2, 4])
        row_g = put("row_g", [4, T])
        row_m = put("row_m", [4, T])
        row_n = put("row_n", [4, T])
        cos = put("cos", [128, T])
        sin = put("sin", [128, T])
        row_i = place("row_i", [4, T], at=cursor[0])
        row_f = place("row_f", [4, T], at=cursor[0] + 4 * T)
        a_q = put("a_q", [128, 2, T])
        a_k = put("a_k", [128, 2, T])
        a_v = put("a_v", [128, 2, T])
        prob_t = put("prob_t", [128, 384])
        a_stat = put("a_stat", [128, 8])
        assert cursor[0] <= C + 32 * 1024, cursor[0] - C
        merged = place("merged", [128, KT, 2 * T], f32r, at=C)
        y_2 = place("y_2", [128, KT, T], at=ACT_SPLIT)
        ps = ctx.enter_context(nc.psum_tensor("ps", [128, 8, 512], f32))

        def P(name, k=0, n=1):
            at = PARAM[name] + k
            return par[:, at:at + n] if isinstance(at, int) else par[:, bass.ds(at, n)]

        def K(name, k=0, n=1):
            return con[:, CONST[name] + k:CONST[name] + k + n]

        identity, ones = K("identity", 0, 128), K("ones", 0, 128)

        def flat(ap):
            return ap.rearrange("p a t -> p (a t)")

        def bcast2(row):
            return row.rearrange("p (a t) -> p a t", a=1).to_broadcast([128, 2, T])

        def sem(name):
            return ctx.enter_context(nc.semaphore(name))

        raw_full = [sem(f"raw_full{i}") for i in range(RAW_SLOTS)]
        hi_ready = sem("hi_ready")
        lo_ready = sem("lo_ready")
        piece_used = sem("piece_used")
        low_ready = sem("low_ready")
        pair_combined = sem("pair_combined")
        x_loaded, small_loaded, pos_loaded, forget_loaded, stored = (
            sem(n) for n in ("x_loaded", "small_loaded", "pos_loaded", "forget_loaded", "stored"))
        cleared = sem("cleared")
        squares_ready = sem("squares_ready")
        squares_added = sem("squares_added")
        stat_summed = sem("stat_summed")
        root_ready = sem("root_ready")
        rsqrt_ready = sem("rsqrt_ready")
        diag_ready = sem("diag_ready")
        bcast_ready = sem("bcast_ready")
        scaled_ready = sem("scaled_ready")
        x_ready = sem("x_ready")
        norm_hi = sem("norm_hi")
        h_ready = sem("h_ready")

        vector_step = sem("vector_step")
        tanh_ready = sem("tanh_ready")
        glu_ready = sem("glu_ready")
        taps_done = sem("taps_done")
        conv_b_ready = sem("conv_b_ready")
        centered = sem("centered")
        ln_squared = sem("ln_squared")
        ln_scaled = sem("ln_scaled")
        ln_affine = sem("ln_affine")
        ln_tanh = sem("ln_tanh")
        ln_silu = sem("ln_silu")
        b_hi = sem("b_hi")
        b_split = sem("b_split")
        cv_ready = sem("cv_ready")
        conv_a_started = sem("conv_a_started")
        a_mixed = sem("a_mixed")
        a_hi = sem("a_hi")
        a_split = sem("a_split")
        pooled_ready = sem("pooled_ready")
        pool_summed = sem("pool_summed")
        c_hi = sem("c_hi")
        c_split = sem("c_split")
        conv_started = sem("conv_started")
        conv_done = sem("conv_done")
        gate_ready = sem("gate_ready")
        units_ready = sem("units_ready")
        unit_hi = sem("unit_hi")
        unit_split = sem("unit_split")
        y_summed = sem("y_summed")
        rows_split = sem("rows_split")
        row_step = sem("row_step")
        rows_ready = sem("rows_ready")
        columns_summed = sem("columns_summed")
        columns_ready = sem("columns_ready")
        angle_ready = sem("angle_ready")
        table_step = sem("table_step")
        qk_started = sem("qk_started")
        qk_convolved = sem("qk_convolved")
        qk_tanh = sem("qk_tanh")
        qk_ready = sem("qk_ready")
        o_ready = sem("o_ready")
        rows_bcast = sem("rows_bcast")
        m_scored = sem("m_scored")
        v_tok_ready = sem("v_tok_ready")
        decay_started = sem("decay_started")
        decay_ready = sem("decay_ready")
        s_ts_ready = sem("s_ts_ready")
        m_valued = sem("m_valued")
        den_ready = sem("den_ready")
        m_divided = sem("m_divided")
        m_squared = sem("m_squared")
        m_gated = sem("m_gated")
        m_hi = sem("m_hi")
        m_split = sem("m_split")
        rope_ready = sem("rope_ready")
        a_scored = sem("a_scored")
        a_v_ready = sem("a_v_ready")
        a_max_ready = sem("a_max_ready")
        a_exp_ready = sem("a_exp_ready")
        prob_ready = sem("prob_ready")
        prob_turned = sem("prob_turned")
        prob_t_ready = sem("prob_t_ready")
        a_valued = sem("a_valued")
        a_hi_2 = sem("a_hi_2")
        a_split_2 = sem("a_split_2")
        merge_tanh = sem("merge_tanh")
        merge_summed = sem("merge_summed")
        merge_hi = sem("merge_hi")
        merge_split = sem("merge_split")

        (N_PRE1, N_LN_MEAN, N_LN_VAR, N_POST1, N_PREF1, N_POSTF1, N_PRE2,
         N_HEAD) = range(8)
        N_POST2, N_PREF2, N_POSTF2 = (N_HEAD + 4 + n for n in range(3))
        SUMMED = {e: n for n, e in enumerate(
            (N_PRE1, N_POST1, N_PREF1, N_POSTF1, N_PRE2, N_POST2, N_PREF2, N_POSTF2))}
        PRE = {e: n for n, e in enumerate((N_PRE1, N_PREF1, N_PRE2, N_PREF2))}
        POST = {e: n for n, e in enumerate((N_POST1, N_POSTF1, N_POST2, N_POSTF2))}
        SCALED = {e: n for n, e in enumerate(
            (N_PRE1, N_POST1, N_PREF1, N_POSTF1, N_PRE2, N_POST2, N_PREF2, N_POSTF2))}

        SUMMED_BEFORE = {e: max((f + 1 for f in SUMMED if f < e), default=0) for e in SUMMED}
        M_STAGE, M_STAGE_END = (0, 3, 7, 9), (2, 5, 9, 11)
        A_STAGE, A_STAGE_END = ((2, 4, 6), (5, 8, 10)), ((3, 5, 7), (7, 9, 11))
        ROUND = 1.5 * 2.0 ** 23
        PI_BELOW = 3.1415925
        TURN_PARTS = turn_parts()

        def at_least(eng, s, value):
            if not isinstance(value, int) or value > 0:
                eng.wait_ge(s, value)

        NARROW, WIDE = 4, 8
        W1 = 0
        O1 = W1 + 17 * NARROW
        M1 = O1 + 4 * WIDE
        GROUPS1 = (4, 4, 3)
        up1, down1, at = [], [], M1
        for n in GROUPS1:
            up1.append(at)
            down1.append(at + n * 2 * WIDE)
            at += n * 2 * WIDE + 4 * (2 * n)
        G2 = at
        W2 = G2 + 2
        Y2 = W2 + 28 * NARROW
        O2 = Y2 + 8 * 12
        M2 = O2 + 4 * WIDE
        END = M2 + 4 * 8 * WIDE
        qW1 = 0
        qO1 = qW1 + 17
        qup1, qdown1, at = [], [], qO1 + 8
        for n in GROUPS1:
            qup1.append(at)
            qdown1.append(at + 4 * n)
            at += 4 * n + 8
        qG2 = at
        qW2 = qG2 + 1
        qY2 = qW2 + 28
        qO2 = qY2 + 8 * 4
        qM2 = qO2 + 8

        CHUNKS1 = [(kind, j) for j in range(3) for kind in ("val", "gate")]
        CHUNKS1 += [(kind, j) for j in range(3) for kind in ("b", "c", "v")]
        CHUNKS1 += [("pool", j) for j in range(2)]
        COLUMN1 = {"b": 0, "c": 768, "v": 1536, "val": 2304, "gate": 3072, "pool": 3840}
        COLUMN2 = {"q": 0, "k": 1024, "v": 2048, "o": 3072, "aq": 4104, "ak": 5128, "av": 6152,
                   "gm": 7176, "ga": 9224}
        CHUNKS2 = [(kind, h) for h in range(4) for kind in ("q", "k", "v", "o")]
        CHUNKS2 += [(kind, j) for j in range(4) for kind in ("aq", "ak", "av")]

        block = ctx.enter_context(nc.Block())

        @block.sync
        def _(sp):
            sp.dma_start(con[:, :], consts).then_inc(small_loaded, 16)
            sp.dma_start(par[:, :], params).then_inc(small_loaded, 16)
            sp.dma_start(x[:, :, :], xT).then_inc(x_loaded, 16)

            def load(n, w, row, col, deep):
                slot, cols = n.slot(RAW_SLOTS), 2048 // deep
                sp.wait_ge(lo_ready, n.times(2).value(2))
                sp.dma_start(raw[:, slot, :].rearrange("p (k n) -> p k n", k=deep),
                             w[row:row + 128 * deep, bass.ds(col, cols)].rearrange("(k p) n -> p k n", p=128)
                             ).then_inc(raw_full[slot], 16)

            for c, (kind, j) in enumerate(CHUNKS1):
                for b in range(2):
                    load(Step(W1 // 2 + 2 * c + b), w_in, 1024 * b, COLUMN1[kind] + 256 * j, 8)
            with sp.Fori(1, 5) as i:
                for b in range(4):
                    load(Step(O1 // 2 + b - 4, i, 4), w_out, 512 * b, i * 512 - 512, 4)
            first = 0
            for g, n in enumerate(GROUPS1):
                with sp.Fori(1, n + 1) as i:
                    for half in range(2):
                        for b in range(4):
                            load(Step(up1[g] // 2 + 4 * half + b - 8, i, 8),
                                 w_up, 512 * b, i * 512 + (FF1 * half + 512 * (first - 1)), 4)
                for i in range(4):
                    for b in range(n):
                        load(Step(down1[g] // 2 + n * i + b), w_down, 512 * (first + b), i * 512, 4)
                first += n
            n = Step(G2 // 2)
            slot = n.slot(RAW_SLOTS)
            sp.wait_ge(lo_ready, n.base * 2 + 2)
            gates = raw[:, slot, :].rearrange("p (k s n) -> p k s n", k=16, s=2)
            for half, s in enumerate((raw_full[slot], forget_loaded)):
                sp.dma_start(gates[:, :, half, :],
                             w_in_2[:, 4096 + 4 * half:4160 + 4 * half].rearrange("(k p) n -> p k n", p=128)
                             ).then_inc(s, 16)
            for c, (kind, j) in enumerate(CHUNKS2):
                for b in range(2):
                    load(Step(W2 // 2 + 2 * c + b), w_in_2, 1024 * b, COLUMN2[kind] + 256 * j, 8)
            with sp.Fori(1, 5) as i:
                for half in range(2):
                    for b, kind in enumerate(("gm", "ga")):
                        for g in range(2):
                            load(Step(Y2 // 2 + 6 * half + 2 * b + g - 12, i, 12),
                                 w_in_2, 1024 * g, i * 512 + (COLUMN2[kind] + 256 * half - 512), 8)
                    for g, w in enumerate((w_branch_m_2, w_branch_a_2)):
                        load(Step(Y2 // 2 + 6 * half + 4 + g - 12, i, 12), w, 0, i * 512 + (256 * half - 512), 8)
            with sp.Fori(1, 5) as i:
                for b in range(4):
                    load(Step(O2 // 2 + b - 4, i, 4), w_out_2, 512 * b, i * 512 - 512, 4)
            for g in range(4):
                with sp.Fori(1, 5) as i:
                    for b in range(4):
                        load(Step(M2 // 2 + 32 * g + b - 4, i, 4), w_up_2, 512 * b, i * 512 + (2048 * g - 512), 4)
                with sp.Fori(1, 5) as i:
                    for b in range(4):
                        load(Step(M2 // 2 + 32 * g + 16 + b - 4, i, 4), w_down_2, 2048 * g + 512 * b, i * 512 - 512, 4)
            for q in range(8):
                sp.wait_ge(x_ready, 8 * POST[N_POSTF2] + q + 1)
                sp.dma_start(outT[:, 2 * q:2 * q + 2, :], x[:, 2 * q:2 * q + 2, :]).then_inc(stored, 16)
            sp.wait_ge(stored, 8 * 16)

        @block.tensor
        def _(pe):
            def piece(n, p, kn, banks, rhs, pieces, need=None):
                slot, across = n.slot(SPLIT_SLOTS), len(banks)
                pe.wait_ge(lo_ready, n.value(LO_CREDIT + 1))
                for kk in range(kn):
                    k = p * kn + kk
                    if need is not None and (k % 2 == 0 or kn == 1):
                        ready, value = need(k)
                        pe.wait_ge(ready, value)
                    for t, bank in enumerate(banks):
                        cols = slice((kk * across + t) * 128, (kk * across + t + 1) * 128)
                        nc.tensor.matmul(ps[:, bank, :], w_hi[:, slot, cols], rhs[:, k, :],
                                         start=(k == 0), stop=False)
                        last = nc.tensor.matmul(ps[:, bank, T:2 * T], w_lo[:, slot, cols], rhs[:, k, 0:T],
                                                start=False, stop=(k == pieces * kn - 1))
                last.then_inc(piece_used, 1)

            def narrow_chunk(n, q, bank, rhs, pieces=4, need=None, between=None):
                pe.wait_ge(pair_combined, q.value(PAIR_CREDIT - 1))
                for p in range(pieces):
                    if between is not None:
                        between(p)
                    piece(n.plus(p), p, 4, (bank, bank + 1), rhs, pieces, need)

            def wide_chunk(n, q, bank, rhs, pieces=8, need=None, after=2, between=None):
                pe.wait_ge(pair_combined, q.value(PAIR_CREDIT - after))
                for p in range(pieces):
                    if between is not None:
                        between(p)
                    piece(n.plus(p), p, 2, range(bank, bank + 4), rhs, pieces, need)

            def sum_tokens(tiles):
                for half in range(2):
                    for i, tile in enumerate(tiles):
                        last = nc.tensor.matmul(ps[:, 6, half:half + 1], tile[:, 128 * half:128 * half + 128],
                                                ones[:, 0:1], start=(i == 0), stop=(i == len(tiles) - 1))
                last.then_inc(stat_summed, 1)

            def broadcast(norm):
                pe.wait_ge(diag_ready, norm + 1)
                for half in range(2):
                    last = nc.tensor.matmul(ps[:, 7, 128 * half:128 * half + 128], ones, diag[:, half, :],
                                            start=True, stop=True)
                last.then_inc(bcast_ready, 1)

            def summed_norm(norm):
                pe.wait_ge(squares_added, 8 * (SUMMED[norm] + 1))
                sum_tokens([square_sum[:, 0, :], square_sum[:, 1, :]])
                broadcast(norm)

            def h_need(norm):
                return lambda k: (h_ready, 8 * PRE[norm] + k // 2 + 1)

            pe.wait_ge(small_loaded, 32)
            pe.sem_inc(piece_used, USED_CREDIT)
            summed_norm(N_PRE1)
            need = h_need(N_PRE1)
            with pe.Fori(0, 7) as i:
                for c in range(2):
                    narrow_chunk(Step(W1 + 4 * c, i, 8), Step(qW1 + c, i, 2), 2 * c, h_split, need=need)

            def layer_norm(c, p):
                if (c, p) == (15, 1):
                    pe.wait_ge(conv_b_ready, 6)
                    sum_tokens([conv_b[:, t, :] for t in range(6)])
                elif (c, p) == (15, 3):
                    broadcast(N_LN_MEAN)
                elif (c, p) == (16, 1):
                    pe.wait_ge(ln_squared, 3)
                    sum_tokens([ln_squares[:, t, :] for t in range(6)])
                elif (c, p) == (16, 3):
                    broadcast(N_LN_VAR)

            for c in range(14, 17):
                narrow_chunk(Step(W1 + 4 * c), Step(qW1 + c), 2 * (c % 2), h_split,
                             between=lambda p: layer_norm(c, p))

            def pool_product(j):
                pe.wait_ge(pooled_ready, j + 1)
                for t in range(2):
                    last = nc.tensor.matmul(ps[:, 4 + j, T * t:T * t + T], P("pool_w", 128 * (2 * j + t), 128),
                                            pooled[:, t, :], start=True, stop=True)
                last.then_inc(pool_summed, 1)

            def mixed(k):
                if k < 6:
                    return a_split, k // 2 + 1
                return (b_split, (k - 6) // 2 + 1) if k < 12 else (c_split, (k - 12) // 2 + 1)

            def pools(p):
                if p == 1:
                    pool_product(0)
                elif p == 5:
                    pool_product(1)

            for c in range(4):
                wide_chunk(Step(O1 + 8 * c), Step(qO1 + 2 * c), 4 * (c % 2), act_split, need=mixed if c == 0 else None,
                           after=2 if c else 0, between=pools if c == 0 else None)
            summed_norm(N_POST1)
            summed_norm(N_PREF1)
            units = 0
            for g, n in enumerate(GROUPS1):
                with pe.Fori(0, n) as i:
                    for half in range(2):
                        wide_chunk(Step(up1[g] + 8 * half, i, 16), Step(qup1[g] + 2 * half, i, 4), 4 * half, h_split,
                                   need=h_need(N_PREF1) if g == 0 and half == 0 else None)
                with pe.Fori(0, 2) as i:
                    for c in range(2):
                        wide_chunk(Step(down1[g] + 2 * n * c, i, 4 * n), Step(qdown1[g] + 2 * c, i, 4), 4 * c,
                                   act_split, pieces=2 * n,
                                   need=(lambda k: (unit_split, units + k // 2 + 1)) if c == 0 else None)
                units += 2 * n
            summed_norm(N_POSTF1)
            summed_norm(N_PRE2)
            pe.wait_ge(pair_combined, PAIR_CREDIT + qG2)
            for p in range(2):
                piece(Step(G2 + p), p, 8, (2,), h_split, 2, h_need(N_PRE2))

            def gate_columns():
                pe.wait_ge(rows_ready, 1)
                for half in range(2):
                    last = nc.tensor.matmul(ps[:, 6, 4 * half:4 * half + 4], row_g[0:4, 128 * half:128 * half + 128],
                                            identity[0:4, 0:4], start=True, stop=True)
                last.then_inc(columns_summed, 1)

            def mlstm(h, stage):
                if stage == 0:
                    pe.wait_ge(columns_ready, 1)
                    pe.wait_ge(qk_ready, 2 * h + 2)
                    pe.wait_ge(pair_combined, PAIR_CREDIT + qW2 + 4 * h + 3)
                    at_least(pe, m_split, h)
                    for r, row in enumerate((row_m, row_n)):
                        last = nc.tensor.matmul(ps[:, 7, T * r:T * r + T], K("select", 128 * h, 128)[0:4, :],
                                                row[0:4, :], start=True, stop=True)
                    last.then_inc(rows_bcast, 1)
                    for s in range(2):
                        out = ps[:, 4, 0:256] if s == 0 else ps[:, 4, 256:384]
                        for t in range(2):
                            nc.tensor.matmul(out, k_m[:, t, 128 * s:128 * s + 128], q_m[:, t, 128 * s:T],
                                             start=(t == 0), stop=(t == 1))
                    for s in range(2):
                        for t in range(2):
                            last = nc.tensor.transpose(ps[:, 5, T * s + 128 * t:T * s + 128 * t + 128],
                                                       v_m[:, t, 128 * s:128 * s + 128], identity)
                    last.then_inc(m_scored, 1)
                elif stage == 1:
                    pe.wait_ge(v_tok_ready, h + 1)
                    pe.wait_ge(s_ts_ready, h + 1)
                    for out, stationary in (((5, 0), lambda s: v_tok[:, s, 0:128]),
                                            ((5, T), lambda s: v_tok[:, s, 128:256]),
                                            ((6, 0), lambda s: ones)):
                        bank, col = out
                        nc.tensor.matmul(ps[:, bank, col:col + T], stationary(0), s_ts[:, 0:256],
                                         start=True, stop=False)
                        last = nc.tensor.matmul(ps[:, bank, col + 128:col + T], stationary(1), s_ts[:, 256:384],
                                                start=False, stop=True)
                    last.then_inc(m_valued, 1)
                elif stage == 2:
                    pe.wait_ge(m_squared, h + 1)
                    sum_tokens([den_m[:, 0, :], den_m[:, 1, :]])
                else:
                    broadcast(N_HEAD + h)

            def attention(j, a, stage):
                t = 2 * j + a
                if stage == 0:
                    pe.wait_ge(rope_ready, 2 * j + 2)
                    pe.wait_ge(pair_combined, PAIR_CREDIT + qW2 + 16 + 3 * j + 3)
                    pe.wait_ge(m_split, 4)
                    at_least(pe, prob_ready, t)
                    at_least(pe, a_v_ready, t)
                    nc.tensor.matmul(ps[:, 4, 0:128], a_q[:, a, 0:128], a_k[:, a, 0:128], start=True, stop=True)
                    nc.tensor.matmul(ps[:, 4, 128:384], a_q[:, a, 128:256], a_k[:, a, :], start=True, stop=True)
                    for s in range(2):
                        last = nc.tensor.transpose(ps[:, 5, 128 * s:128 * s + 128],
                                                   a_v[:, a, 128 * s:128 * s + 128], identity)
                    last.then_inc(a_scored, 1)
                elif stage == 1:
                    pe.wait_ge(prob_ready, t + 1)
                    for s in range(3):
                        last = nc.tensor.transpose(ps[:, 6, 128 * s:128 * s + 128],
                                                   s_ts[:, 128 * s:128 * s + 128], identity)
                    last.then_inc(prob_turned, 1)
                else:
                    pe.wait_ge(prob_t_ready, t + 1)
                    at_least(pe, a_split_2, t)
                    nc.tensor.matmul(ps[:, 7, 0:256], v_tok[:, 0, 0:128], prob_t[:, 0:256], start=True, stop=False)
                    nc.tensor.matmul(ps[:, 7, 128:256], v_tok[:, 0, 128:256], prob_t[:, 256:384],
                                     start=False, stop=True).then_inc(a_valued, 1)

            def inner(piece_number):
                if piece_number == 12:
                    gate_columns()
                for h in range(4):
                    r = piece_number - 16 * (h + 1)
                    if r in M_STAGE:
                        mlstm(h, M_STAGE.index(r))
                for j in range(4):
                    r = piece_number - (64 + 12 * (j + 1))
                    for a in range(2):
                        if r in A_STAGE[a]:
                            attention(j, a, A_STAGE[a].index(r))

            for c in range(28):
                narrow_chunk(Step(W2 + 4 * c), Step(qW2 + c), 2 * (c % 2), h_split,
                             between=lambda p: inner(4 * c + p))

            def merge_chunks(i, between=lambda n: None):
                for half in range(2):
                    n, q = Step(Y2 + 12 * half, i, 24), Step(qY2 + 4 * half, i, 8)
                    narrow_chunk(n, q, 0, h_split, between=lambda p: between(12 * half + p))
                    narrow_chunk(n.plus(4), q.plus(1), 2, h_split, between=lambda p: between(12 * half + 4 + p))
                    narrow_chunk(n.plus(8), q.plus(2), 0, act_split[:, 0:8, :], pieces=2,
                                 between=lambda p: between(12 * half + 8 + p),
                                 need=lambda k: (m_split, 4))
                    narrow_chunk(n.plus(10), q.plus(3), 2, act_split[:, 8:16, :], pieces=2,
                                 between=lambda p: between(12 * half + 10 + p),
                                 need=lambda k: (a_split_2, 8))

            merge_chunks(None, between=lambda n: inner(112 + n))
            with pe.Fori(1, 4) as i:
                merge_chunks(i)
            wide_chunk(Step(O2), Step(qO2), 0, merged, need=lambda k: (merge_split, k // 2 + 1), after=0)
            for c in range(1, 4):
                wide_chunk(Step(O2 + 8 * c), Step(qO2 + 2 * c), 4 * (c % 2), merged)
            summed_norm(N_POST2)
            summed_norm(N_PREF2)
            with pe.Fori(0, 4) as g:
                with pe.Fori(0, 2) as i:
                    for c in range(2):
                        n = Step(M2 + 8 * c, terms=((i, 16), (g, 64)))
                        q = Step(qM2 + 2 * c, terms=((i, 4), (g, 16)))
                        wide_chunk(n, q, 4 * c, h_split, need=h_need(N_PREF2) if c == 0 else None)
                with pe.Fori(0, 2) as i:
                    for c in range(2):
                        n = Step(M2 + 32 + 8 * c, terms=((i, 16), (g, 64)))
                        q = Step(qM2 + 8 + 2 * c, terms=((i, 4), (g, 16)))
                        wide_chunk(n, q, 4 * c, act_split,
                                   need=(lambda k: (unit_split, g * 8 + (22 + k // 2 + 1))) if c == 0 else None)
            summed_norm(N_POSTF2)

        @block.scalar
        def _(act):
            def split(n):
                block_n = Step(n.base // 2, terms=tuple((i, r // 2) for i, r in n.terms))
                slot, half = block_n.slot(RAW_SLOTS), 1024 * (n.base % 2)
                if not half:
                    act.wait_ge(raw_full[slot], block_n.turn(RAW_SLOTS).times(16).value(16))
                act.wait_ge(piece_used, n.value(1))
                nc.scalar.activation(w_hi[:, n.slot(SPLIT_SLOTS), :], raw[:, slot, half:half + 1024],
                                     ACT.Copy).then_inc(hi_ready, 1)

            def low_copy(q, bank, last, tiles=2):
                act.wait_ge(piece_used, last.value(USED_CREDIT + 1))
                act.wait_ge(pair_combined, q.value(PAIR_CREDIT - 1))
                nc.scalar.activation(low[:, q.slot(2), 0:tiles, :], ps[:, bank:bank + tiles, T:2 * T],
                                     ACT.Copy).then_inc(low_ready, 1)

            def combined(q):
                act.wait_ge(pair_combined, q.value(PAIR_CREDIT + 1))

            def square(norm, q, ready, value, source):
                s = 8 * SUMMED[norm] + q
                act.wait_ge(ready, value)
                at_least(act, squares_added, s - 1)
                nc.scalar.activation(squares[:, s % 2, :, :], source[:, 2 * q:2 * q + 2, :],
                                     ACT.Square).then_inc(squares_ready, 1)

            def take_root(norm, channels, times=1):
                act.wait_ge(stat_summed, norm + 1)
                eps = K("epsilon", {1: 0, 2: 2}[times] if norm != N_LN_VAR else 1)
                nc.scalar.activation(root[:, :], ps[:, 6, 0:2], ACT.Sqrt, bias=eps,
                                     scale=times * times / channels).then_inc(root_ready, 1)

            def pre_norm(norm, gain):
                take_root(norm, D)
                for q in range(8):
                    act.wait_ge(scaled_ready, 8 * PRE[norm] + q + 1)
                    for t in range(2):
                        k = 2 * q + t
                        nc.scalar.activation(h_split[:, k, 0:T], scaled[:, q % 2, t, :], ACT.Copy,
                                             scale=P(gain, k)).then_inc(norm_hi, 1)

            act.dma_start(pos_i[:, :], positions.partition_broadcast(128)).then_inc(pos_loaded, 16)
            act.wait_ge(small_loaded, 32)
            for q in range(8):
                square(N_PRE1, q, x_loaded, 16, x)
            for p in range(3):
                split(Step(W1 + p))
            pre_norm(N_PRE1, "norm_mix_pre")

            def finish_conv_b(j):
                act.wait_ge(taps_done, j + 1)
                for t in range(2 * j, 2 * j + 2):
                    nc.scalar.activation(conv_b[:, t, :], conv_b[:, t, :], ACT.Identity, scale=0.5,
                                         bias=P("conv_b_bias", t)).then_inc(conv_b_ready, 1)

            def chunk_end_1(c):
                kind, j = CHUNKS1[c]
                q = Step(qW1 + c)
                low_copy(q, 2 * (c % 2), Step(W1 + 4 * c + 3))
                if kind == "gate":
                    combined(q)
                    nc.scalar.activation(tanh_b[:, :, :], tanh_b[:, :, :], ACT.Tanh, scale=0.5).then_inc(tanh_ready, 1)
                elif kind == "v":
                    act.wait_ge(cv_ready, j + 1)
                    for t in range(2):
                        nc.scalar.activation(conv_a[:, t, :], cv[:, t, 2:2 + T], ACT.Copy,
                                             scale=P("conv_a_w", 12 + 2 * j + t)).then_inc(conv_a_started, 1)
                    act.wait_ge(a_mixed, j + 1)
                    nc.scalar.activation(act_split[:, 2 * j:2 * j + 2, 0:T], conv_a[:, :, :],
                                         ACT.Copy).then_inc(a_hi, 1)

            def layer_norm(n):
                if n == 63:
                    act.wait_ge(stat_summed, N_LN_MEAN + 1)
                    nc.scalar.activation(root[:, :], ps[:, 6, 0:2], ACT.Copy, scale=1 / 768).then_inc(root_ready, 1)
                elif n == 65:
                    for j in range(3):
                        act.wait_ge(centered, j + 1)
                        nc.scalar.activation(ln_squares[:, 2 * j:2 * j + 2, :], conv_b[:, 2 * j:2 * j + 2, :],
                                             ACT.Square).then_inc(ln_squared, 1)
                elif n == 67:
                    take_root(N_LN_VAR, 768)
                elif n == O1 + 1:
                    for j in range(3):
                        act.wait_ge(ln_scaled, j + 1)
                        for t in range(2 * j, 2 * j + 2):
                            nc.scalar.activation(conv_b[:, t, :], conv_b[:, t, :], ACT.Identity,
                                                 scale=P("ln_b_gain", t), bias=P("ln_b_bias", t)).then_inc(ln_affine, 1)
                        act.wait_ge(ln_affine, 2 * j + 2)
                        nc.scalar.activation(ln_squares[:, 2 * j:2 * j + 2, :], conv_b[:, 2 * j:2 * j + 2, :],
                                             ACT.Tanh, scale=0.5).then_inc(ln_tanh, 1)
                    for j in range(3):
                        act.wait_ge(ln_silu, j + 1)
                        nc.scalar.activation(act_split[:, 6 + 2 * j:8 + 2 * j, 0:T], conv_b[:, 2 * j:2 * j + 2, :],
                                             ACT.Copy, scale=0.5).then_inc(b_hi, 1)

            def pool_end(j):
                act.wait_ge(pool_summed, j + 1)
                for t in range(2):
                    k = 2 * j + t
                    nc.scalar.activation(act_split[:, 12 + k, 0:T], ps[:, 4 + j, T * t:T * t + T], ACT.Copy,
                                         scale=P("pool_scale", k)).then_inc(c_hi, 1)

            for c in range(17):
                for p in range(4):
                    n = 4 * c + p
                    if n > 2:
                        split(Step(W1 + n))
                    if p == 3 and c > 0:
                        chunk_end_1(c - 1)
                    if n in (28, 44, 60):
                        finish_conv_b((n - 28) // 16)
                    layer_norm(n)

            def wide_end(q, bank, last, r):
                low_copy(q.plus(r), bank + 2 * r, last)

            def y_squares(norm, q0, q, y):
                square(norm, q, *y_pair_ready(norm, q0, q), y)

            def y_pair_ready(norm, q0, q):
                if norm in (N_POST1, N_POST2):
                    return pair_combined, PAIR_CREDIT + q0 + q + 1
                groups = len(GROUPS1) - 1 if norm == N_POSTF1 else len(GROUPS1) - 1 + 3
                return y_summed, 8 * (groups - 1) + q + 1

            def out_product(n0, q0, pieces, norm, y, before, between=lambda n: None):
                for c in range(4):
                    for p in range(pieces):
                        split(Step(n0 + pieces * c + p))
                        between(n0 + pieces * c + p)
                        if p in (3, 4):
                            r = p - 3
                            if c == 0:
                                before(r)
                            else:
                                wide_end(Step(q0 + 2 * c - 2), 4 * ((c - 1) % 2), Step(n0 + pieces * c - 1), r)
                                if norm is not None:
                                    y_squares(norm, q0, 2 * c - 2 + r, y)

            def last_chunk(n0, q0, pieces, norm, y):
                for r in range(2):
                    wide_end(Step(q0 + 6), 4, Step(n0 + 4 * pieces - 1), r)
                    if norm is not None:
                        y_squares(norm, q0, 6 + r, y)

            def post_and_pre(post, pre, gain, next_piece):
                take_root(post, D)
                for p in range(3):
                    split(Step(next_piece + p))
                for q in range(8):
                    square(pre, q, x_ready, 8 * POST[post] + q + 1, x)
                pre_norm(pre, gain)

            def first_pools(n):
                layer_norm(n)
                if n == O1 + 4:
                    pool_end(0)
                elif n == O1 + 6:
                    pool_end(1)

            out_product(O1, qO1, 8, N_POST1, y,
                        before=lambda r: chunk_end_1(16) if r == 0 else None, between=first_pools)
            last_chunk(O1, qO1, 8, N_POST1, y)
            post_and_pre(N_POST1, N_PREF1, "norm_ffn_pre", M1)

            def start_conv(chunk, r, half, out):
                for t in range(2):
                    k = chunk.times(4).value(44 * half + 2 * r + t)
                    nc.scalar.activation(out[:, t, :], up_in[:, t, 2:2 + T], ACT.Identity,
                                         scale=P("conv_ffn_w", 2 * 88 + k), bias=P("conv_ffn_bias", k)
                                         ).then_inc(conv_started, 1)

            def gate_end(n0, q0, chunk, r):
                low_copy(q0.plus(r), 2 * r, n0.plus(7))
                combined(q0.plus(r))
                start_conv(chunk, r, 0, gate_conv[:, 2 * r:2 * r + 2, :])
                act.wait_ge(conv_done, chunk.times(2).value(r + 1))
                nc.scalar.activation(gate_tanh[:, 2 * r:2 * r + 2, :], gate_conv[:, 2 * r:2 * r + 2, :], ACT.Tanh,
                                     scale=0.5).then_inc(gate_ready, 1)

            def val_end(n0, q0, chunk, first, r):
                low_copy(q0.plus(2 + r), 4 + 2 * r, n0.plus(15))
                combined(q0.plus(2 + r))
                start_conv(chunk, r, 1, val_conv)
                act.wait_ge(units_ready, chunk.times(2).value(r + 1))
                k = chunk.times(4).value(2 * r - 4 * first)
                nc.scalar.activation(act_split[:, at2(k), 0:T], hidden[:, :, :], ACT.Copy, scale=0.5
                                     ).then_inc(unit_hi, 1)

            def at2(k):
                return slice(k, k + 2) if isinstance(k, int) else bass.ds(k, 2)

            def up_chunks(g, first, i, before, skip=0):
                n0, q0 = Step(up1[g], i, 16), Step(qup1[g], i, 4)
                chunk = Step(first, i, 1)
                for p in range(16):
                    if p >= skip:
                        split(n0.plus(p))
                    if p in (3, 5):
                        before((p - 3) // 2)
                    if p in (11, 13):
                        gate_end(n0, q0, chunk, (p - 11) // 2)

            first = 0
            for g, n in enumerate(GROUPS1):
                if g == 0:
                    up_chunks(0, 0, None, lambda r: None, skip=3)
                else:
                    up_chunks(g, first, None, lambda r: wide_end(
                        Step(qdown1[g - 1] + 6), 4, Step(down1[g - 1] + 8 * GROUPS1[g - 1] - 1), r))
                with act.Fori(1, n) as i:
                    up_chunks(g, first, i, lambda r: val_end(
                        Step(up1[g] - 16, i, 16), Step(qup1[g] - 4, i, 4), Step(first - 1, i, 1), first, r))
                last = g == len(GROUPS1) - 1
                out_product(down1[g], qdown1[g], 2 * n, N_POSTF1 if last else None, y, before=lambda r: val_end(
                    Step(up1[g] + 16 * (n - 1)), Step(qup1[g] + 4 * (n - 1)), Step(first + n - 1), first, r))
                first += n
            last_chunk(down1[-1], qdown1[-1], 2 * n, N_POSTF1, y)
            take_root(N_POSTF1, D)
            act.wait_ge(forget_loaded, 16)
            for p in range(2):
                split(Step(G2 + p))
            for q in range(8):
                square(N_PRE2, q, x_ready, 8 * POST[N_POSTF1] + q + 1, x)
            pre_norm(N_PRE2, "norm_mix_pre_2")

            def gate_rows():
                low_copy(Step(qG2), 2, Step(G2 + 1), tiles=1)
                act.wait_ge(rows_split, 1)
                nc.scalar.activation(row_g[0:4, :], row_f[0:4, :], ACT.Abs).then_inc(row_step, 1)
                act.wait_ge(row_step, 1)
                nc.scalar.activation(row_g[0:4, :], row_g[0:4, :], ACT.Exp, scale=-1.0).then_inc(row_step, 1)
                act.wait_ge(row_step, 2)
                nc.scalar.activation(row_g[0:4, :], row_g[0:4, :], ACT.Ln, bias=ones[0:4, 0:1]).then_inc(row_step, 1)

            def rope_tables():
                act.wait_ge(angle_ready, 1)
                nc.scalar.activation(sin[:, :], cos[:, :], ACT.Sin, scale=K("sign")).then_inc(table_step, 1)
                act.wait_ge(table_step, 1)
                nc.scalar.activation(cos[:, :], cos[:, :], ACT.Abs).then_inc(table_step, 1)
                act.wait_ge(table_step, 2)
                nc.scalar.activation(cos[:, :], cos[:, :], ACT.Sin, scale=-1.0, bias=K("half_pi")
                                     ).then_inc(table_step, 1)

            def chunk_end_2(c):
                kind, h = CHUNKS2[c]
                q = Step(qW2 + c)
                low_copy(q, 2 * (c % 2), Step(W2 + 4 * c + 3))
                if kind in ("q", "k"):
                    is_k = int(kind == "k")
                    out = (q_m, k_m)[is_k]
                    combined(q)
                    at_least(act, m_scored, h)
                    for t in range(2):
                        k = 8 * is_k + 2 * h + t
                        nc.scalar.activation(out[:, t, :], qk_in[:, t, 3:3 + T], ACT.Identity,
                                             scale=P("conv_w_2", 48 + k), bias=P("conv_b_2", k)
                                             ).then_inc(qk_started, 1)
                    act.wait_ge(qk_convolved, 2 * h + is_k + 1)
                    nc.scalar.activation(squares[:, is_k, :, :], out[:, :, :], ACT.Tanh, scale=0.5
                                         ).then_inc(qk_tanh, 1)
                elif kind == "o":
                    combined(q)
                    nc.scalar.activation(o_m[:, :, :], o_m[:, :, :], ACT.Tanh, scale=0.5).then_inc(o_ready, 1)

            def mlstm(h, stage):
                if stage == 0:
                    act.wait_ge(m_scored, h + 1)
                    at_least(act, m_valued, h)
                    nc.scalar.activation(v_tok[:, :, :].rearrange("p a t -> p (a t)"), ps[:, 5, :],
                                         ACT.Copy).then_inc(v_tok_ready, 1)
                    act.wait_ge(decay_started, h + 1)
                    nc.scalar.activation(decay[:, :], decay[:, :], ACT.Exp, scale=-1.0).then_inc(decay_ready, 1)
                elif stage == 1:
                    act.wait_ge(m_valued, h + 1)
                    nc.scalar.activation(den_m[:, 0, :], ps[:, 6, 0:T], ACT.Abs).then_inc(den_ready, 1)
                    nc.scalar.activation(den_m[:, 1, :], ps[:, 7, T:2 * T], ACT.Exp).then_inc(den_ready, 1)
                    act.wait_ge(m_divided, h + 1)
                    nc.scalar.activation(den_m[:, :, :], h_m[:, :, :], ACT.Square).then_inc(m_squared, 1)
                elif stage == 2:
                    take_root(N_HEAD + h, 256, times=2)
                else:
                    act.wait_ge(m_gated, h + 1)
                    for t in range(2):
                        nc.scalar.activation(act_split[:, 2 * h + t, 0:T], h_m[:, t, :], ACT.Copy,
                                             scale=P("mlstm_norm_2", 2 * h + t)).then_inc(m_hi, 1)

            def attention(t, stage):
                if stage == 0:
                    act.wait_ge(a_scored, t + 1)
                    act.wait_ge(m_valued, 4)
                    at_least(act, a_valued, t)
                    nc.scalar.activation(v_tok[:, 0, :], ps[:, 5, 0:T], ACT.Copy).then_inc(a_v_ready, 1)
                    act.wait_ge(a_max_ready, t + 1)
                    for half, cols in enumerate((slice(0, 128), slice(128, 384))):
                        nc.scalar.activation(decay[:, cols], decay[:, cols], ACT.Exp,
                                             bias=a_stat[:, 2 + half:3 + half],
                                             accum_out=a_stat[:, 4 + half:5 + half]).then_inc(a_exp_ready, 1)
                elif stage == 1:
                    act.wait_ge(prob_turned, t + 1)
                    at_least(act, a_valued, t)
                    nc.scalar.activation(prob_t[:, :], ps[:, 6, 0:384], ACT.Copy).then_inc(prob_t_ready, 1)
                else:
                    act.wait_ge(a_valued, t + 1)
                    nc.scalar.activation(act_split[:, 8 + t, 0:T], ps[:, 7, 0:T], ACT.Copy).then_inc(a_hi_2, 1)

            def inner(n):
                if n == 3:
                    gate_rows()
                    rope_tables()
                for h in range(4):
                    r = n - 16 * (h + 1)
                    if r in M_STAGE_END:
                        mlstm(h, M_STAGE_END.index(r))
                for j in range(4):
                    r = n - (64 + 12 * (j + 1))
                    for a in range(2):
                        if r in A_STAGE_END[a]:
                            attention(2 * j + a, A_STAGE_END[a].index(r))

            for c in range(28):
                for p in range(4):
                    split(Step(W2 + 4 * c + p))
                    if p == 3 and c > 0:
                        chunk_end_2(c - 1)
                    inner(4 * c + p)

            def merge_end(kind, turn, half):
                q = turn.times(8).plus(qY2 + 4 * half + kind)
                low_copy(q, 2 * (kind % 2), turn.times(24).plus(Y2 + 12 * half + (3, 7, 9, 11)[kind]))
                j = turn.times(2).plus(half)
                if kind < 2:
                    combined(q)
                    nc.scalar.activation(gate_pair[:, kind, :, :], gate_pair[:, kind, :, :], ACT.Tanh, scale=0.5
                                         ).then_inc(merge_tanh, 1)
                elif kind == 3:
                    act.wait_ge(merge_summed, j.value(1))
                    nc.scalar.activation(merged[:, at2(j.times(2).value()), 0:T], scaled[:, 0, :, :],
                                         ACT.Copy, scale=0.5).then_inc(merge_hi, 1)

            def merge_chunks(i, before, inner=lambda n: None):
                for half in range(2):
                    for p in range(12):
                        split(Step(Y2 + 12 * half + p, i, 24))
                        if p == 3:
                            if half:
                                merge_end(3, Step(0, i, 1), 0)
                            else:
                                before()
                        elif p in (7, 9, 11):
                            merge_end((p - 7) // 2, Step(0, i, 1), half)
                        inner(12 * half + p)

            merge_chunks(None, lambda: chunk_end_2(27), inner=lambda n: inner(112 + n))
            with act.Fori(1, 4) as i:
                merge_chunks(i, lambda: merge_end(3, Step(-1, i, 1), 1))
            out_product(O2, qO2, 8, N_POST2, y_2, before=lambda r: merge_end(3, Step(3), 1) if r == 0 else None)
            last_chunk(O2, qO2, 8, N_POST2, y_2)
            post_and_pre(N_POST2, N_PREF2, "norm_ffn_pre_2", M2)

            def relu_end(g, c, r):
                n, q = M2 + 64 * g + 8 * c, qM2 + 16 * g + 2 * c
                low_copy(Step(q + r), 4 * (c % 2) + 2 * r, Step(n + 7))
                u = 22 + 8 * g + 2 * c + r
                act.wait_ge(units_ready, u + 1)
                nc.scalar.activation(act_split[:, 4 * c + 2 * r:4 * c + 2 * r + 2, 0:T], hidden[:, :, :],
                                     ACT.Copy).then_inc(unit_hi, 1)

            for g in range(4):
                for c in range(4):
                    for p in range(8):
                        if g or c or p > 2:
                            split(Step(M2 + 64 * g + 8 * c + p))
                        if p in (3, 4):
                            if c:
                                relu_end(g, c - 1, p - 3)
                            elif g:
                                wide_end(Step(qM2 + 16 * g - 2), 4, Step(M2 + 64 * g - 1), p - 3)
                out_product(M2 + 64 * g + 32, qM2 + 16 * g + 8, 8, N_POSTF2 if g == 3 else None, y,
                            before=lambda r: relu_end(g, 3, r))
            last_chunk(M2 + 64 * 3 + 32, qM2 + 16 * 3 + 8, 8, N_POSTF2, y)
            take_root(N_POSTF2, D)

        @block.gpsimd
        def _(pool):
            nc.gpsimd.memset(glu[:, :, 0:30], 0.0).then_inc(cleared, 1)
            nc.gpsimd.memset(cv[:, :, 0:2], 0.0).then_inc(cleared, 1)
            nc.gpsimd.memset(pool_in[:, :, 0:16], 0.0).then_inc(cleared, 1)

            def sum_squares(norm):
                at_least(pool, stat_summed, SUMMED_BEFORE[norm])
                for q in range(8):
                    s = 8 * SUMMED[norm] + q
                    pool.wait_ge(squares_ready, s + 1)
                    at_least(pool, squares_added, s)
                    if q == 0:
                        ins = nc.gpsimd.tensor_copy(square_sum[:, :, :], squares[:, s % 2, :, :])
                    else:
                        ins = nc.gpsimd.tensor_tensor(square_sum[:, :, :], square_sum[:, :, :],
                                                      squares[:, s % 2, :, :], ALU.add)
                    ins.then_inc(squares_added, 1)

            for norm in SUMMED:
                sum_squares(norm)
                if norm == N_POST1:
                    nc.gpsimd.memset(up_in[:, :, 0:2], 0.0).then_inc(cleared, 1)
                elif norm == N_PRE2:
                    nc.gpsimd.memset(qk_in[:, :, 0:3], 0.0).then_inc(cleared, 1)

        @block.vector
        def _(dve):
            class Taken:

                def __init__(self):
                    self.count = Step(0)

                def one(self):
                    self.count = self.count.plus(1)
                    return 1

                def all(self, but=0):
                    return self.count.value(-but)

                def enter(self, i, start, rate):
                    self.outside, self.rate, self.start = self.count, rate, start
                    self.count = self.inside = self.count.plus(-start * rate).along(i, rate)

                def leave(self, end):
                    assert self.count.base - self.inside.base == self.rate, self.count.base - self.inside.base
                    self.count = self.outside.plus((end - self.start) * self.rate)

            steps = Taken()

            def tt(out, a, b, op):
                return nc.vector.tensor_tensor(out, a, b, op)

            def stt(out, a, scalar, b, op0, op1):
                return nc.vector.scalar_tensor_tensor(out=out, in0=a, scalar=scalar, in1=b, op0=op0, op1=op1)

            def split(n):
                block_n = Step(n.base // 2, terms=tuple((i, r // 2) for i, r in n.terms))
                slot, half = block_n.slot(RAW_SLOTS), 1024 * (n.base % 2)
                dve.wait_ge(hi_ready, n.value(1))
                tt(w_lo[:, n.slot(SPLIT_SLOTS), :], raw[:, slot, half:half + 1024],
                   w_hi[:, n.slot(SPLIT_SLOTS), :].bitcast(f32), ALU.subtract).then_inc(lo_ready, 1)

            def combine(q, bank, out, tiles=2):
                dve.wait_ge(low_ready, q.value(1))
                tt(out, ps[:, bank:bank + tiles, 0:T], low[:, q.slot(2), 0:tiles, :], ALU.add
                   ).then_inc(pair_combined, 1)

            def combined(q):
                dve.wait_ge(pair_combined, q.value(PAIR_CREDIT + 1))

            def low_half(out, value, scale, high):
                return stt(out, value, scale, high.bitcast(f32), ALU.mult, ALU.subtract)

            def make_scales(norm, roots=True):
                dve.wait_ge(root_ready, norm + 1)
                scales = root
                if roots:
                    scales = stat
                    nc.vector.reciprocal(stat[:, :], root[:, :]).then_inc(vector_step, steps.one())
                    dve.wait_ge(vector_step, steps.all())
                for half in range(2):
                    last = nc.vector.tensor_scalar(diag[:, half, :], identity, scales[:, half:half + 1], None, ALU.mult)
                last.then_inc(diag_ready, 1)

            def post_norm(norm, y, gain):
                make_scales(norm)
                dve.wait_ge(bcast_ready, norm + 1)
                for q in range(8):
                    if q >= 2:
                        dve.wait_ge(x_ready, 8 * POST[norm] + q - 1)
                    tt(scaled[:, q % 2, :, :], y[:, 2 * q:2 * q + 2, :], bcast2(ps[:, 7, 0:T]), ALU.mult
                       ).then_inc(vector_step, steps.one())
                    dve.wait_ge(vector_step, steps.all())
                    for t in range(2):
                        k = 2 * q + t
                        last = stt(x[:, k, :], scaled[:, q % 2, t, :], P(gain, k), x[:, k, :], ALU.mult, ALU.add)
                    last.then_inc(x_ready, 1)

            def pre_norm(norm, gain):
                make_scales(norm)
                dve.wait_ge(bcast_ready, norm + 1)

                def low_of(q):
                    dve.wait_ge(norm_hi, 2 * (8 * PRE[norm] + q + 1))
                    for t in range(2):
                        k = 2 * q + t
                        last = low_half(h_split[:, k, T:2 * T], scaled[:, q % 2, t, :], P(gain, k),
                                        h_split[:, k, 0:T])
                    last.then_inc(h_ready, 1)

                for q in range(8):
                    if q >= 2:
                        dve.wait_ge(h_ready, 8 * PRE[norm] + q - 1)
                    tt(scaled[:, q % 2, :, :], x[:, 2 * q:2 * q + 2, :], bcast2(ps[:, 7, 0:T]), ALU.mult
                       ).then_inc(scaled_ready, 1)
                    if q:
                        low_of(q - 1)
                low_of(7)

            dve.sem_inc(lo_ready, LO_CREDIT)
            dve.sem_inc(pair_combined, PAIR_CREDIT)
            dve.wait_ge(small_loaded, 32)
            dve.wait_ge(x_loaded, 16)
            for p in range(3):
                split(Step(W1 + p))
            pre_norm(N_PRE1, "norm_mix_pre")

            def taps_b(j, first, count):
                for k in range(first, min(first + count, 31)):
                    if k == 0:
                        dve.wait_ge(glu_ready, j + 1)
                        dve.wait_ge(cleared, 3)
                    for t in range(2 * j, 2 * j + 2):
                        weight = P("conv_b_w", 6 * k + t)
                        window = glu[:, t, k:k + T]
                        if k == 0:
                            ins = nc.vector.tensor_scalar(conv_b[:, t, :], window, weight, None, ALU.mult)
                        else:
                            dve.wait_ge(vector_step, steps.all(but=1))
                            ins = stt(conv_b[:, t, :], window, weight, conv_b[:, t, :], ALU.mult, ALU.add)
                        if (k, t) == (30, 2 * j + 1):
                            ins.then_inc(taps_done, 1)
                        else:
                            ins.then_inc(vector_step, steps.one())

            def chunk_end_1(c):
                kind, j = CHUNKS1[c]
                q, bank = Step(qW1 + c), 2 * (c % 2)
                if kind == "val":
                    combine(q, bank, val_b[:, :, :])
                elif kind == "gate":
                    combine(q, bank, tanh_b[:, :, :])
                    dve.wait_ge(tanh_ready, j + 1)
                    stt(glu[:, 2 * j:2 * j + 2, 30:30 + T], tanh_b[:, :, :], 1.0, val_b[:, :, :], ALU.add, ALU.mult
                        ).then_inc(glu_ready, 1)
                elif kind == "b":
                    combine(q, bank, b_gate[:, :, :])
                elif kind == "c":
                    combine(q, bank, c_gate[:, :, :])
                elif kind == "v":
                    combine(q, bank, conv_a[:, :, :])
                    combined(q)
                    tt(cv[:, :, 2:2 + T], c_gate[:, :, :], conv_a[:, :, :], ALU.mult).then_inc(cv_ready, 1)
                    for k in (1, 0):
                        for t in range(2):
                            dve.wait_ge(conv_a_started, 2 * j + t + 1)
                            if k == 0:
                                dve.wait_ge(vector_step, steps.all(but=1))
                            stt(conv_a[:, t, :], cv[:, t, k:k + T], P("conv_a_w", 6 * k + 2 * j + t),
                                             conv_a[:, t, :], ALU.mult, ALU.add).then_inc(vector_step, steps.one())
                    dve.wait_ge(vector_step, steps.all())
                    tt(conv_a[:, :, :], conv_a[:, :, :], b_gate[:, :, :], ALU.mult).then_inc(a_mixed, 1)
                    dve.wait_ge(a_hi, j + 1)
                    tt(act_split[:, 2 * j:2 * j + 2, T:2 * T], conv_a[:, :, :],
                       act_split[:, 2 * j:2 * j + 2, 0:T].bitcast(f32), ALU.subtract).then_inc(a_split, 1)
                else:
                    dve.wait_ge(vector_step, steps.all())
                    combine(q, bank, pool_in[:, :, 16:16 + T])
                    combined(q)
                    at_least(dve, pool_summed, j)
                    for t in range(2):
                        g = 2 * j + t
                        source = pool_in[:, t, :]
                        for s in range(g + 1):
                            w, out = 1 << s, pool_sum[:, s % 2, :]
                            dve.wait_ge(vector_step, steps.all())
                            tt(out[:, 2 * w - 1:16 + T], source[:, 2 * w - 1:16 + T],
                                            source[:, w - 1:16 + T - w], ALU.add).then_inc(vector_step, steps.one())
                            source = out
                        dve.wait_ge(vector_step, steps.all())
                        w = 2 << g
                        tt(pooled[:, t, 0:16], source[:, 16:32], K("pool_first", 16 * g, 16), ALU.mult
                           ).then_inc(vector_step, steps.one())
                        stt(pooled[:, t, 16:T], source[:, 32:16 + T], 1 / w, pool_in[:, t, 32:16 + T],
                                         ALU.mult, ALU.subtract).then_inc(vector_step, steps.one())
                        dve.wait_ge(vector_step, steps.all(but=1))
                        last = tt(pooled[:, t, 0:16], pooled[:, t, 0:16], pool_in[:, t, 16:32], ALU.subtract)
                        if t:
                            last.then_inc(pooled_ready, 1)
                        else:
                            last.then_inc(vector_step, steps.one())

            def layer_norm(n):
                if n == 63:
                    make_scales(N_LN_MEAN, roots=False)
                elif n == 65:
                    dve.wait_ge(bcast_ready, N_LN_MEAN + 1)
                    for j in range(3):
                        dve.wait_ge(conv_b_ready, 2 * j + 2)
                        pair = conv_b[:, 2 * j:2 * j + 2, :]
                        tt(pair, pair, bcast2(ps[:, 7, 0:T]), ALU.subtract).then_inc(centered, 1)
                elif n == 67:
                    make_scales(N_LN_VAR)
                elif n == O1 + 1:
                    dve.wait_ge(bcast_ready, N_LN_VAR + 1)
                    for j in range(3):
                        dve.wait_ge(ln_squared, j + 1)
                        pair = conv_b[:, 2 * j:2 * j + 2, :]
                        tt(pair, pair, bcast2(ps[:, 7, 0:T]), ALU.mult).then_inc(ln_scaled, 1)
                    for j in range(3):
                        dve.wait_ge(ln_tanh, j + 1)
                        pair = conv_b[:, 2 * j:2 * j + 2, :]
                        stt(pair, ln_squares[:, 2 * j:2 * j + 2, :], 1.0, pair, ALU.add, ALU.mult
                            ).then_inc(ln_silu, 1)
                    for j in range(3):
                        dve.wait_ge(b_hi, j + 1)
                        low_half(act_split[:, 6 + 2 * j:8 + 2 * j, T:2 * T], conv_b[:, 2 * j:2 * j + 2, :], 0.5,
                                 act_split[:, 6 + 2 * j:8 + 2 * j, 0:T]).then_inc(b_split, 1)

            def pool_end(j):
                dve.wait_ge(c_hi, 2 * j + 2)
                for t in range(2):
                    k = 2 * j + t
                    last = low_half(act_split[:, 12 + k, T:2 * T], ps[:, 4 + j, T * t:T * t + T], P("pool_scale", k),
                                    act_split[:, 12 + k, 0:T])
                last.then_inc(c_split, 1)

            for c in range(17):
                for p in range(4):
                    n = 4 * c + p
                    if n > 2:
                        split(Step(W1 + n))
                    if p == 3 and c > 0:
                        chunk_end_1(c - 1)
                    if 12 <= n < 60:
                        taps_b((n - 12) // 16, 2 * ((n - 12) % 16), 2)
                    layer_norm(n)

            def y_pair(g, q, bank, y, n):
                if g == 0:
                    combine(q, bank, y[:, 2 * n:2 * n + 2, :])
                    return
                combine(q, bank, scaled[:, n % 2, :, :])
                combined(q)
                tt(y[:, 2 * n:2 * n + 2, :], y[:, 2 * n:2 * n + 2, :], scaled[:, n % 2, :, :], ALU.add
                   ).then_inc(y_summed, 1)

            def out_product(n0, q0, pieces, g, y, before, between=lambda n: None):
                for c in range(4):
                    for p in range(pieces):
                        split(Step(n0 + pieces * c + p))
                        between(n0 + pieces * c + p)
                        if p in (3, 4):
                            r = p - 3
                            if c == 0:
                                before(r)
                            else:
                                y_pair(g, Step(q0 + 2 * c - 2 + r), 4 * ((c - 1) % 2) + 2 * r, y, 2 * c - 2 + r)

            def last_chunk(q0, g, y):
                for r in range(2):
                    y_pair(g, Step(q0 + 6 + r), 4 + 2 * r, y, 6 + r)

            def post_and_pre(post, y, post_gain, pre, pre_gain, next_piece, pieces=3):
                for p in range(pieces):
                    split(Step(next_piece + p))
                post_norm(post, y, post_gain)
                pre_norm(pre, pre_gain)

            def first_pools(n):
                layer_norm(n)
                if n == O1 + 4:
                    pool_end(0)
                elif n == O1 + 6:
                    pool_end(1)

            out_product(O1, qO1, 8, 0, y, before=lambda r: chunk_end_1(16) if r == 0 else None, between=first_pools)
            last_chunk(qO1, 0, y)
            post_and_pre(N_POST1, y, "norm_mix_post", N_PREF1, "norm_ffn_pre", M1)

            def taps_ffn(chunk, r, half, out, last_signal):
                for k in (1, 0):
                    for t in range(2):
                        weight = P("conv_ffn_w", chunk.times(4).value(88 * k + 44 * half + 2 * r + t))
                        if k:
                            dve.wait_ge(conv_started, chunk.times(8).value(4 * half + 2 * r + t + 1))
                        else:
                            dve.wait_ge(vector_step, steps.all(but=1))
                        ins = stt(out[:, t, :], up_in[:, t, k:k + T], weight, out[:, t, :], ALU.mult, ALU.add)
                        if last_signal is not None and (k, t) == (0, 1):
                            ins.then_inc(last_signal, 1)
                        else:
                            ins.then_inc(vector_step, steps.one())

            def gate_end(q0, chunk, r):
                if r:
                    dve.wait_ge(conv_done, chunk.times(2).value(1))
                combine(q0.plus(r), 2 * r, up_in[:, :, 2:2 + T])
                taps_ffn(chunk, r, 0, gate_conv[:, 2 * r:2 * r + 2, :], conv_done)

            def at2(k):
                return slice(k, k + 2) if isinstance(k, int) else bass.ds(k, 2)

            def split_hidden(u, k, scale):
                dve.wait_ge(unit_hi, u + 1)
                low_half(act_split[:, at2(k), T:2 * T], hidden[:, :, :], scale, act_split[:, at2(k), 0:T]
                         ).then_inc(unit_split, 1)

            def val_end(q0, chunk, first, r):
                dve.wait_ge(vector_step, steps.all())
                combine(q0.plus(2 + r), 4 + 2 * r, up_in[:, :, 2:2 + T])
                taps_ffn(chunk, r, 1, val_conv, None)
                dve.wait_ge(gate_ready, chunk.times(2).value(r + 1))
                if r:
                    dve.wait_ge(unit_split, chunk.times(2).value(1))
                pair = gate_conv[:, 2 * r:2 * r + 2, :]
                stt(hidden[:, :, :], gate_tanh[:, 2 * r:2 * r + 2, :], 1.0, pair, ALU.add, ALU.mult
                    ).then_inc(vector_step, steps.one())
                dve.wait_ge(vector_step, steps.all())
                tt(hidden[:, :, :], hidden[:, :, :], val_conv[:, :, :], ALU.mult).then_inc(units_ready, 1)
                split_hidden(chunk.times(2).value(r), chunk.times(4).value(2 * r - 4 * first), 0.5)

            def up_chunks(g, first, i, before, skip=0):
                q0 = Step(qup1[g], i, 4)
                chunk = Step(first, i, 1)
                for p in range(16):
                    if p >= skip:
                        split(Step(up1[g] + p, i, 16))
                    if p in (3, 5):
                        before((p - 3) // 2)
                    if p in (11, 13):
                        gate_end(q0, chunk, (p - 11) // 2)

            dve.wait_ge(cleared, 4)
            first = 0
            for g, n in enumerate(GROUPS1):
                if g == 0:
                    up_chunks(0, 0, None, lambda r: None, skip=3)
                else:
                    up_chunks(g, first, None, lambda r: y_pair(
                        g - 1, Step(qdown1[g - 1] + 6 + r), 4 + 2 * r, y, 6 + r))
                with dve.Fori(1, n) as i:
                    steps.enter(i, 1, 16)
                    up_chunks(g, first, i, lambda r: val_end(
                        Step(qup1[g] - 4, i, 4), Step(first - 1, i, 1), first, r))
                    steps.leave(n)
                out_product(down1[g], qdown1[g], 2 * n, g, y, before=lambda r: val_end(
                    Step(qup1[g] + 4 * (n - 1)), Step(first + n - 1), first, r))
                first += n
            last_chunk(qdown1[-1], 2, y)
            post_and_pre(N_POSTF1, y, "norm_ffn_post", N_PRE2, "norm_mix_pre_2", G2, pieces=2)

            def gate_rows():
                combine(Step(qG2), 2, scaled[:, 0, 0:1, :], tiles=1)
                combined(Step(qG2))
                nc.vector.tensor_scalar(row_i[0:4, :], scaled[0:4, 0, 0, :], P("gate_bias", 0)[0:4, :], None, ALU.add
                                        ).then_inc(vector_step, steps.one())
                nc.vector.tensor_scalar(row_f[0:4, :], scaled[64:68, 0, 0, :], P("gate_bias", 1)[64:68, :], None,
                                        ALU.add).then_inc(rows_split, 1)
                dve.wait_ge(rows_split, 1)
                nc.vector.tensor_scalar(row_m[0:4, :], row_f[0:4, :], 0.0, None, ALU.min
                                        ).then_inc(vector_step, steps.one())
                dve.wait_ge(row_step, 3)
                dve.wait_ge(vector_step, steps.all())
                tt(row_m[0:4, :], row_m[0:4, :], row_g[0:4, :], ALU.subtract).then_inc(vector_step, steps.one())
                dve.wait_ge(vector_step, steps.all())
                one = ones[0:4, 0:1].to_broadcast([4, T])
                nc.vector.tensor_tensor_scan(row_n[0:4, :], one, row_m[0:4, :], 0.0, ALU.mult, ALU.add
                                             ).then_inc(vector_step, steps.one())
                dve.wait_ge(vector_step, steps.all())
                tt(row_g[0:4, :], row_i[0:4, :], row_n[0:4, :], ALU.subtract).then_inc(vector_step, steps.one())
                dve.wait_ge(vector_step, steps.all())
                nc.vector.tensor_tensor_scan(row_m[0:4, :], one, row_g[0:4, :], 0.0, ALU.mult, ALU.max
                                             ).then_inc(vector_step, steps.one())
                dve.wait_ge(vector_step, steps.all())
                stt(row_n[0:4, :], row_n[0:4, :], -1.0, row_m[0:4, :], ALU.mult, ALU.subtract
                    ).then_inc(rows_ready, 1)

            def angles():
                turns, angle = scaled[:, 1, 0, :], cos[:, :]
                dve.wait_ge(pos_loaded, 16)
                nc.vector.tensor_copy(angle, pos_i[:, :]).then_inc(vector_step, steps.one())
                dve.wait_ge(vector_step, steps.all())
                nc.vector.tensor_scalar(angle, angle, K("inv_freq"), None, ALU.mult).then_inc(vector_step, steps.one())
                dve.wait_ge(vector_step, steps.all())
                nc.vector.tensor_scalar(turns, angle, 1 / (2 * math.pi), ROUND, ALU.mult, ALU.add
                                        ).then_inc(vector_step, steps.one())
                dve.wait_ge(vector_step, steps.all())
                nc.vector.tensor_scalar(turns, turns, ROUND, None, ALU.subtract).then_inc(vector_step, steps.one())
                for part in TURN_PARTS:
                    dve.wait_ge(vector_step, steps.all())
                    stt(angle, turns, -part, angle, ALU.mult, ALU.add).then_inc(vector_step, steps.one())
                dve.wait_ge(vector_step, steps.all())
                nc.vector.tensor_scalar(angle, angle, PI_BELOW, -PI_BELOW, ALU.min, ALU.max).then_inc(angle_ready, 1)

            def columns():
                dve.wait_ge(columns_summed, 1)
                nc.vector.tensor_copy(gcol[:, :, :].rearrange("p a t -> p (a t)"), ps[:, 6, 0:8]
                                      ).then_inc(columns_ready, 1)

            def chunk_end_2(c):
                kind, h = CHUNKS2[c]
                q, bank = Step(qW2 + c), 2 * (c % 2)
                if kind in ("q", "k"):
                    is_k = int(kind == "k")
                    out = (q_m, k_m)[is_k]
                    combine(q, bank, qk_in[:, :, 3:3 + T])
                    for k in (2, 1, 0):
                        for t in range(2):
                            if k == 2:
                                dve.wait_ge(qk_started, 4 * h + 2 * is_k + t + 1)
                            else:
                                dve.wait_ge(vector_step, steps.all(but=1))
                            ins = stt(out[:, t, :], qk_in[:, t, k:k + T], P("conv_w_2", 16 * k + 8 * is_k + 2 * h + t),
                                      out[:, t, :], ALU.mult, ALU.add)
                            if (k, t) == (0, 1):
                                ins.then_inc(qk_convolved, 1)
                            else:
                                ins.then_inc(vector_step, steps.one())
                    dve.wait_ge(qk_tanh, 2 * h + is_k + 1)
                    stt(out[:, :, :], squares[:, is_k, :, :], 1.0, out[:, :, :], ALU.add, ALU.mult
                        ).then_inc(qk_ready, 1)
                elif kind == "v":
                    at_least(dve, m_scored, h)
                    combine(q, bank, v_m[:, :, :])
                elif kind == "o":
                    combine(q, bank, o_m[:, :, :])
                elif kind == "av":
                    at_least(dve, a_scored, 2 * h)
                    combine(q, bank, a_v[:, :, :])
                else:
                    is_k = int(kind == "ak")
                    at_least(dve, a_scored, 2 * h)
                    a = (a_q, a_k)[is_k]
                    combine(q, bank, a[:, :, :])
                    combined(q)
                    dve.wait_ge(table_step, 3)
                    at_least(dve, rope_ready, 2 * h + is_k)
                    for lo_, hi_ in ((0, 64), (64, 0)):
                        for t in range(2):
                            tt(scaled[lo_:lo_ + 64, 0, t, :], a[hi_:hi_ + 64, t, :],
                                            sin[hi_:hi_ + 64, :], ALU.mult).then_inc(vector_step, steps.one())
                    dve.wait_ge(vector_step, steps.all())
                    tt(a[:, :, :], a[:, :, :], bcast2(cos[:, :]), ALU.mult).then_inc(vector_step, steps.one())
                    dve.wait_ge(vector_step, steps.all())
                    tt(a[:, :, :], a[:, :, :], scaled[:, 0, :, :], ALU.add).then_inc(rope_ready, 1)

            def mlstm(h, stage):
                if stage == 0:
                    dve.wait_ge(rows_bcast, h + 1)
                    for s, cols, queries in ((0, slice(0, 256), slice(0, 256)), (1, slice(256, 384), slice(128, 256))):
                        last = nc.vector.tensor_scalar(decay[:, cols], ps[:, 7, queries], gcol[:, s, h:h + 1], 0.0,
                                                       ALU.subtract, ALU.max)
                    last.then_inc(decay_started, 1)
                    dve.wait_ge(decay_ready, h + 1)
                    for cols in (slice(0, 128), slice(256, 384)):
                        tt(decay[:, cols], decay[:, cols], K("keep", 0, 128), ALU.mult
                           ).then_inc(vector_step, steps.one())
                    dve.wait_ge(vector_step, steps.all())
                    dve.wait_ge(m_scored, h + 1)
                    at_least(dve, m_valued, h)
                    stt(s_ts[:, :], ps[:, 4, 0:384], 1 / 64, decay[:, :], ALU.mult, ALU.mult).then_inc(s_ts_ready, 1)
                elif stage == 1:
                    dve.wait_ge(den_ready, 2 * h + 2)
                    tt(den_m[:, 0, :], den_m[:, 0, :], den_m[:, 1, :], ALU.max).then_inc(vector_step, steps.one())
                    dve.wait_ge(vector_step, steps.all())
                    nc.vector.reciprocal(den_m[:, 0, :], den_m[:, 0, :]).then_inc(vector_step, steps.one())
                    dve.wait_ge(vector_step, steps.all())
                    tt(h_m[:, :, :], ps[:, 5, :].rearrange("p (a t) -> p a t", a=2), bcast2(den_m[:, 0, :]), ALU.mult
                       ).then_inc(m_divided, 1)
                elif stage == 2:
                    make_scales(N_HEAD + h)
                else:
                    dve.wait_ge(bcast_ready, N_HEAD + h + 1)
                    dve.wait_ge(m_squared, h + 1)
                    tt(h_m[:, :, :], h_m[:, :, :], bcast2(ps[:, 7, 0:T]), ALU.mult).then_inc(vector_step, steps.one())
                    dve.wait_ge(o_ready, h + 1)
                    dve.wait_ge(vector_step, steps.all())
                    stt(h_m[:, :, :], o_m[:, :, :], 1.0, h_m[:, :, :], ALU.add, ALU.mult).then_inc(m_gated, 1)
                    dve.wait_ge(m_hi, 2 * h + 2)
                    for t in range(2):
                        last = low_half(act_split[:, 2 * h + t, T:2 * T], h_m[:, t, :], P("mlstm_norm_2", 2 * h + t),
                                        act_split[:, 2 * h + t, 0:T])
                    last.then_inc(m_split, 1)

            def attention(t, stage):
                if stage == 0:
                    scale = 128 ** -0.5
                    dve.wait_ge(a_scored, t + 1)
                    at_least(dve, prob_turned, t)
                    for cols in (slice(0, 128), slice(256, 384)):
                        stt(decay[:, cols], ps[:, 4, cols], scale, K("masked", 0, 128), ALU.mult, ALU.add
                            ).then_inc(vector_step, steps.one())
                    nc.vector.tensor_scalar(decay[:, 128:256], ps[:, 4, 128:256], scale, None, ALU.mult
                                            ).then_inc(vector_step, steps.one())
                    dve.wait_ge(vector_step, steps.all())
                    for half, cols in enumerate((slice(0, 128), slice(128, 384))):
                        nc.vector.reduce_max(a_stat[:, half:half + 1], decay[:, cols], AX.X
                                             ).then_inc(vector_step, steps.one())
                    dve.wait_ge(vector_step, steps.all())
                    nc.vector.tensor_scalar(a_stat[:, 2:4], a_stat[:, 0:2], -1.0, None, ALU.mult
                                            ).then_inc(a_max_ready, 1)
                    dve.wait_ge(a_exp_ready, 2 * t + 2)
                    nc.vector.reciprocal(a_stat[:, 6:8], a_stat[:, 4:6]).then_inc(vector_step, steps.one())
                    dve.wait_ge(vector_step, steps.all())
                    for half, cols in enumerate((slice(0, 128), slice(128, 384))):
                        last = nc.vector.tensor_scalar(s_ts[:, cols], decay[:, cols], a_stat[:, 6 + half:7 + half],
                                                       None, ALU.mult)
                    last.then_inc(prob_ready, 1)
                elif stage == 2:
                    dve.wait_ge(a_hi_2, t + 1)
                    tt(act_split[:, 8 + t, T:2 * T], ps[:, 7, 0:T], act_split[:, 8 + t, 0:T].bitcast(f32),
                       ALU.subtract).then_inc(a_split_2, 1)

            def inner(n):
                if n == 3:
                    gate_rows()
                    angles()
                if n == 14:
                    columns()
                for h in range(4):
                    r = n - 16 * (h + 1)
                    if r in M_STAGE_END:
                        mlstm(h, M_STAGE_END.index(r))
                for j in range(4):
                    r = n - (64 + 12 * (j + 1))
                    for a in range(2):
                        if r in A_STAGE_END[a]:
                            attention(2 * j + a, A_STAGE_END[a].index(r))

            dve.wait_ge(cleared, 5)
            for c in range(28):
                for p in range(4):
                    split(Step(W2 + 4 * c + p))
                    if p == 3 and c > 0:
                        chunk_end_2(c - 1)
                    inner(4 * c + p)

            def merge_end(kind, turn, half):
                q = turn.times(8).plus(qY2 + 4 * half + kind)
                bank = 2 * (kind % 2)
                if kind < 2:
                    combine(q, bank, gate_pair[:, kind, :, :])
                    return
                out = scaled[:, kind - 2, :, :]
                combine(q, bank, out)
                combined(q)
                dve.wait_ge(merge_tanh, turn.times(4).value(2 * half + 2))
                stt(out, gate_pair[:, kind - 2, :, :], 1.0, out, ALU.add, ALU.mult).then_inc(vector_step, steps.one())
                if kind == 3:
                    j = turn.times(2).plus(half)
                    k = j.times(2).value()
                    dve.wait_ge(vector_step, steps.all())
                    tt(scaled[:, 0, :, :], scaled[:, 0, :, :], out, ALU.add).then_inc(merge_summed, 1)
                    dve.wait_ge(merge_hi, j.value(1))
                    low_half(merged[:, at2(k), T:2 * T], scaled[:, 0, :, :], 0.5, merged[:, at2(k), 0:T]
                             ).then_inc(merge_split, 1)

            def merge_chunks(i, before, inner=lambda n: None):
                turn = Step(0, i, 1)
                for half in range(2):
                    for p in range(12):
                        split(Step(Y2 + 12 * half + p, i, 24))
                        if p == 3:
                            if half:
                                merge_end(3, turn, 0)
                            else:
                                before()
                        elif p in (7, 9, 11):
                            merge_end((p - 7) // 2, turn, half)
                        inner(12 * half + p)

            merge_chunks(None, lambda: chunk_end_2(27), inner=lambda n: inner(112 + n))
            with dve.Fori(1, 4) as i:
                steps.enter(i, 1, 4)
                merge_chunks(i, lambda: merge_end(3, Step(-1, i, 1), 1))
                steps.leave(4)
            out_product(O2, qO2, 8, 0, y_2, before=lambda r: merge_end(3, Step(3), 1) if r == 0 else None)
            last_chunk(qO2, 0, y_2)
            post_and_pre(N_POST2, y_2, "norm_mix_post_2", N_PREF2, "norm_ffn_pre_2", M2)

            def relu_end(g, c, r):
                combine(Step(qM2 + 16 * g + 2 * c + r), 4 * (c % 2) + 2 * r, squares[:, r, :, :])
                combined(Step(qM2 + 16 * g + 2 * c + r))
                u = 22 + 8 * g + 2 * c + r
                dve.wait_ge(unit_split, u)
                stt(hidden[:, :, :], squares[:, r, :, :], 0.0, squares[:, r, :, :], ALU.max, ALU.mult
                    ).then_inc(units_ready, 1)
                split_hidden(u, 4 * c + 2 * r, 1.0)

            for g in range(4):
                for c in range(4):
                    for p in range(8):
                        if g or c or p > 2:
                            split(Step(M2 + 64 * g + 8 * c + p))
                        if p in (3, 4):
                            if c:
                                relu_end(g, c - 1, p - 3)
                            elif g:
                                y_pair(g - 1, Step(qM2 + 16 * g - 2 + p - 3), 4 + 2 * (p - 3), y, 6 + p - 3)
                out_product(M2 + 64 * g + 32, qM2 + 16 * g + 8, 8, g, y, before=lambda r: relu_end(g, 3, r))
            last_chunk(qM2 + 16 * 3 + 8, 3, y)
            post_norm(N_POSTF2, y, "norm_ffn_post_2")


_WEIGHTS = ["w_in", "w_out", "w_up", "w_down", "w_in_2", "w_branch_m_2", "w_branch_a_2", "w_out_2",
            "w_up_2", "w_down_2"]


def pack_params(inputs):
    import numpy as np

    def columns(name):
        if name == "gate_bias":
            out = np.zeros((128, 2), np.float32)
            out[0:4, 0] = inputs["i_bias_2"][0]
            out[64:68, 1] = inputs["f_bias_2"][0]
            return out
        a = np.asarray(inputs[name][0])
        if name == "pool_w":
            return a.transpose(1, 0, 2).reshape(128, -1)
        return a.reshape(-1, 128).T

    return np.ascontiguousarray(np.concatenate([columns(name) for name, _ in PARAM_COLUMNS], 1), np.float32)


def constants():
    import numpy as np

    p, one = np.arange(128), np.ones((128, 128), np.float32)
    select = np.zeros((128, 4, 128), np.float32)
    for h in range(4):
        select[h, h] = 1
    first = np.array([[1 / min(t + 1, w) for t in range(16)] for w in (2, 4, 8, 16)], np.float32).reshape(1, 64)
    column = {
        "identity": np.eye(128), "ones": one,
        "keep": np.triu(one),
        "masked": np.triu(one, 1) * np.float32(-1e38),
        "select": select.reshape(128, -1),
        "pool_first": np.repeat(first, 128, 0),
        "inv_freq": (np.float32(1) / np.float32(10000) ** ((2 * (p % 64)).astype(np.float32) / np.float32(128)))[:, None],
        "epsilon": np.repeat(np.array([[1e-6, 1e-5, 4e-6]]), 128, 0),
        "half_pi": np.full((128, 1), np.pi / 2), "sign": np.where(p < 64, 1, -1)[:, None],
    }
    return np.ascontiguousarray(np.concatenate([column[n] for n, _ in CONST_COLUMNS], 1), np.float32)


def kernel(**inputs):
    import concourse.bacc as bacc
    import numpy as np
    from concourse import mybir
    from concourse.bass_utils import run_bass_kernel_spmd

    nc = bacc.Bacc("TRN2", target_bir_lowering=False, num_devices=1)
    arrays = {
        "xT": np.ascontiguousarray(np.asarray(inputs["x"])[0].reshape(256, 16, 128).transpose(2, 1, 0)),
        "params": pack_params(inputs), "consts": constants(),
        "positions": np.ascontiguousarray(inputs["positions_2"]).astype(np.int32),
    }
    for name in _WEIGHTS:
        arrays[name] = np.ascontiguousarray(inputs[name][0])
    aps = [nc.dram_tensor(name, a.shape, mybir.dt.from_np(a.dtype), kind="ExternalInput").ap()
           for name, a in arrays.items()]
    out = nc.dram_tensor("outT", (128, 16, 256), mybir.dt.float32, kind="ExternalOutput").ap()
    build(nc, *aps, out)
    result = run_bass_kernel_spmd(nc, [arrays], core_ids=[0]).results[0]["outT"]
    return result.transpose(2, 1, 0).reshape(1, 256, 2048)
```

```python
def plan(shapes):
    off, at = {}, 0
    for name, n in shapes:
        off[name] = at
        at += n
    return off, at


PARAM_COLUMNS = [
    ("norm_mix_pre", 16), ("norm_mix_post", 16), ("norm_ffn_pre", 16), ("norm_ffn_post", 16),
    ("norm_mix_pre_2", 16), ("norm_mix_post_2", 16), ("norm_ffn_pre_2", 16), ("norm_ffn_post_2", 16),
    ("conv_a_w", 3 * 6), ("conv_b_w", 31 * 6), ("conv_b_bias", 6), ("ln_b_gain", 6), ("ln_b_bias", 6),
    ("pool_scale", 4), ("conv_ffn_w", 3 * 88), ("conv_ffn_bias", 88),
    ("conv_w_2", 4 * 16), ("conv_b_2", 16), ("mlstm_norm_2", 8), ("gate_bias", 2),
    ("pool_w", 4 * 128),
]
CONST_COLUMNS = [
    ("identity", 128), ("ones", 128), ("keep", 128), ("masked", 128), ("select", 4 * 128),
    ("pool_first", 4 * 16), ("inv_freq", 1), ("epsilon", 3), ("half_pi", 1), ("sign", 1),
]


def turn_parts():
    import math

    import numpy as np

    first = 6.28125
    second = math.floor((2 * math.pi - first) * 2.0 ** 20) / 2.0 ** 20
    return first, second, float(np.float32(2 * math.pi - first - second))


class Step:

    def __init__(self, base, i=None, rate=0, terms=()):
        self.base = base
        self.terms = tuple(terms) + (() if i is None else ((i, rate),))

    def plus(self, k):
        return Step(self.base + k, terms=self.terms)

    def times(self, k):
        return Step(self.base * k, terms=tuple((i, r * k) for i, r in self.terms))

    def along(self, i, rate):
        return Step(self.base, i, rate, self.terms)

    def value(self, k=0):
        out = self.base + k
        for i, rate in self.terms:
            out = i * rate + out
        return out

    def slot(self, slots):
        assert all(rate % slots == 0 for _, rate in self.terms)
        return self.base % slots

    def turn(self, slots):
        assert all(rate % slots == 0 for _, rate in self.terms)
        return Step(self.base // slots, terms=tuple((i, rate // slots) for i, rate in self.terms))


def build(nc, xT, params, consts, positions, w_in, w_out, w_up, w_down,
          w_in_2, w_branch_m_2, w_branch_a_2, w_out_2, w_up_2, w_down_2, outT):
    import math
    from contextlib import ExitStack

    import concourse.bass as bass
    from concourse import mybir

    f32, f32r, i32 = mybir.dt.float32, mybir.dt.float32r, mybir.dt.int32
    ALU, ACT, AX = mybir.AluOpType, mybir.ActivationFunctionType, mybir.AxisListType

    T = 256
    D = 2048
    KT = D // 128
    FF1, FF2 = 5632, 8192
    RAW_SLOTS, SPLIT_SLOTS = 4, 4
    PARAM, N_PARAM = plan(PARAM_COLUMNS)
    CONST, N_CONST = plan(CONST_COLUMNS)
    LO_CREDIT = 2 * RAW_SLOTS
    USED_CREDIT = SPLIT_SLOTS
    PAIR_CREDIT = 4

    ctx = ExitStack()
    with ctx:
        top = [(nc.sbuf_base + 31) // 32 * 32]

        def place(name, shape, dtype=f32, at=None):
            size = 4 * math.prod(shape[1:])
            if at is None:
                at = top[0]
                top[0] += (size + 31) // 32 * 32
            return nc.alloc_sbuf_tensor_at(name, shape, dtype, offset=at)

        cursor = [0]

        def put(name, shape):
            at = cursor[0]
            cursor[0] += (4 * math.prod(shape[1:]) + 31) // 32 * 32
            return place(name, shape, at=at)

        def region(size):
            at = top[0]
            top[0] += size
            return at


        raw = place("raw", [128, RAW_SLOTS, 2048])
        w_hi = place("w_hi", [128, SPLIT_SLOTS, 1024], f32r)
        w_lo = place("w_lo", [128, SPLIT_SLOTS, 1024], f32r)
        x = place("x", [128, KT, T])
        h_split = place("h_split", [128, KT, 2 * T], f32r)
        ACT_SPLIT = top[0]
        act_split = place("act_split", [128, KT, 2 * T], f32r)
        par = place("par", [128, N_PARAM])
        con = place("con", [128, N_CONST])
        low = place("low", [128, 2, 2, T])
        scaled = place("scaled", [128, 2, 2, T])
        squares = place("squares", [128, 2, 2, T])
        square_sum = place("square_sum", [128, 2, T])
        gate_pair = place("gate_pair", [128, 2, 2, T])
        root = place("root", [128, T])
        scale = place("scale", [128, T])
        pre_scale = place("pre_scale", [128, T])
        pos_i = place("pos_i", [128, T], i32)
        REGION = 32 * 1024 + 64
        C = region(REGION)
        assert top[0] <= nc.sbuf_top, (top[0], nc.sbuf_top)

        cursor[0] = C
        glu = put("glu", [128, 6, 30 + T])
        conv_b = put("conv_b", [128, 6, T])
        val_b = put("val_b", [128, 2, T])
        tanh_b = put("tanh_b", [128, 2, T])
        b_gate = put("b_gate", [128, 2, T])
        c_gate = put("c_gate", [128, 2, T])
        cv = put("cv", [128, 2, 2 + T])
        conv_a = put("conv_a", [128, 2, T])
        pool_in = put("pool_in", [128, 2, 16 + T])
        pool_sum = put("pool_sum", [128, 2, 16 + T])
        pooled = put("pooled", [128, 2, T])
        assert cursor[0] <= C + REGION, cursor[0] - C

        ln_squares = place("ln_squares", [128, 6, T], at=C)
        y = place("y", [128, KT, T], at=C)
        cursor[0] = C + KT * T * 4
        up_in = put("up_in", [128, 4, 2 + T])
        gate_conv = put("gate_conv", [128, 4, T])
        gate_tanh = put("gate_tanh", [128, 4, T])
        val_conv = put("val_conv", [128, 4, T])
        assert cursor[0] <= C + REGION, cursor[0] - C
        cursor[0] = C
        qk_in = put("qk_in", [128, 2, 3 + T])
        q_m = put("q_m", [128, 2, T])
        k_m = put("k_m", [128, 2, T])
        v_m = put("v_m", [128, 2, T])
        o_m = put("o_m", [128, 2, T])
        v_tok = put("v_tok", [128, 2, T])
        decay = put("decay", [128, 384])
        s_ts = put("s_ts", [128, 384])
        den_m = put("den_m", [128, 2, T])
        h_m = put("h_m", [128, 2, T])
        gcol = put("gcol", [128, 2, 4])
        row_g = put("row_g", [4, T])
        row_m = put("row_m", [4, T])
        row_n = put("row_n", [4, T])
        cos = put("cos", [128, T])
        sin = put("sin", [128, T])
        row_i = place("row_i", [4, T], at=cursor[0])
        row_f = place("row_f", [4, T], at=cursor[0] + 4 * T)
        a_q = put("a_q", [128, 2, T])
        a_k = put("a_k", [128, 2, T])
        a_v = put("a_v", [128, 2, T])
        prob_t = put("prob_t", [128, 384])
        a_stat = put("a_stat", [128, 8])
        assert cursor[0] <= C + REGION, cursor[0] - C
        merged = place("merged", [128, KT, 2 * T], f32r, at=C)
        y_2 = place("y_2", [128, KT, T], at=ACT_SPLIT)
        ps = ctx.enter_context(nc.psum_tensor("ps", [128, 8, 512], f32))

        def P(name, k=0, n=1):
            at = PARAM[name] + k
            return par[:, at:at + n] if isinstance(at, int) else par[:, bass.ds(at, n)]

        def K(name, k=0, n=1):
            return con[:, CONST[name] + k:CONST[name] + k + n]

        identity, ones = K("identity", 0, 128), K("ones", 0, 128)

        def flat(ap):
            return ap.rearrange("p a t -> p (a t)")

        def bcast(row, tiles=2):
            return row.rearrange("p (a t) -> p a t", a=1).to_broadcast([128, tiles, T])

        def sem(name):
            return ctx.enter_context(nc.semaphore(name))

        raw_full = [sem(f"raw_full{i}") for i in range(RAW_SLOTS)]
        hi_ready = sem("hi_ready")
        lo_ready = sem("lo_ready")
        piece_used = sem("piece_used")
        low_ready = sem("low_ready")
        pair_combined = sem("pair_combined")
        x_loaded = [sem(f"x_loaded{i}") for i in range(4)]
        gains_loaded, small_loaded, pos_loaded, forget_loaded, stored = (
            sem(n) for n in ("gains_loaded", "small_loaded", "pos_loaded", "forget_loaded", "stored"))
        cleared = sem("cleared")
        squares_ready = sem("squares_ready")
        squares_added = sem("squares_added")
        stat_summed = sem("stat_summed")
        mean_summed = sem("mean_summed")
        root_ready = sem("root_ready")
        scale_ready = sem("scale_ready")
        x_ready = sem("x_ready")
        norm_hi = sem("norm_hi")
        h_ready = sem("h_ready")

        vector_step = sem("vector_step")
        tanh_ready = sem("tanh_ready")
        glu_ready = sem("glu_ready")
        taps_done = sem("taps_done")
        tap_ready = sem("tap_ready")
        taps_added = sem("taps_added")
        conv_b_ready = sem("conv_b_ready")
        centered = sem("centered")
        ln_squared = sem("ln_squared")
        ln_scaled = sem("ln_scaled")
        ln_affine = sem("ln_affine")
        ln_tanh = sem("ln_tanh")
        ln_silu = sem("ln_silu")
        b_hi = sem("b_hi")
        b_split = sem("b_split")
        cv_ready = sem("cv_ready")
        conv_a_started = sem("conv_a_started")
        a_mixed = sem("a_mixed")
        a_hi = sem("a_hi")
        a_split = sem("a_split")
        pooled_ready = sem("pooled_ready")
        pool_summed = sem("pool_summed")
        c_hi = sem("c_hi")
        c_split = sem("c_split")
        conv_started = sem("conv_started")
        conv_done = sem("conv_done")
        gate_ready = sem("gate_ready")
        units_ready = sem("units_ready")
        unit_hi = sem("unit_hi")
        unit_split = sem("unit_split")
        y_summed = sem("y_summed")
        rows_split = sem("rows_split")
        row_step = sem("row_step")
        rows_ready = sem("rows_ready")
        columns_summed = sem("columns_summed")
        columns_ready = sem("columns_ready")
        angle_ready = sem("angle_ready")
        table_step = sem("table_step")
        qk_started = sem("qk_started")
        qk_convolved = sem("qk_convolved")
        qk_tanh = sem("qk_tanh")
        qk_ready = sem("qk_ready")
        o_ready = sem("o_ready")
        rows_bcast = sem("rows_bcast")
        m_scored = sem("m_scored")
        v_tok_ready = sem("v_tok_ready")
        decay_started = sem("decay_started")
        decay_ready = sem("decay_ready")
        s_ts_ready = sem("s_ts_ready")
        m_valued = sem("m_valued")
        den_ready = sem("den_ready")
        m_divided = sem("m_divided")
        m_squared = sem("m_squared")
        m_gated = sem("m_gated")
        m_hi = sem("m_hi")
        m_split = sem("m_split")
        rope_ready = sem("rope_ready")
        a_scored = sem("a_scored")
        a_v_ready = sem("a_v_ready")
        a_max_ready = sem("a_max_ready")
        a_exp_ready = sem("a_exp_ready")
        prob_ready = sem("prob_ready")
        prob_turned = sem("prob_turned")
        prob_t_ready = sem("prob_t_ready")
        a_valued = sem("a_valued")
        a_hi_2 = sem("a_hi_2")
        a_split_2 = sem("a_split_2")
        merge_tanh = sem("merge_tanh")
        merge_summed = sem("merge_summed")
        merge_hi = sem("merge_hi")
        merge_split = sem("merge_split")

        (N_PRE1, N_LN, N_POST1, N_PREF1, N_POSTF1, N_PRE2, N_HEAD) = range(7)
        N_POST2, N_PREF2, N_POSTF2 = (N_HEAD + 4 + n for n in range(3))
        SUMMED = {e: n for n, e in enumerate(
            (N_PRE1, N_POST1, N_PREF1, N_POSTF1, N_PRE2, N_POST2, N_PREF2, N_POSTF2))}
        PRE = {e: n for n, e in enumerate((N_PRE1, N_PREF1, N_PRE2, N_PREF2))}
        POST = {e: n for n, e in enumerate((N_POST1, N_POSTF1, N_POST2, N_POSTF2))}
        NORM_BANK = {N_POSTF1: 0, N_POSTF2: 0}
        FIRST_TWO = [(n // 2 % 2, n // 4 * 2 + n % 2) for n in range(8)]

        SUMMED_BEFORE = {e: max((f + 1 for f in SUMMED if f < e), default=0) for e in SUMMED}
        M_STAGE, M_STAGE_END = (0, 3, 7, 9), (2, 5, 9, 11)
        GATE_COLUMNS, GATE_COLUMNS_END = 14, 15
        A_STAGE, A_STAGE_END = ((2, 4, 6), (5, 8, 10)), ((3, 5, 7), (7, 9, 11))
        ROUND = 1.5 * 2.0 ** 23
        PI_BELOW = 3.1415925
        TURN_PARTS = turn_parts()

        def at_least(eng, s, value):
            if not isinstance(value, int) or value > 0:
                eng.wait_ge(s, value)

        NARROW, WIDE = 4, 8
        W1 = 0
        O1 = W1 + 17 * NARROW
        M1 = O1 + 4 * WIDE
        GROUPS1 = (4, 4, 3)
        up1, down1, at = [], [], M1
        for n in GROUPS1:
            up1.append(at)
            down1.append(at + n * 2 * WIDE)
            at += n * 2 * WIDE + 4 * (2 * n)
        W2 = at
        G2 = W2 + 2 * NARROW
        Y2 = W2 + 28 * NARROW + 2
        O2 = Y2 + 8 * 12
        M2 = O2 + 4 * WIDE
        END = M2 + 4 * 8 * WIDE
        qW1 = 0
        qO1 = qW1 + 17
        qup1, qdown1, at = [], [], qO1 + 8
        for n in GROUPS1:
            qup1.append(at)
            qdown1.append(at + 4 * n)
            at += 4 * n + 8
        qW2 = at
        qG2 = qW2 + 2
        qY2 = qW2 + 29
        qO2 = qY2 + 8 * 4
        qM2 = qO2 + 8

        def piece2(n):
            return W2 + n + (2 if n >= 2 * NARROW else 0)

        def pair2(c):
            return qW2 + c + (1 if c >= 2 else 0)

        def last_of(first, c):
            return first(NARROW * c + 3 + (2 if c == 0 else 0))

        CHUNKS1 = [(kind, j) for j in range(3) for kind in ("val", "gate")]
        CHUNKS1 += [(kind, j) for j in range(3) for kind in ("b", "c", "v")]
        CHUNKS1 += [("pool", j) for j in range(2)]
        COLUMN1 = {"b": 0, "c": 768, "v": 1536, "val": 2304, "gate": 3072, "pool": 3840}
        COLUMN2 = {"q": 0, "k": 1024, "v": 2048, "o": 3072, "aq": 4104, "ak": 5128, "av": 6152,
                   "gm": 7176, "ga": 9224}
        CHUNKS2 = [(kind, h) for h in range(4) for kind in ("q", "k", "v", "o")]
        CHUNKS2 += [(kind, j) for j in range(4) for kind in ("aq", "ak", "av")]

        block = ctx.enter_context(nc.Block())

        @block.sync
        def _(sp):
            GAINS = PARAM["conv_a_w"]

            def load_x(quarter):
                tiles = slice(4 * quarter, 4 * quarter + 4)
                sp.dma_start(x[:, tiles, :], xT[:, tiles, :]).then_inc(x_loaded[quarter], 16)

            def load(n, w, row, col, deep):
                slot, cols = n.slot(RAW_SLOTS), 2048 // deep
                sp.wait_ge(lo_ready, n.times(2).value(2))
                sp.dma_start(raw[:, slot, :].rearrange("p (k n) -> p k n", k=deep),
                             w[row:row + 128 * deep, bass.ds(col, cols)].rearrange("(k p) n -> p k n", p=128)
                             ).then_inc(raw_full[slot], 16)

            def load_in(n, w, chunks, column, c, b):
                kind, j = chunks[c]
                load(Step(n), w, 1024 * b, column[kind] + 256 * j, 8)

            def load_first_two(i, w, chunks, column, first):
                load_in(first // 2 + i, w, chunks, column, i % 2, i // 2)

            load_x(0)
            sp.dma_start(par[:, 0:GAINS], params[:, 0:GAINS]).then_inc(gains_loaded, 16)
            load_first_two(0, w_in, CHUNKS1, COLUMN1, W1)
            load_x(1)
            load_x(2)
            load_x(3)
            load_first_two(1, w_in, CHUNKS1, COLUMN1, W1)
            sp.dma_start(con[:, :], consts).then_inc(small_loaded, 16)
            sp.dma_start(par[:, GAINS:], params[:, GAINS:]).then_inc(small_loaded, 16)
            load_first_two(2, w_in, CHUNKS1, COLUMN1, W1)
            load_first_two(3, w_in, CHUNKS1, COLUMN1, W1)
            for c in range(2, 17):
                for b in range(2):
                    load_in(W1 // 2 + 2 * c + b, w_in, CHUNKS1, COLUMN1, c, b)
            with sp.Fori(1, 5) as i:
                for b in range(4):
                    load(Step(O1 // 2 + b - 4, i, 4), w_out, 512 * b, i * 512 - 512, 4)
            first = 0
            for g, n in enumerate(GROUPS1):
                with sp.Fori(1, n + 1) as i:
                    for half in range(2):
                        for b in range(4):
                            load(Step(up1[g] // 2 + 4 * half + b - 8, i, 8),
                                 w_up, 512 * b, i * 512 + (FF1 * half + 512 * (first - 1)), 4)
                for i in range(4):
                    for b in range(n):
                        load(Step(down1[g] // 2 + n * i + b), w_down, 512 * (first + b), i * 512, 4)
                first += n
            for i in range(4):
                load_first_two(i, w_in_2, CHUNKS2, COLUMN2, W2)
            n = Step(G2 // 2)
            slot = n.slot(RAW_SLOTS)
            sp.wait_ge(lo_ready, n.base * 2 + 2)
            gates = raw[:, slot, :].rearrange("p (k s n) -> p k s n", k=16, s=2)
            for half, s in enumerate((raw_full[slot], forget_loaded)):
                sp.dma_start(gates[:, :, half, :],
                             w_in_2[:, 4096 + 4 * half:4160 + 4 * half].rearrange("(k p) n -> p k n", p=128)
                             ).then_inc(s, 16)
            for c in range(2, 28):
                for b in range(2):
                    load_in(piece2(4 * c + 2 * b) // 2, w_in_2, CHUNKS2, COLUMN2, c, b)
            with sp.Fori(1, 5) as i:
                for half in range(2):
                    for b, kind in enumerate(("gm", "ga")):
                        for g in range(2):
                            load(Step(Y2 // 2 + 6 * half + 2 * b + g - 12, i, 12),
                                 w_in_2, 1024 * g, i * 512 + (COLUMN2[kind] + 256 * half - 512), 8)
                    for g, w in enumerate((w_branch_m_2, w_branch_a_2)):
                        load(Step(Y2 // 2 + 6 * half + 4 + g - 12, i, 12), w, 0, i * 512 + (256 * half - 512), 8)
            with sp.Fori(1, 5) as i:
                for b in range(4):
                    load(Step(O2 // 2 + b - 4, i, 4), w_out_2, 512 * b, i * 512 - 512, 4)
            for g in range(4):
                with sp.Fori(1, 5) as i:
                    for b in range(4):
                        load(Step(M2 // 2 + 32 * g + b - 4, i, 4), w_up_2, 512 * b, i * 512 + (2048 * g - 512), 4)
                with sp.Fori(1, 5) as i:
                    for b in range(4):
                        load(Step(M2 // 2 + 32 * g + 16 + b - 4, i, 4), w_down_2, 2048 * g + 512 * b, i * 512 - 512, 4)
            for q in range(8):
                sp.wait_ge(x_ready, 8 * POST[N_POSTF2] + q + 1)
                sp.dma_start(outT[:, 2 * q:2 * q + 2, :], x[:, 2 * q:2 * q + 2, :]).then_inc(stored, 16)
            sp.wait_ge(stored, 8 * 16)

        @block.tensor
        def _(pe):
            def piece(n, p, kn, banks, rhs, pieces, need=None):
                slot, across = n.slot(SPLIT_SLOTS), len(banks)
                pe.wait_ge(lo_ready, n.value(LO_CREDIT + 1))
                for kk in range(kn):
                    k = p * kn + kk
                    if need is not None and (k % 2 == 0 or kn == 1):
                        ready, value = need(k)
                        pe.wait_ge(ready, value)
                    for t, bank in enumerate(banks):
                        cols = slice((kk * across + t) * 128, (kk * across + t + 1) * 128)
                        nc.tensor.matmul(ps[:, bank, :], w_hi[:, slot, cols], rhs[:, k, :],
                                         start=(k == 0), stop=False)
                        last = nc.tensor.matmul(ps[:, bank, T:2 * T], w_lo[:, slot, cols], rhs[:, k, 0:T],
                                                start=False, stop=(k == pieces * kn - 1))
                last.then_inc(piece_used, 1)

            def narrow_chunk(n, q, bank, rhs, pieces=4, need=None, between=None, after=1):
                pe.wait_ge(pair_combined, q.value(PAIR_CREDIT - after))
                for p in range(pieces):
                    if between is not None:
                        between(p)
                    piece(n.plus(p), p, 4, (bank, bank + 1), rhs, pieces, need)

            def wide_chunk(n, q, bank, rhs, pieces=8, need=None, after=2, between=None):
                if after is not None:
                    pe.wait_ge(pair_combined, q.value(PAIR_CREDIT - after))
                for p in range(pieces):
                    if between is not None:
                        between(p)
                    piece(n.plus(p), p, 2, range(bank, bank + 4), rhs, pieces, need)

            def sum_channels(tiles, bank, summed, first=True, last=True):
                for i, tile in enumerate(tiles):
                    ins = nc.tensor.matmul(ps[:, bank, 0:T], ones, tile, start=first and i == 0,
                                           stop=last and i == len(tiles) - 1)
                if last:
                    ins.then_inc(summed, 1)

            def sum_norm(norm):
                bank = NORM_BANK.get(norm, 7)
                pe.wait_ge(squares_added, 7 * (SUMMED[norm] + 1))
                sum_channels([square_sum[:, 0, :], square_sum[:, 1, :]], bank, None, last=False)
                pe.wait_ge(squares_ready, 8 * (SUMMED[norm] + 1))
                sum_channels([squares[:, 1, 0, :], squares[:, 1, 1, :]], bank, stat_summed, first=False)

            def first_two(first, need, norm):
                for n, (c, p) in enumerate(FIRST_TWO):
                    if n == 6:
                        sum_norm(norm)
                    piece(Step(first + n), p, 4, (2 * c, 2 * c + 1), h_split, 4, need)

            def h_need(norm):
                return lambda k: (h_ready, 8 * PRE[norm] + k // 2 + 1)

            pe.sem_inc(piece_used, USED_CREDIT)
            first_two(W1, h_need(N_PRE1), N_PRE1)
            with pe.Fori(1, 7) as i:
                for c in range(2):
                    narrow_chunk(Step(W1 + 4 * c, i, 8), Step(qW1 + c, i, 2), 2 * c, h_split)

            def layer_norm(c, p):
                if (c, p) == (15, 1):
                    pe.wait_ge(conv_b_ready, 6)
                    sum_channels([conv_b[:, t, :] for t in range(6)], 7, mean_summed)
                elif (c, p) == (16, 1):
                    pe.wait_ge(ln_squared, 3)
                    sum_channels([ln_squares[:, t, :] for t in range(6)], 7, stat_summed)

            for c in range(14, 17):
                narrow_chunk(Step(W1 + 4 * c), Step(qW1 + c), 2 * (c % 2), h_split,
                             between=lambda p: layer_norm(c, p))

            def pool_product(j):
                pe.wait_ge(pooled_ready, j + 1)
                for t in range(2):
                    last = nc.tensor.matmul(ps[:, 2 + j, T * t:T * t + T], P("pool_w", 128 * (2 * j + t), 128),
                                            pooled[:, t, :], start=True, stop=True)
                last.then_inc(pool_summed, 1)

            def mixed(k):
                if k < 6:
                    return a_split, k // 2 + 1
                return (b_split, (k - 6) // 2 + 1) if k < 12 else (c_split, (k - 12) // 2 + 1)

            def pools(p):
                if p == 1:
                    pool_product(0)
                elif p == 5:
                    pool_product(1)

            pe.wait_ge(root_ready, N_LN + 1)
            for c in range(4):
                wide_chunk(Step(O1 + 8 * c), Step(qO1 + 2 * c), 4 * ((c + 1) % 2), act_split,
                           need=mixed if c == 0 else None, after=2 if c else None, between=pools if c == 0 else None)
            sum_norm(N_POST1)

            def last_piece_sum(norm):
                return lambda p: sum_norm(norm) if p == 7 else None

            units = 0
            wide_chunk(Step(M1), Step(qup1[0]), 0, h_split, need=h_need(N_PREF1), between=last_piece_sum(N_PREF1))
            pe.wait_ge(root_ready, N_PREF1 + 1)
            wide_chunk(Step(M1 + 8), Step(qup1[0] + 2), 4, h_split)
            for g, n in enumerate(GROUPS1):
                with pe.Fori(0 if g else 1, n) as i:
                    for half in range(2):
                        wide_chunk(Step(up1[g] + 8 * half, i, 16), Step(qup1[g] + 2 * half, i, 4), 4 * half, h_split)
                with pe.Fori(0, 2) as i:
                    for c in range(2):
                        wide_chunk(Step(down1[g] + 2 * n * c, i, 4 * n), Step(qdown1[g] + 2 * c, i, 4), 4 * c,
                                   act_split, pieces=2 * n,
                                   need=(lambda k: (unit_split, units + k // 2 + 1)) if c == 0 else None)
                units += 2 * n
            sum_norm(N_POSTF1)
            first_two(W2, h_need(N_PRE2), N_PRE2)
            for p in range(2):
                piece(Step(G2 + p), p, 8, (4,), h_split, 2)

            def gate_columns():
                pe.wait_ge(rows_ready, 1)
                for half in range(2):
                    last = nc.tensor.matmul(ps[:, 6, 4 * half:4 * half + 4], row_g[0:4, 128 * half:128 * half + 128],
                                            identity[0:4, 0:4], start=True, stop=True)
                last.then_inc(columns_summed, 1)

            def mlstm(h, stage):
                if stage == 0:
                    pe.wait_ge(columns_ready, 1)
                    pe.wait_ge(qk_ready, 2 * h + 2)
                    pe.wait_ge(pair_combined, PAIR_CREDIT + pair2(4 * h + 2) + 1)
                    at_least(pe, m_split, h)
                    for r, row in enumerate((row_m, row_n)):
                        last = nc.tensor.matmul(ps[:, 7, T * r:T * r + T], K("select", 128 * h, 128)[0:4, :],
                                                row[0:4, :], start=True, stop=True)
                    last.then_inc(rows_bcast, 1)
                    for s in range(2):
                        out = ps[:, 4, 0:256] if s == 0 else ps[:, 4, 256:384]
                        for t in range(2):
                            nc.tensor.matmul(out, k_m[:, t, 128 * s:128 * s + 128], q_m[:, t, 128 * s:T],
                                             start=(t == 0), stop=(t == 1))
                    for s in range(2):
                        for t in range(2):
                            last = nc.tensor.transpose(ps[:, 5, T * s + 128 * t:T * s + 128 * t + 128],
                                                       v_m[:, t, 128 * s:128 * s + 128], identity)
                    last.then_inc(m_scored, 1)
                elif stage == 1:
                    pe.wait_ge(v_tok_ready, h + 1)
                    pe.wait_ge(s_ts_ready, h + 1)
                    for out, stationary in (((5, 0), lambda s: v_tok[:, s, 0:128]),
                                            ((5, T), lambda s: v_tok[:, s, 128:256]),
                                            ((6, 0), lambda s: ones)):
                        bank, col = out
                        nc.tensor.matmul(ps[:, bank, col:col + T], stationary(0), s_ts[:, 0:256],
                                         start=True, stop=False)
                        last = nc.tensor.matmul(ps[:, bank, col + 128:col + T], stationary(1), s_ts[:, 256:384],
                                                start=False, stop=True)
                    last.then_inc(m_valued, 1)
                elif stage == 2:
                    pe.wait_ge(m_squared, h + 1)
                    sum_channels([den_m[:, 0, :], den_m[:, 1, :]], 7, stat_summed)

            def attention(j, a, stage):
                t = 2 * j + a
                if stage == 0:
                    pe.wait_ge(rope_ready, 2 * j + 2)
                    pe.wait_ge(pair_combined, PAIR_CREDIT + pair2(16 + 3 * j + 2) + 1)
                    pe.wait_ge(m_split, 4)
                    at_least(pe, prob_ready, t)
                    at_least(pe, a_v_ready, t)
                    nc.tensor.matmul(ps[:, 4, 0:128], a_q[:, a, 0:128], a_k[:, a, 0:128], start=True, stop=True)
                    nc.tensor.matmul(ps[:, 4, 128:384], a_q[:, a, 128:256], a_k[:, a, :], start=True, stop=True)
                    for s in range(2):
                        last = nc.tensor.transpose(ps[:, 5, 128 * s:128 * s + 128],
                                                   a_v[:, a, 128 * s:128 * s + 128], identity)
                    last.then_inc(a_scored, 1)
                elif stage == 1:
                    pe.wait_ge(prob_ready, t + 1)
                    for s in range(3):
                        last = nc.tensor.transpose(ps[:, 6, 128 * s:128 * s + 128],
                                                   s_ts[:, 128 * s:128 * s + 128], identity)
                    last.then_inc(prob_turned, 1)
                else:
                    pe.wait_ge(prob_t_ready, t + 1)
                    at_least(pe, a_split_2, t)
                    nc.tensor.matmul(ps[:, 7, 0:256], v_tok[:, 0, 0:128], prob_t[:, 0:256], start=True, stop=False)
                    nc.tensor.matmul(ps[:, 7, 128:256], v_tok[:, 0, 128:256], prob_t[:, 256:384],
                                     start=False, stop=True).then_inc(a_valued, 1)

            def inner(piece_number):
                if piece_number == GATE_COLUMNS:
                    gate_columns()
                for h in range(4):
                    r = piece_number - 16 * (h + 1)
                    if r in M_STAGE:
                        mlstm(h, M_STAGE.index(r))
                for j in range(4):
                    r = piece_number - (64 + 12 * (j + 1))
                    for a in range(2):
                        if r in A_STAGE[a]:
                            attention(j, a, A_STAGE[a].index(r))

            for c in range(2, 28):
                narrow_chunk(Step(piece2(4 * c)), Step(pair2(c)), 2 * (c % 2), h_split,
                             between=lambda p: inner(4 * c + p), after=2 if c == 2 else 1)

            def merge_chunks(i, between=lambda n: None):
                for half in range(2):
                    n, q = Step(Y2 + 12 * half, i, 24), Step(qY2 + 4 * half, i, 8)
                    narrow_chunk(n, q, 0, h_split, between=lambda p: between(12 * half + p))
                    narrow_chunk(n.plus(4), q.plus(1), 2, h_split, between=lambda p: between(12 * half + 4 + p))
                    narrow_chunk(n.plus(8), q.plus(2), 0, act_split[:, 0:8, :], pieces=2,
                                 between=lambda p: between(12 * half + 8 + p),
                                 need=lambda k: (m_split, 4))
                    narrow_chunk(n.plus(10), q.plus(3), 2, act_split[:, 8:16, :], pieces=2,
                                 between=lambda p: between(12 * half + 10 + p),
                                 need=lambda k: (a_split_2, 8))

            merge_chunks(None, between=lambda n: inner(112 + n))
            with pe.Fori(1, 4) as i:
                merge_chunks(i)
            wide_chunk(Step(O2), Step(qO2), 4, merged, need=lambda k: (merge_split, k // 2 + 1), after=None)
            for c in range(1, 4):
                wide_chunk(Step(O2 + 8 * c), Step(qO2 + 2 * c), 4 * ((c + 1) % 2), merged)
            sum_norm(N_POST2)
            wide_chunk(Step(M2), Step(qM2), 0, h_split, need=h_need(N_PREF2), between=last_piece_sum(N_PREF2))
            pe.wait_ge(root_ready, N_PREF2 + 1)

            def group_2(g, up_from=0):
                for c in range(up_from, 4):
                    wide_chunk(Step(M2 + 8 * c).along(g, 64), Step(qM2 + 2 * c).along(g, 16), 4 * (c % 2), h_split)
                with pe.Fori(0, 2) as i:
                    for c in range(2):
                        wide_chunk(Step(M2 + 32 + 8 * c, i, 16).along(g, 64), Step(qM2 + 8 + 2 * c, i, 4).along(g, 16),
                                   4 * c, act_split,
                                   need=(lambda k: (unit_split, Step(22 + k // 2 + 1).along(g, 8).value()))
                                   if c == 0 else None)

            group_2(None, up_from=1)
            with pe.Fori(1, 4) as g:
                group_2(g)
            sum_norm(N_POSTF2)

        @block.scalar
        def _(act):
            def split(n):
                block_n = Step(n.base // 2, terms=tuple((i, r // 2) for i, r in n.terms))
                slot, half = block_n.slot(RAW_SLOTS), 1024 * (n.base % 2)
                if not half:
                    act.wait_ge(raw_full[slot], block_n.turn(RAW_SLOTS).times(16).value(16))
                act.wait_ge(piece_used, n.value(1))
                nc.scalar.activation(w_hi[:, n.slot(SPLIT_SLOTS), :], raw[:, slot, half:half + 1024],
                                     ACT.Copy).then_inc(hi_ready, 1)

            def low_copy(q, bank, last, tiles=2):
                act.wait_ge(piece_used, last.value(USED_CREDIT + 1))
                act.wait_ge(pair_combined, q.value(PAIR_CREDIT - 1))
                nc.scalar.activation(low[:, q.slot(2), 0:tiles, :], ps[:, bank:bank + tiles, T:2 * T],
                                     ACT.Copy).then_inc(low_ready, 1)

            def combined(q):
                act.wait_ge(pair_combined, q.value(PAIR_CREDIT + 1))

            def square(norm, q, ready, value, source):
                s = 8 * SUMMED[norm] + q
                act.wait_ge(ready, value)
                if q == 1:
                    at_least(act, stat_summed, SUMMED_BEFORE[norm])
                else:
                    at_least(act, squares_added, 7 * SUMMED[norm] + max(q - 1, 0))
                nc.scalar.activation(squares[:, s % 2, :, :], source[:, 2 * q:2 * q + 2, :],
                                     ACT.Square).then_inc(squares_ready, 1)

            def take_root(norm, channels, times=1):
                act.wait_ge(stat_summed, norm + 1)
                at_least(act, scale_ready, norm)
                eps = K("epsilon", {1: 0, 2: 2}[times] if norm != N_LN else 1)
                nc.scalar.activation(root[:, :], ps[:, NORM_BANK.get(norm, 7), 0:T], ACT.Sqrt, bias=eps,
                                     scale=times * times / channels).then_inc(root_ready, 1)

            def pre_pair(norm, gain, q, ready, value):
                act.wait_ge(ready, value)
                for k in range(2 * q, 2 * q + 2):
                    nc.scalar.activation(h_split[:, k, 0:T], x[:, k, :], ACT.Copy, scale=P(gain, k)
                                         ).then_inc(norm_hi, 1)
                square(norm, q, ready, value, x)

            act.dma_start(pos_i[:, :], positions.partition_broadcast(128)).then_inc(pos_loaded, 16)
            act.wait_ge(gains_loaded, 16)
            split(Step(W1))
            for q in range(8):
                pre_pair(N_PRE1, "norm_mix_pre", q, x_loaded[q // 2], 16)
                if q in (1, 3, 5, 7):
                    split(Step(W1 + q // 2 + 1))
            act.wait_ge(small_loaded, 32)

            def finish_conv_b(j):
                if j == 2:
                    act.wait_ge(taps_added, 30)
                else:
                    act.wait_ge(taps_done, j + 1)
                for t in range(2 * j, 2 * j + 2):
                    nc.scalar.activation(conv_b[:, t, :], conv_b[:, t, :], ACT.Identity, scale=0.5,
                                         bias=P("conv_b_bias", t)).then_inc(conv_b_ready, 1)

            def tap_b(k):
                if k == 0:
                    act.wait_ge(glu_ready, 3)
                    act.wait_ge(cleared, 3)
                elif k > 2:
                    act.wait_ge(taps_added, k - 2)
                for t in range(2):
                    out = gate_pair[:, k % 2, t, :] if k else conv_b[:, 4 + t, :]
                    nc.scalar.activation(out, glu[:, 4 + t, k:k + T], ACT.Copy, scale=P("conv_b_w", 6 * k + 4 + t)
                                         ).then_inc(tap_ready, 1)

            def chunk_end_1(c):
                kind, j = CHUNKS1[c]
                q = Step(qW1 + c)
                low_copy(q, 2 * (c % 2), Step(last_of(lambda n: W1 + n, c)))
                if kind == "gate":
                    combined(q)
                    nc.scalar.activation(tanh_b[:, :, :], tanh_b[:, :, :], ACT.Tanh, scale=0.5).then_inc(tanh_ready, 1)
                elif kind == "v":
                    act.wait_ge(cv_ready, j + 1)
                    for t in range(2):
                        nc.scalar.activation(conv_a[:, t, :], cv[:, t, 2:2 + T], ACT.Copy,
                                             scale=P("conv_a_w", 12 + 2 * j + t)).then_inc(conv_a_started, 1)
                    act.wait_ge(a_mixed, j + 1)
                    nc.scalar.activation(act_split[:, 2 * j:2 * j + 2, 0:T], conv_a[:, :, :],
                                         ACT.Copy).then_inc(a_hi, 1)

            def layer_norm(n):
                if n == 63:
                    for j in range(3):
                        act.wait_ge(centered, j + 1)
                        nc.scalar.activation(ln_squares[:, 2 * j:2 * j + 2, :], conv_b[:, 2 * j:2 * j + 2, :],
                                             ACT.Square).then_inc(ln_squared, 1)
                elif n == 66:
                    take_root(N_LN, 768)
                elif n == O1:
                    for j in range(3):
                        act.wait_ge(ln_scaled, j + 1)
                        for t in range(2 * j, 2 * j + 2):
                            nc.scalar.activation(conv_b[:, t, :], conv_b[:, t, :], ACT.Identity,
                                                 scale=P("ln_b_gain", t), bias=P("ln_b_bias", t)).then_inc(ln_affine, 1)
                        act.wait_ge(ln_affine, 2 * j + 2)
                        nc.scalar.activation(ln_squares[:, 2 * j:2 * j + 2, :], conv_b[:, 2 * j:2 * j + 2, :],
                                             ACT.Tanh, scale=0.5).then_inc(ln_tanh, 1)
                elif n == O1 + 1:
                    for j in range(3):
                        act.wait_ge(ln_silu, j + 1)
                        nc.scalar.activation(act_split[:, 6 + 2 * j:8 + 2 * j, 0:T], conv_b[:, 2 * j:2 * j + 2, :],
                                             ACT.Copy, scale=0.5).then_inc(b_hi, 1)

            def pool_end(j):
                act.wait_ge(pool_summed, j + 1)
                for t in range(2):
                    k = 2 * j + t
                    nc.scalar.activation(act_split[:, 12 + k, 0:T], ps[:, 2 + j, T * t:T * t + T], ACT.Copy,
                                         scale=P("pool_scale", k)).then_inc(c_hi, 1)

            for c in range(17):
                for p in range(4):
                    n = 4 * c + p
                    if n > 4:
                        split(Step(W1 + n))
                    if n == 9:
                        take_root(N_PRE1, D)
                        chunk_end_1(0)
                    elif p == 3 and c > 1:
                        chunk_end_1(c - 1)
                    if 27 <= n < 58:
                        tap_b(n - 27)
                    if n in (40, 59, 60):
                        finish_conv_b({40: 0, 59: 2, 60: 1}[n])
                    layer_norm(n)

            def wide_end(q, bank, last, r):
                low_copy(q.plus(r), bank + 2 * r, last)

            def y_squares(norm, q0, q, y):
                square(norm, q, *y_pair_ready(norm, q0, q), y)

            def y_pair_ready(norm, q0, q):
                if norm in (N_POST1, N_POST2):
                    return pair_combined, PAIR_CREDIT + q0 + q + 1
                groups = len(GROUPS1) - 1 if norm == N_POSTF1 else len(GROUPS1) - 1 + 3
                return y_summed, 8 * (groups - 1) + q + 1

            def out_product(n0, q0, pieces, norm, y, before, between=lambda n: None, flip=0):
                for c in range(4):
                    for p in range(pieces):
                        split(Step(n0 + pieces * c + p))
                        between(n0 + pieces * c + p)
                        before(pieces * c + p)
                        if p in (3, 4):
                            r = p - 3
                            if c:
                                wide_end(Step(q0 + 2 * c - 2), 4 * ((c - 1 + flip) % 2),
                                         Step(n0 + pieces * c - 1), r)
                                if norm is not None:
                                    y_squares(norm, q0, 2 * c - 2 + r, y)

            def last_chunk(n0, q0, pieces, norm, y, next_piece=None, flip=0):
                if next_piece is not None:
                    for p in range(3):
                        split(Step(next_piece + p))
                for r in range(2):
                    wide_end(Step(q0 + 6), 4 * (1 - flip), Step(n0 + 4 * pieces - 1), r)
                    if norm is not None:
                        y_squares(norm, q0, 6 + r, y)

            def post_and_pre(post, pre, gain, next_piece):
                split(Step(next_piece + 3))
                take_root(post, D)
                for q in range(8):
                    pre_pair(pre, gain, q, x_ready, 8 * POST[post] + q + 1)
                    if 3 <= q < 7:
                        split(Step(next_piece + q + 1))

            def first_pools(n):
                layer_norm(n)
                if n == O1 + 4:
                    pool_end(0)
                elif n == O1 + 6:
                    pool_end(1)

            out_product(O1, qO1, 8, N_POST1, y, before=lambda p: chunk_end_1(16) if p == 3 else None,
                        between=first_pools, flip=1)
            last_chunk(O1, qO1, 8, N_POST1, y, M1, flip=1)
            post_and_pre(N_POST1, N_PREF1, "norm_ffn_pre", M1)

            def start_conv(chunk, r, half, out):
                for t in range(2):
                    k = chunk.times(4).value(44 * half + 2 * r + t)
                    nc.scalar.activation(out[:, 2 * r + t, :], up_in[:, 2 * r + t, 2:2 + T], ACT.Identity,
                                         scale=P("conv_ffn_w", 2 * 88 + k), bias=P("conv_ffn_bias", k)
                                         ).then_inc(conv_started, 1)

            def gate_end(n0, q0, chunk, p):
                if p in (3, 4):
                    r = p - 3
                    low_copy(q0.plus(r), 2 * r, n0.plus(7))
                if p in (4, 5):
                    r = p - 4
                    combined(q0.plus(r))
                    start_conv(chunk, r, 0, gate_conv)
                if p in (6, 7):
                    r = p - 6
                    act.wait_ge(conv_done, chunk.times(2).value(r + 1))
                    pair = slice(2 * r, 2 * r + 2)
                    nc.scalar.activation(gate_tanh[:, pair, :], gate_conv[:, pair, :], ACT.Tanh,
                                         scale=0.5).then_inc(gate_ready, 1)

            def val_end(n0, q0, chunk, first, p):
                if p in (3, 4):
                    r = p - 3
                    low_copy(q0.plus(2 + r), 4 + 2 * r, n0.plus(15))
                if p in (4, 5):
                    r = p - 4
                    combined(q0.plus(2 + r))
                    start_conv(chunk, r, 1, val_conv)
                if p in (6, 7):
                    r = p - 6
                    act.wait_ge(units_ready, chunk.times(2).value(r + 1))
                    k = chunk.times(4).value(2 * r - 4 * first)
                    nc.scalar.activation(act_split[:, at2(k), 0:T], gate_conv[:, 2 * r:2 * r + 2, :], ACT.Copy,
                                         scale=0.5).then_inc(unit_hi, 1)

            def at2(k):
                return slice(k, k + 2) if isinstance(k, int) else bass.ds(k, 2)

            def up_chunks(g, first, i, before, skip=0):
                n0, q0 = Step(up1[g], i, 16), Step(qup1[g], i, 4)
                chunk = Step(first, i, 1)
                for p in range(16):
                    if p >= skip:
                        split(n0.plus(p))
                    if skip and p == 9:
                        take_root(N_PREF1, D)
                    before(p)
                    gate_end(n0, q0, chunk, p - 8)

            def down_end(q0, last):
                def before(p):
                    if p in (3, 4):
                        wide_end(Step(q0 + 6), 4, Step(last), p - 3)
                return before

            first = 0
            for g, n in enumerate(GROUPS1):
                if g == 0:
                    up_chunks(0, 0, None, lambda p: None, skip=8)
                else:
                    up_chunks(g, first, None, down_end(qdown1[g - 1], down1[g - 1] + 8 * GROUPS1[g - 1] - 1))
                with act.Fori(1, n) as i:
                    up_chunks(g, first, i, lambda p: val_end(
                        Step(up1[g] - 16, i, 16), Step(qup1[g] - 4, i, 4), Step(first - 1, i, 1), first, p))
                last = g == len(GROUPS1) - 1
                out_product(down1[g], qdown1[g], 2 * n, N_POSTF1 if last else None, y, before=lambda p: val_end(
                    Step(up1[g] + 16 * (n - 1)), Step(qup1[g] + 4 * (n - 1)), Step(first + n - 1), first, p))
                first += n
            last_chunk(down1[-1], qdown1[-1], 2 * n, N_POSTF1, y, W2)
            post_and_pre(N_POSTF1, N_PRE2, "norm_mix_pre_2", W2)

            def gate_rows():
                low_copy(Step(qG2), 4, Step(G2 + 1), tiles=1)
                act.wait_ge(rows_split, 1)
                nc.scalar.activation(row_g[0:4, :], row_f[0:4, :], ACT.Abs).then_inc(row_step, 1)
                act.wait_ge(row_step, 1)
                nc.scalar.activation(row_g[0:4, :], row_g[0:4, :], ACT.Exp, scale=-1.0).then_inc(row_step, 1)
                act.wait_ge(row_step, 2)
                nc.scalar.activation(row_g[0:4, :], row_g[0:4, :], ACT.Ln, bias=ones[0:4, 0:1]).then_inc(row_step, 1)

            def rope_tables():
                act.wait_ge(angle_ready, 1)
                nc.scalar.activation(sin[:, :], cos[:, :], ACT.Sin, scale=K("sign")).then_inc(table_step, 1)
                act.wait_ge(table_step, 1)
                nc.scalar.activation(cos[:, :], cos[:, :], ACT.Abs).then_inc(table_step, 1)
                act.wait_ge(table_step, 2)
                nc.scalar.activation(cos[:, :], cos[:, :], ACT.Sin, scale=-1.0, bias=K("half_pi")
                                     ).then_inc(table_step, 1)

            def chunk_end_2(c):
                kind, h = CHUNKS2[c]
                q = Step(pair2(c))
                low_copy(q, 2 * (c % 2), Step(last_of(piece2, c)))
                if kind in ("q", "k"):
                    is_k = int(kind == "k")
                    out = (q_m, k_m)[is_k]
                    combined(q)
                    at_least(act, m_scored, h)
                    for t in range(2):
                        k = 8 * is_k + 2 * h + t
                        nc.scalar.activation(out[:, t, :], qk_in[:, t, 3:3 + T], ACT.Identity,
                                             scale=P("conv_w_2", 48 + k), bias=P("conv_b_2", k)
                                             ).then_inc(qk_started, 1)
                    act.wait_ge(qk_convolved, 2 * h + is_k + 1)
                    nc.scalar.activation(squares[:, is_k, :, :], out[:, :, :], ACT.Tanh, scale=0.5
                                         ).then_inc(qk_tanh, 1)
                elif kind == "o":
                    combined(q)
                    nc.scalar.activation(o_m[:, :, :], o_m[:, :, :], ACT.Tanh, scale=0.5).then_inc(o_ready, 1)

            def mlstm(h, stage):
                if stage == 0:
                    act.wait_ge(m_scored, h + 1)
                    at_least(act, m_valued, h)
                    nc.scalar.activation(v_tok[:, :, :].rearrange("p a t -> p (a t)"), ps[:, 5, :],
                                         ACT.Copy).then_inc(v_tok_ready, 1)
                    act.wait_ge(decay_started, h + 1)
                    nc.scalar.activation(decay[:, :], decay[:, :], ACT.Exp, scale=-1.0).then_inc(decay_ready, 1)
                elif stage == 1:
                    act.wait_ge(m_valued, h + 1)
                    nc.scalar.activation(den_m[:, 0, :], ps[:, 6, 0:T], ACT.Abs).then_inc(den_ready, 1)
                    nc.scalar.activation(den_m[:, 1, :], ps[:, 7, T:2 * T], ACT.Exp).then_inc(den_ready, 1)
                    act.wait_ge(m_divided, h + 1)
                    nc.scalar.activation(den_m[:, :, :], h_m[:, :, :], ACT.Square).then_inc(m_squared, 1)
                elif stage == 2:
                    take_root(N_HEAD + h, 256, times=2)
                else:
                    act.wait_ge(m_gated, h + 1)
                    for t in range(2):
                        nc.scalar.activation(act_split[:, 2 * h + t, 0:T], h_m[:, t, :], ACT.Copy,
                                             scale=P("mlstm_norm_2", 2 * h + t)).then_inc(m_hi, 1)

            def attention(t, stage):
                if stage == 0:
                    act.wait_ge(a_scored, t + 1)
                    act.wait_ge(m_valued, 4)
                    at_least(act, a_valued, t)
                    nc.scalar.activation(v_tok[:, 0, :], ps[:, 5, 0:T], ACT.Copy).then_inc(a_v_ready, 1)
                    act.wait_ge(a_max_ready, t + 1)
                    for half, cols in enumerate((slice(0, 128), slice(128, 384))):
                        nc.scalar.activation(decay[:, cols], decay[:, cols], ACT.Exp,
                                             bias=a_stat[:, 2 + half:3 + half],
                                             accum_out=a_stat[:, 4 + half:5 + half]).then_inc(a_exp_ready, 1)
                elif stage == 1:
                    act.wait_ge(prob_turned, t + 1)
                    at_least(act, a_valued, t)
                    nc.scalar.activation(prob_t[:, :], ps[:, 6, 0:384], ACT.Copy).then_inc(prob_t_ready, 1)
                else:
                    act.wait_ge(a_valued, t + 1)
                    nc.scalar.activation(act_split[:, 8 + t, 0:T], ps[:, 7, 0:T], ACT.Copy).then_inc(a_hi_2, 1)

            def inner(n):
                if n == 11:
                    gate_rows()
                elif n == 14:
                    rope_tables()
                for h in range(4):
                    r = n - 16 * (h + 1)
                    if r in M_STAGE_END:
                        mlstm(h, M_STAGE_END.index(r))
                for j in range(4):
                    r = n - (64 + 12 * (j + 1))
                    for a in range(2):
                        if r in A_STAGE_END[a]:
                            attention(2 * j + a, A_STAGE_END[a].index(r))

            for n in range(7, 4 * 28):
                if n > 7:
                    split(Step(piece2(n)))
                else:
                    act.wait_ge(forget_loaded, 16)
                    for p in range(2):
                        split(Step(G2 + p))
                    take_root(N_PRE2, D)
                    chunk_end_2(0)
                if n == 9:
                    chunk_end_2(1)
                elif n % 4 == 3 and n > 11:
                    chunk_end_2(n // 4 - 1)
                inner(n)

            def merge_end(kind, turn, half):
                q = turn.times(8).plus(qY2 + 4 * half + kind)
                low_copy(q, 2 * (kind % 2), turn.times(24).plus(Y2 + 12 * half + (3, 7, 9, 11)[kind]))
                j = turn.times(2).plus(half)
                if kind < 2:
                    combined(q)
                    nc.scalar.activation(gate_pair[:, kind, :, :], gate_pair[:, kind, :, :], ACT.Tanh, scale=0.5
                                         ).then_inc(merge_tanh, 1)
                elif kind == 3:
                    act.wait_ge(merge_summed, j.value(1))
                    nc.scalar.activation(merged[:, at2(j.times(2).value()), 0:T], scaled[:, 0, :, :],
                                         ACT.Copy, scale=0.5).then_inc(merge_hi, 1)

            def merge_chunks(i, before, inner=lambda n: None):
                for half in range(2):
                    for p in range(12):
                        split(Step(Y2 + 12 * half + p, i, 24))
                        if p == 3:
                            if half:
                                merge_end(3, Step(0, i, 1), 0)
                            else:
                                before()
                        elif p in (7, 9, 11):
                            merge_end((p - 7) // 2, Step(0, i, 1), half)
                        inner(12 * half + p)

            merge_chunks(None, lambda: chunk_end_2(27), inner=lambda n: inner(112 + n))
            with act.Fori(1, 4) as i:
                merge_chunks(i, lambda: merge_end(3, Step(-1, i, 1), 1))
            out_product(O2, qO2, 8, N_POST2, y_2, before=lambda p: merge_end(3, Step(3), 1) if p == 3 else None,
                        flip=1)
            last_chunk(O2, qO2, 8, N_POST2, y_2, M2, flip=1)
            post_and_pre(N_POST2, N_PREF2, "norm_ffn_pre_2", M2)

            def relu_end(g, c, p):
                n, q = M2 + 64 * g + 8 * c, qM2 + 16 * g + 2 * c
                if p in (4, 5):
                    r = p - 4
                    act.wait_ge(units_ready, 22 + 8 * g + 2 * c + r + 1)
                    nc.scalar.activation(act_split[:, 4 * c + 2 * r:4 * c + 2 * r + 2, 0:T],
                                         gate_conv[:, 2 * r:2 * r + 2, :], ACT.Copy).then_inc(unit_hi, 1)
                if p in (3, 4):
                    low_copy(Step(q + p - 3), 4 * (c % 2) + 2 * (p - 3), Step(n + 7))

            for g in range(4):
                for c in range(4):
                    for p in range(8):
                        if g or c or p > 7:
                            split(Step(M2 + 64 * g + 8 * c + p))
                        if (g, c, p) == (0, 1, 1):
                            take_root(N_PREF2, D)
                        if c:
                            relu_end(g, c - 1, p)
                        elif g and p in (3, 4):
                            wide_end(Step(qM2 + 16 * g - 2), 4, Step(M2 + 64 * g - 1), p - 3)
                out_product(M2 + 64 * g + 32, qM2 + 16 * g + 8, 8, N_POSTF2 if g == 3 else None, y,
                            before=lambda p: relu_end(g, 3, p))
            last_chunk(M2 + 64 * 3 + 32, qM2 + 16 * 3 + 8, 8, N_POSTF2, y)
            take_root(N_POSTF2, D)

        @block.gpsimd
        def _(pool):
            nc.gpsimd.memset(glu[:, :, 0:30], 0.0).then_inc(cleared, 1)
            nc.gpsimd.memset(cv[:, :, 0:2], 0.0).then_inc(cleared, 1)
            nc.gpsimd.memset(pool_in[:, :, 0:16], 0.0).then_inc(cleared, 1)

            def sum_squares(norm):
                at_least(pool, stat_summed, SUMMED_BEFORE[norm])
                for q in range(7):
                    s = 8 * SUMMED[norm] + q
                    pool.wait_ge(squares_ready, s + 1)
                    at_least(pool, squares_added, 7 * SUMMED[norm] + q)
                    if q == 0:
                        ins = nc.gpsimd.tensor_copy(square_sum[:, :, :], squares[:, s % 2, :, :])
                    else:
                        ins = nc.gpsimd.tensor_tensor(square_sum[:, :, :], square_sum[:, :, :],
                                                      squares[:, s % 2, :, :], ALU.add)
                    ins.then_inc(squares_added, 1)

            def long_convolution():
                for k in range(1, 31):
                    pool.wait_ge(tap_ready, 2 * k + 2)
                    at_least(pool, taps_added, k - 1)
                    nc.gpsimd.tensor_tensor(conv_b[:, 4:6, :], conv_b[:, 4:6, :], gate_pair[:, k % 2, :, :], ALU.add
                                            ).then_inc(taps_added, 1)

            for norm in SUMMED:
                sum_squares(norm)
                if norm == N_PRE1:
                    long_convolution()
                elif norm == N_POST1:
                    nc.gpsimd.memset(up_in[:, :, 0:2], 0.0).then_inc(cleared, 1)
                elif norm == N_PRE2:
                    nc.gpsimd.memset(qk_in[:, :, 0:3], 0.0).then_inc(cleared, 1)

        @block.vector
        def _(dve):
            class Taken:

                def __init__(self):
                    self.count = Step(0)

                def one(self):
                    self.count = self.count.plus(1)
                    return 1

                def all(self, but=0):
                    return self.count.value(-but)

                def enter(self, i, start, rate):
                    self.outside, self.rate, self.start = self.count, rate, start
                    self.count = self.inside = self.count.plus(-start * rate).along(i, rate)

                def leave(self, end):
                    assert self.count.base - self.inside.base == self.rate, self.count.base - self.inside.base
                    self.count = self.outside.plus((end - self.start) * self.rate)

            steps = Taken()

            def tt(out, a, b, op):
                return nc.vector.tensor_tensor(out, a, b, op)

            def stt(out, a, scalar, b, op0, op1):
                return nc.vector.scalar_tensor_tensor(out=out, in0=a, scalar=scalar, in1=b, op0=op0, op1=op1)

            def split(n):
                block_n = Step(n.base // 2, terms=tuple((i, r // 2) for i, r in n.terms))
                slot, half = block_n.slot(RAW_SLOTS), 1024 * (n.base % 2)
                dve.wait_ge(hi_ready, n.value(1))
                tt(w_lo[:, n.slot(SPLIT_SLOTS), :], raw[:, slot, half:half + 1024],
                   w_hi[:, n.slot(SPLIT_SLOTS), :].bitcast(f32), ALU.subtract).then_inc(lo_ready, 1)

            def combine(q, bank, out, tiles=2, by=None):
                dve.wait_ge(low_ready, q.value(1))
                ins = tt(out, ps[:, bank:bank + tiles, 0:T], low[:, q.slot(2), 0:tiles, :], ALU.add)
                if by is not None:
                    ins.then_inc(vector_step, steps.one())
                    dve.wait_ge(vector_step, steps.all())
                    ins = tt(out, out, bcast(by[:, :], tiles), ALU.mult)
                ins.then_inc(pair_combined, 1)

            def combined(q):
                dve.wait_ge(pair_combined, q.value(PAIR_CREDIT + 1))

            def low_half(out, value, scale, high):
                return stt(out, value, scale, high.bitcast(f32), ALU.mult, ALU.subtract)

            def make_scale(norm, out=scale):
                dve.wait_ge(root_ready, norm + 1)
                nc.vector.reciprocal(out[:, :], root[:, :]).then_inc(scale_ready, 1)
                dve.wait_ge(scale_ready, norm + 1)

            def post_pair(norm, y, gain, q):
                if q >= 2:
                    dve.wait_ge(x_ready, 8 * POST[norm] + q - 1)
                tt(scaled[:, q % 2, :, :], y[:, 2 * q:2 * q + 2, :], bcast(scale[:, :]), ALU.mult
                   ).then_inc(vector_step, steps.one())
                dve.wait_ge(vector_step, steps.all())
                for t in range(2):
                    k = 2 * q + t
                    last = stt(x[:, k, :], scaled[:, q % 2, t, :], P(gain, k), x[:, k, :], ALU.mult, ALU.add)
                last.then_inc(x_ready, 1)

            def pre_pair(norm, gain, q):
                dve.wait_ge(norm_hi, 2 * (8 * PRE[norm] + q + 1))
                for k in range(2 * q, 2 * q + 2):
                    last = low_half(h_split[:, k, T:2 * T], x[:, k, :], P(gain, k), h_split[:, k, 0:T])
                last.then_inc(h_ready, 1)

            dve.sem_inc(lo_ready, LO_CREDIT)
            dve.sem_inc(pair_combined, PAIR_CREDIT)
            dve.wait_ge(gains_loaded, 16)
            split(Step(W1))
            for q in range(8):
                if q % 2 == 0:
                    dve.wait_ge(x_loaded[q // 2], 16)
                pre_pair(N_PRE1, "norm_mix_pre", q)
                if q % 2:
                    split(Step(W1 + q // 2 + 1))
            dve.wait_ge(small_loaded, 32)

            def tap_b(j, k):
                if k == 0:
                    dve.wait_ge(glu_ready, j + 1)
                    dve.wait_ge(cleared, 3)
                for t in range(2 * j, 2 * j + 2):
                    weight = P("conv_b_w", 6 * k + t)
                    window = glu[:, t, k:k + T]
                    if k == 0:
                        ins = nc.vector.tensor_scalar(conv_b[:, t, :], window, weight, None, ALU.mult)
                    else:
                        dve.wait_ge(vector_step, steps.all(but=1))
                        ins = stt(conv_b[:, t, :], window, weight, conv_b[:, t, :], ALU.mult, ALU.add)
                    if (k, t) == (30, 2 * j + 1):
                        ins.then_inc(taps_done, 1)
                    else:
                        ins.then_inc(vector_step, steps.one())

            def chunk_end_1(c):
                kind, j = CHUNKS1[c]
                q, bank = Step(qW1 + c), 2 * (c % 2)
                if kind == "val":
                    combine(q, bank, val_b[:, :, :], by=pre_scale)
                elif kind == "gate":
                    combine(q, bank, tanh_b[:, :, :], by=pre_scale)
                    dve.wait_ge(tanh_ready, j + 1)
                    stt(glu[:, 2 * j:2 * j + 2, 30:30 + T], tanh_b[:, :, :], 1.0, val_b[:, :, :], ALU.add, ALU.mult
                        ).then_inc(glu_ready, 1)
                elif kind == "b":
                    combine(q, bank, b_gate[:, :, :], by=pre_scale)
                elif kind == "c":
                    combine(q, bank, c_gate[:, :, :], by=pre_scale)
                elif kind == "v":
                    combine(q, bank, conv_a[:, :, :], by=pre_scale)
                    combined(q)
                    tt(cv[:, :, 2:2 + T], c_gate[:, :, :], conv_a[:, :, :], ALU.mult).then_inc(cv_ready, 1)
                    for k in (1, 0):
                        for t in range(2):
                            dve.wait_ge(conv_a_started, 2 * j + t + 1)
                            if k == 0:
                                dve.wait_ge(vector_step, steps.all(but=1))
                            stt(conv_a[:, t, :], cv[:, t, k:k + T], P("conv_a_w", 6 * k + 2 * j + t),
                                             conv_a[:, t, :], ALU.mult, ALU.add).then_inc(vector_step, steps.one())
                    dve.wait_ge(vector_step, steps.all())
                    tt(conv_a[:, :, :], conv_a[:, :, :], b_gate[:, :, :], ALU.mult).then_inc(a_mixed, 1)
                    dve.wait_ge(a_hi, j + 1)
                    tt(act_split[:, 2 * j:2 * j + 2, T:2 * T], conv_a[:, :, :],
                       act_split[:, 2 * j:2 * j + 2, 0:T].bitcast(f32), ALU.subtract).then_inc(a_split, 1)
                else:
                    dve.wait_ge(vector_step, steps.all())
                    combine(q, bank, pool_in[:, :, 16:16 + T], by=pre_scale)
                    combined(q)
                    at_least(dve, pool_summed, j)
                    for t in range(2):
                        g = 2 * j + t
                        source = pool_in[:, t, :]
                        for s in range(g + 1):
                            w, out = 1 << s, pool_sum[:, s % 2, :]
                            dve.wait_ge(vector_step, steps.all())
                            tt(out[:, 2 * w - 1:16 + T], source[:, 2 * w - 1:16 + T],
                                            source[:, w - 1:16 + T - w], ALU.add).then_inc(vector_step, steps.one())
                            source = out
                        dve.wait_ge(vector_step, steps.all())
                        w = 2 << g
                        tt(pooled[:, t, 0:16], source[:, 16:32], K("pool_first", 16 * g, 16), ALU.mult
                           ).then_inc(vector_step, steps.one())
                        stt(pooled[:, t, 16:T], source[:, 32:16 + T], 1 / w, pool_in[:, t, 32:16 + T],
                                         ALU.mult, ALU.subtract).then_inc(vector_step, steps.one())
                        dve.wait_ge(vector_step, steps.all(but=1))
                        last = tt(pooled[:, t, 0:16], pooled[:, t, 0:16], pool_in[:, t, 16:32], ALU.subtract)
                        if t:
                            last.then_inc(pooled_ready, 1)
                        else:
                            last.then_inc(vector_step, steps.one())

            def layer_norm(n):
                if n == 62:
                    dve.wait_ge(mean_summed, 1)
                    for j in range(3):
                        pair = conv_b[:, 2 * j:2 * j + 2, :]
                        stt(pair, bcast(ps[:, 7, 0:T]), -1 / 768, pair, ALU.mult, ALU.add).then_inc(centered, 1)
                elif n == 67:
                    make_scale(N_LN)
                    for j in range(3):
                        dve.wait_ge(ln_squared, j + 1)
                        pair = conv_b[:, 2 * j:2 * j + 2, :]
                        tt(pair, pair, bcast(scale[:, :]), ALU.mult).then_inc(ln_scaled, 1)
                elif n == O1 + 1:
                    for j in range(3):
                        dve.wait_ge(ln_tanh, j + 1)
                        pair = conv_b[:, 2 * j:2 * j + 2, :]
                        stt(pair, ln_squares[:, 2 * j:2 * j + 2, :], 1.0, pair, ALU.add, ALU.mult
                            ).then_inc(ln_silu, 1)
                    for j in range(3):
                        dve.wait_ge(b_hi, j + 1)
                        low_half(act_split[:, 6 + 2 * j:8 + 2 * j, T:2 * T], conv_b[:, 2 * j:2 * j + 2, :], 0.5,
                                 act_split[:, 6 + 2 * j:8 + 2 * j, 0:T]).then_inc(b_split, 1)

            def pool_end(j):
                dve.wait_ge(c_hi, 2 * j + 2)
                for t in range(2):
                    k = 2 * j + t
                    last = low_half(act_split[:, 12 + k, T:2 * T], ps[:, 2 + j, T * t:T * t + T], P("pool_scale", k),
                                    act_split[:, 12 + k, 0:T])
                last.then_inc(c_split, 1)

            for c in range(17):
                for p in range(4):
                    n = 4 * c + p
                    if n > 4:
                        split(Step(W1 + n))
                    if n == 9:
                        make_scale(N_PRE1, pre_scale)
                        chunk_end_1(0)
                    elif p == 3 and c > 1:
                        chunk_end_1(c - 1)
                    if 12 <= n < 60:
                        for m in range(62 * (n - 12) // 48, 62 * (n - 11) // 48):
                            tap_b(m // 31, m % 31)
                    layer_norm(n)

            def y_pair(g, q, bank, y, n):
                if g == 0:
                    combine(q, bank, y[:, 2 * n:2 * n + 2, :])
                    return
                combine(q, bank, scaled[:, n % 2, :, :])
                combined(q)
                tt(y[:, 2 * n:2 * n + 2, :], y[:, 2 * n:2 * n + 2, :], scaled[:, n % 2, :, :], ALU.add
                   ).then_inc(y_summed, 1)

            def out_product(n0, q0, pieces, g, y, before, between=lambda n: None, flip=0):
                for c in range(4):
                    for p in range(pieces):
                        split(Step(n0 + pieces * c + p))
                        between(n0 + pieces * c + p)
                        before(pieces * c + p)
                        if p in (3, 4) and c:
                            r = p - 3
                            y_pair(g, Step(q0 + 2 * c - 2 + r), 4 * ((c - 1 + flip) % 2) + 2 * r, y, 2 * c - 2 + r)

            def last_chunk(q0, g, y, next_piece=None, flip=0):
                if next_piece is not None:
                    for p in range(3):
                        split(Step(next_piece + p))
                for r in range(2):
                    y_pair(g, Step(q0 + 6 + r), 4 * (1 - flip) + 2 * r, y, 6 + r)

            def post_and_pre(post, y, post_gain, pre, pre_gain, next_piece):
                split(Step(next_piece + 3))
                make_scale(post)
                for q in range(8):
                    post_pair(post, y, post_gain, q)
                    if q:
                        pre_pair(pre, pre_gain, q - 1)
                    if 3 <= q < 7:
                        split(Step(next_piece + q + 1))
                pre_pair(pre, pre_gain, 7)

            def first_pools(n):
                layer_norm(n)
                if n == O1 + 4:
                    pool_end(0)
                elif n == O1 + 6:
                    pool_end(1)

            out_product(O1, qO1, 8, 0, y, before=lambda p: chunk_end_1(16) if p == 3 else None,
                        between=first_pools, flip=1)
            last_chunk(qO1, 0, y, M1, flip=1)
            post_and_pre(N_POST1, y, "norm_mix_post", N_PREF1, "norm_ffn_pre", M1)

            def taps_ffn(chunk, r, half, out, last_signal):
                for k in (1, 0):
                    for t in range(2 * r, 2 * r + 2):
                        weight = P("conv_ffn_w", chunk.times(4).value(88 * k + 44 * half + t))
                        if k:
                            dve.wait_ge(conv_started, chunk.times(8).value(4 * half + t + 1))
                        else:
                            dve.wait_ge(vector_step, steps.all(but=1))
                        ins = stt(out[:, t, :], up_in[:, t, k:k + T], weight, out[:, t, :], ALU.mult, ALU.add)
                        if last_signal is not None and (k, t) == (0, 2 * r + 1):
                            ins.then_inc(last_signal, 1)
                        else:
                            ins.then_inc(vector_step, steps.one())

            def gate_end(q0, chunk, p):
                if p in (3, 4):
                    r = p - 3
                    combine(q0.plus(r), 2 * r, up_in[:, 2 * r:2 * r + 2, 2:2 + T], by=pre_scale)
                if p in (5, 6):
                    taps_ffn(chunk, p - 5, 0, gate_conv, conv_done)

            def at2(k):
                return slice(k, k + 2) if isinstance(k, int) else bass.ds(k, 2)

            def split_hidden(u, r, k, scale):
                dve.wait_ge(unit_hi, u + 1)
                low_half(act_split[:, at2(k), T:2 * T], gate_conv[:, 2 * r:2 * r + 2, :], scale,
                         act_split[:, at2(k), 0:T]).then_inc(unit_split, 1)

            def val_end(q0, chunk, first, p):
                if p in (3, 4):
                    r = p - 3
                    combine(q0.plus(2 + r), 4 + 2 * r, up_in[:, 2 * r:2 * r + 2, 2:2 + T], by=pre_scale)
                if p in (5, 6):
                    r = p - 5
                    taps_ffn(chunk, r, 1, val_conv, None)
                    dve.wait_ge(gate_ready, chunk.times(2).value(r + 1))
                    pair = slice(2 * r, 2 * r + 2)
                    stt(gate_conv[:, pair, :], gate_tanh[:, pair, :], 1.0, gate_conv[:, pair, :], ALU.add, ALU.mult
                        ).then_inc(vector_step, steps.one())
                    dve.wait_ge(vector_step, steps.all())
                    tt(gate_conv[:, pair, :], gate_conv[:, pair, :], val_conv[:, pair, :], ALU.mult
                       ).then_inc(units_ready, 1)
                if p in (7, 8):
                    r = p - 7
                    split_hidden(chunk.times(2).value(r), r, chunk.times(4).value(2 * r - 4 * first), 0.5)

            def up_chunks(g, first, i, before, skip=0):
                q0 = Step(qup1[g], i, 4)
                chunk = Step(first, i, 1)
                for p in range(16):
                    if p >= skip:
                        split(Step(up1[g] + p, i, 16))
                    if skip and p == 9:
                        make_scale(N_PREF1, pre_scale)
                    before(p)
                    gate_end(q0, chunk, p - 8)

            def down_end(g):
                def before(p):
                    if p in (3, 4):
                        y_pair(g, Step(qdown1[g] + 6 + p - 3), 4 + 2 * (p - 3), y, 6 + p - 3)
                return before

            dve.wait_ge(cleared, 4)
            first = 0
            for g, n in enumerate(GROUPS1):
                if g == 0:
                    up_chunks(0, 0, None, lambda p: None, skip=8)
                else:
                    up_chunks(g, first, None, down_end(g - 1))
                with dve.Fori(1, n) as i:
                    steps.enter(i, 1, 20)
                    up_chunks(g, first, i, lambda p: val_end(
                        Step(qup1[g] - 4, i, 4), Step(first - 1, i, 1), first, p))
                    steps.leave(n)
                out_product(down1[g], qdown1[g], 2 * n, g, y, before=lambda p: val_end(
                    Step(qup1[g] + 4 * (n - 1)), Step(first + n - 1), first, p))
                first += n
            last_chunk(qdown1[-1], 2, y, W2)
            post_and_pre(N_POSTF1, y, "norm_ffn_post", N_PRE2, "norm_mix_pre_2", W2)

            def gate_rows():
                combine(Step(qG2), 4, scaled[:, 0, 0:1, :], tiles=1, by=pre_scale)
                combined(Step(qG2))
                nc.vector.tensor_scalar(row_i[0:4, :], scaled[0:4, 0, 0, :], P("gate_bias", 0)[0:4, :], None, ALU.add
                                        ).then_inc(vector_step, steps.one())
                nc.vector.tensor_scalar(row_f[0:4, :], scaled[64:68, 0, 0, :], P("gate_bias", 1)[64:68, :], None,
                                        ALU.add).then_inc(rows_split, 1)
                dve.wait_ge(rows_split, 1)
                nc.vector.tensor_scalar(row_m[0:4, :], row_f[0:4, :], 0.0, None, ALU.min
                                        ).then_inc(vector_step, steps.one())
                dve.wait_ge(row_step, 3)
                dve.wait_ge(vector_step, steps.all())
                tt(row_m[0:4, :], row_m[0:4, :], row_g[0:4, :], ALU.subtract).then_inc(vector_step, steps.one())
                dve.wait_ge(vector_step, steps.all())
                one = ones[0:4, 0:1].to_broadcast([4, T])
                nc.vector.tensor_tensor_scan(row_n[0:4, :], one, row_m[0:4, :], 0.0, ALU.mult, ALU.add
                                             ).then_inc(vector_step, steps.one())
                dve.wait_ge(vector_step, steps.all())
                tt(row_g[0:4, :], row_i[0:4, :], row_n[0:4, :], ALU.subtract).then_inc(vector_step, steps.one())
                dve.wait_ge(vector_step, steps.all())
                nc.vector.tensor_tensor_scan(row_m[0:4, :], one, row_g[0:4, :], 0.0, ALU.mult, ALU.max
                                             ).then_inc(vector_step, steps.one())
                dve.wait_ge(vector_step, steps.all())
                stt(row_n[0:4, :], row_n[0:4, :], -1.0, row_m[0:4, :], ALU.mult, ALU.subtract
                    ).then_inc(rows_ready, 1)

            def angles():
                turns, angle = scaled[:, 1, 0, :], cos[:, :]
                dve.wait_ge(pos_loaded, 16)
                nc.vector.tensor_copy(angle, pos_i[:, :]).then_inc(vector_step, steps.one())
                dve.wait_ge(vector_step, steps.all())
                nc.vector.tensor_scalar(angle, angle, K("inv_freq"), None, ALU.mult).then_inc(vector_step, steps.one())
                dve.wait_ge(vector_step, steps.all())
                nc.vector.tensor_scalar(turns, angle, 1 / (2 * math.pi), ROUND, ALU.mult, ALU.add
                                        ).then_inc(vector_step, steps.one())
                dve.wait_ge(vector_step, steps.all())
                nc.vector.tensor_scalar(turns, turns, ROUND, None, ALU.subtract).then_inc(vector_step, steps.one())
                for part in TURN_PARTS:
                    dve.wait_ge(vector_step, steps.all())
                    stt(angle, turns, -part, angle, ALU.mult, ALU.add).then_inc(vector_step, steps.one())
                dve.wait_ge(vector_step, steps.all())
                nc.vector.tensor_scalar(angle, angle, PI_BELOW, -PI_BELOW, ALU.min, ALU.max).then_inc(angle_ready, 1)

            def columns():
                dve.wait_ge(columns_summed, 1)
                nc.vector.tensor_copy(gcol[:, :, :].rearrange("p a t -> p (a t)"), ps[:, 6, 0:8]
                                      ).then_inc(columns_ready, 1)

            def chunk_end_2(c):
                kind, h = CHUNKS2[c]
                q, bank = Step(pair2(c)), 2 * (c % 2)
                if kind in ("q", "k"):
                    is_k = int(kind == "k")
                    out = (q_m, k_m)[is_k]
                    combine(q, bank, qk_in[:, :, 3:3 + T], by=pre_scale)
                    for k in (2, 1, 0):
                        for t in range(2):
                            if k == 2:
                                dve.wait_ge(qk_started, 4 * h + 2 * is_k + t + 1)
                            else:
                                dve.wait_ge(vector_step, steps.all(but=1))
                            ins = stt(out[:, t, :], qk_in[:, t, k:k + T], P("conv_w_2", 16 * k + 8 * is_k + 2 * h + t),
                                      out[:, t, :], ALU.mult, ALU.add)
                            if (k, t) == (0, 1):
                                ins.then_inc(qk_convolved, 1)
                            else:
                                ins.then_inc(vector_step, steps.one())
                    dve.wait_ge(qk_tanh, 2 * h + is_k + 1)
                    stt(out[:, :, :], squares[:, is_k, :, :], 1.0, out[:, :, :], ALU.add, ALU.mult
                        ).then_inc(qk_ready, 1)
                elif kind == "v":
                    at_least(dve, m_scored, h)
                    combine(q, bank, v_m[:, :, :], by=pre_scale)
                elif kind == "o":
                    combine(q, bank, o_m[:, :, :], by=pre_scale)
                elif kind == "av":
                    at_least(dve, a_scored, 2 * h)
                    combine(q, bank, a_v[:, :, :], by=pre_scale)
                else:
                    is_k = int(kind == "ak")
                    at_least(dve, a_scored, 2 * h)
                    a = (a_q, a_k)[is_k]
                    combine(q, bank, a[:, :, :], by=pre_scale)
                    combined(q)
                    dve.wait_ge(table_step, 3)
                    at_least(dve, rope_ready, 2 * h + is_k)
                    for lo_, hi_ in ((0, 64), (64, 0)):
                        for t in range(2):
                            tt(scaled[lo_:lo_ + 64, 0, t, :], a[hi_:hi_ + 64, t, :],
                                            sin[hi_:hi_ + 64, :], ALU.mult).then_inc(vector_step, steps.one())
                    dve.wait_ge(vector_step, steps.all())
                    tt(a[:, :, :], a[:, :, :], bcast(cos[:, :]), ALU.mult).then_inc(vector_step, steps.one())
                    dve.wait_ge(vector_step, steps.all())
                    tt(a[:, :, :], a[:, :, :], scaled[:, 0, :, :], ALU.add).then_inc(rope_ready, 1)

            def mlstm(h, stage):
                if stage == 0:
                    dve.wait_ge(rows_bcast, h + 1)
                    for s, cols, queries in ((0, slice(0, 256), slice(0, 256)), (1, slice(256, 384), slice(128, 256))):
                        last = nc.vector.tensor_scalar(decay[:, cols], ps[:, 7, queries], gcol[:, s, h:h + 1], 0.0,
                                                       ALU.subtract, ALU.max)
                    last.then_inc(decay_started, 1)
                    dve.wait_ge(decay_ready, h + 1)
                    for cols in (slice(0, 128), slice(256, 384)):
                        tt(decay[:, cols], decay[:, cols], K("keep", 0, 128), ALU.mult
                           ).then_inc(vector_step, steps.one())
                    dve.wait_ge(vector_step, steps.all())
                    dve.wait_ge(m_scored, h + 1)
                    at_least(dve, m_valued, h)
                    stt(s_ts[:, :], ps[:, 4, 0:384], 1 / 64, decay[:, :], ALU.mult, ALU.mult).then_inc(s_ts_ready, 1)
                elif stage == 1:
                    dve.wait_ge(den_ready, 2 * h + 2)
                    tt(den_m[:, 0, :], den_m[:, 0, :], den_m[:, 1, :], ALU.max).then_inc(vector_step, steps.one())
                    dve.wait_ge(vector_step, steps.all())
                    nc.vector.reciprocal(den_m[:, 0, :], den_m[:, 0, :]).then_inc(vector_step, steps.one())
                    dve.wait_ge(vector_step, steps.all())
                    tt(h_m[:, :, :], ps[:, 5, :].rearrange("p (a t) -> p a t", a=2), bcast(den_m[:, 0, :]), ALU.mult
                       ).then_inc(m_divided, 1)
                elif stage == 2:
                    make_scale(N_HEAD + h)
                else:
                    dve.wait_ge(m_squared, h + 1)
                    tt(h_m[:, :, :], h_m[:, :, :], bcast(scale[:, :]), ALU.mult).then_inc(vector_step, steps.one())
                    dve.wait_ge(o_ready, h + 1)
                    dve.wait_ge(vector_step, steps.all())
                    stt(h_m[:, :, :], o_m[:, :, :], 1.0, h_m[:, :, :], ALU.add, ALU.mult).then_inc(m_gated, 1)
                    dve.wait_ge(m_hi, 2 * h + 2)
                    for t in range(2):
                        last = low_half(act_split[:, 2 * h + t, T:2 * T], h_m[:, t, :], P("mlstm_norm_2", 2 * h + t),
                                        act_split[:, 2 * h + t, 0:T])
                    last.then_inc(m_split, 1)

            def attention(t, stage):
                if stage == 0:
                    scale = 128 ** -0.5
                    dve.wait_ge(a_scored, t + 1)
                    at_least(dve, prob_turned, t)
                    for cols in (slice(0, 128), slice(256, 384)):
                        stt(decay[:, cols], ps[:, 4, cols], scale, K("masked", 0, 128), ALU.mult, ALU.add
                            ).then_inc(vector_step, steps.one())
                    nc.vector.tensor_scalar(decay[:, 128:256], ps[:, 4, 128:256], scale, None, ALU.mult
                                            ).then_inc(vector_step, steps.one())
                    dve.wait_ge(vector_step, steps.all())
                    for half, cols in enumerate((slice(0, 128), slice(128, 384))):
                        nc.vector.reduce_max(a_stat[:, half:half + 1], decay[:, cols], AX.X
                                             ).then_inc(vector_step, steps.one())
                    dve.wait_ge(vector_step, steps.all())
                    nc.vector.tensor_scalar(a_stat[:, 2:4], a_stat[:, 0:2], -1.0, None, ALU.mult
                                            ).then_inc(a_max_ready, 1)
                    dve.wait_ge(a_exp_ready, 2 * t + 2)
                    nc.vector.reciprocal(a_stat[:, 6:8], a_stat[:, 4:6]).then_inc(vector_step, steps.one())
                    dve.wait_ge(vector_step, steps.all())
                    for half, cols in enumerate((slice(0, 128), slice(128, 384))):
                        last = nc.vector.tensor_scalar(s_ts[:, cols], decay[:, cols], a_stat[:, 6 + half:7 + half],
                                                       None, ALU.mult)
                    last.then_inc(prob_ready, 1)
                elif stage == 2:
                    dve.wait_ge(a_hi_2, t + 1)
                    tt(act_split[:, 8 + t, T:2 * T], ps[:, 7, 0:T], act_split[:, 8 + t, 0:T].bitcast(f32),
                       ALU.subtract).then_inc(a_split_2, 1)

            def inner(n):
                if n == 11:
                    gate_rows()
                elif n == 13:
                    angles()
                elif n == GATE_COLUMNS_END:
                    columns()
                for h in range(4):
                    r = n - 16 * (h + 1)
                    if r in M_STAGE_END:
                        mlstm(h, M_STAGE_END.index(r))
                for j in range(4):
                    r = n - (64 + 12 * (j + 1))
                    for a in range(2):
                        if r in A_STAGE_END[a]:
                            attention(2 * j + a, A_STAGE_END[a].index(r))

            dve.wait_ge(cleared, 5)
            for n in range(7, 4 * 28):
                if n > 7:
                    split(Step(piece2(n)))
                else:
                    for p in range(2):
                        split(Step(G2 + p))
                    make_scale(N_PRE2, pre_scale)
                    chunk_end_2(0)
                if n == 9:
                    chunk_end_2(1)
                elif n % 4 == 3 and n > 11:
                    chunk_end_2(n // 4 - 1)
                inner(n)

            def merge_end(kind, turn, half):
                q = turn.times(8).plus(qY2 + 4 * half + kind)
                bank = 2 * (kind % 2)
                if kind < 2:
                    combine(q, bank, gate_pair[:, kind, :, :], by=pre_scale)
                    return
                out = scaled[:, kind - 2, :, :]
                combine(q, bank, out)
                combined(q)
                dve.wait_ge(merge_tanh, turn.times(4).value(2 * half + 2))
                stt(out, gate_pair[:, kind - 2, :, :], 1.0, out, ALU.add, ALU.mult).then_inc(vector_step, steps.one())
                if kind == 3:
                    j = turn.times(2).plus(half)
                    k = j.times(2).value()
                    dve.wait_ge(vector_step, steps.all())
                    tt(scaled[:, 0, :, :], scaled[:, 0, :, :], out, ALU.add).then_inc(merge_summed, 1)
                    dve.wait_ge(merge_hi, j.value(1))
                    low_half(merged[:, at2(k), T:2 * T], scaled[:, 0, :, :], 0.5, merged[:, at2(k), 0:T]
                             ).then_inc(merge_split, 1)

            def merge_chunks(i, before, inner=lambda n: None):
                turn = Step(0, i, 1)
                for half in range(2):
                    for p in range(12):
                        split(Step(Y2 + 12 * half + p, i, 24))
                        if p == 3:
                            if half:
                                merge_end(3, turn, 0)
                            else:
                                before()
                        elif p in (7, 9, 11):
                            merge_end((p - 7) // 2, turn, half)
                        inner(12 * half + p)

            merge_chunks(None, lambda: chunk_end_2(27), inner=lambda n: inner(112 + n))
            with dve.Fori(1, 4) as i:
                steps.enter(i, 1, 8)
                merge_chunks(i, lambda: merge_end(3, Step(-1, i, 1), 1))
                steps.leave(4)
            out_product(O2, qO2, 8, 0, y_2, before=lambda p: merge_end(3, Step(3), 1) if p == 3 else None, flip=1)
            last_chunk(qO2, 0, y_2, M2, flip=1)
            post_and_pre(N_POST2, y_2, "norm_mix_post_2", N_PREF2, "norm_ffn_pre_2", M2)

            def relu_end(g, c, p):
                if p in (4, 5):
                    split_hidden(22 + 8 * g + 2 * c + p - 4, p - 4, 4 * c + 2 * (p - 4), 1.0)
                if p in (3, 4):
                    r = p - 3
                    combine(Step(qM2 + 16 * g + 2 * c + r), 4 * (c % 2) + 2 * r, squares[:, r, :, :], by=pre_scale)
                    combined(Step(qM2 + 16 * g + 2 * c + r))
                    stt(gate_conv[:, 2 * r:2 * r + 2, :], squares[:, r, :, :], 0.0, squares[:, r, :, :],
                        ALU.max, ALU.mult).then_inc(units_ready, 1)

            for g in range(4):
                for c in range(4):
                    for p in range(8):
                        if g or c or p > 7:
                            split(Step(M2 + 64 * g + 8 * c + p))
                        if (g, c, p) == (0, 1, 1):
                            make_scale(N_PREF2, pre_scale)
                        if c:
                            relu_end(g, c - 1, p)
                        elif g and p in (3, 4):
                            y_pair(g - 1, Step(qM2 + 16 * g - 2 + p - 3), 4 + 2 * (p - 3), y, 6 + p - 3)
                out_product(M2 + 64 * g + 32, qM2 + 16 * g + 8, 8, g, y, before=lambda p: relu_end(g, 3, p))
            last_chunk(qM2 + 16 * 3 + 8, 3, y)
            make_scale(N_POSTF2)
            for q in range(8):
                post_pair(N_POSTF2, y, "norm_ffn_post_2", q)


_WEIGHTS = ["w_in", "w_out", "w_up", "w_down", "w_in_2", "w_branch_m_2", "w_branch_a_2", "w_out_2",
            "w_up_2", "w_down_2"]


def pack_params(inputs):
    import numpy as np

    def columns(name):
        if name == "gate_bias":
            out = np.zeros((128, 2), np.float32)
            out[0:4, 0] = inputs["i_bias_2"][0]
            out[64:68, 1] = inputs["f_bias_2"][0]
            return out
        a = np.asarray(inputs[name][0])
        if name == "pool_w":
            return a.transpose(1, 0, 2).reshape(128, -1)
        return a.reshape(-1, 128).T

    return np.ascontiguousarray(np.concatenate([columns(name) for name, _ in PARAM_COLUMNS], 1), np.float32)


def constants():
    import numpy as np

    p, one = np.arange(128), np.ones((128, 128), np.float32)
    select = np.zeros((128, 4, 128), np.float32)
    for h in range(4):
        select[h, h] = 1
    first = np.array([[1 / min(t + 1, w) for t in range(16)] for w in (2, 4, 8, 16)], np.float32).reshape(1, 64)
    column = {
        "identity": np.eye(128), "ones": one,
        "keep": np.triu(one),
        "masked": np.triu(one, 1) * np.float32(-1e38),
        "select": select.reshape(128, -1),
        "pool_first": np.repeat(first, 128, 0),
        "inv_freq": (np.float32(1) / np.float32(10000) ** ((2 * (p % 64)).astype(np.float32) / np.float32(128)))[:, None],
        "epsilon": np.repeat(np.array([[1e-6, 1e-5, 4e-6]]), 128, 0),
        "half_pi": np.full((128, 1), np.pi / 2), "sign": np.where(p < 64, 1, -1)[:, None],
    }
    return np.ascontiguousarray(np.concatenate([column[n] for n, _ in CONST_COLUMNS], 1), np.float32)


def kernel(**inputs):
    import concourse.bacc as bacc
    import numpy as np
    from concourse import mybir
    from concourse.bass_utils import run_bass_kernel_spmd

    nc = bacc.Bacc("TRN2", target_bir_lowering=False, num_devices=1)
    arrays = {
        "xT": np.ascontiguousarray(np.asarray(inputs["x"])[0].reshape(256, 16, 128).transpose(2, 1, 0)),
        "params": pack_params(inputs), "consts": constants(),
        "positions": np.ascontiguousarray(inputs["positions_2"]).astype(np.int32),
    }
    for name in _WEIGHTS:
        arrays[name] = np.ascontiguousarray(inputs[name][0])
    aps = [nc.dram_tensor(name, a.shape, mybir.dt.from_np(a.dtype), kind="ExternalInput").ap()
           for name, a in arrays.items()]
    out = nc.dram_tensor("outT", (128, 16, 256), mybir.dt.float32, kind="ExternalOutput").ap()
    build(nc, *aps, out)
    result = run_bass_kernel_spmd(nc, [arrays], core_ids=[0]).results[0]["outT"]
    return result.transpose(2, 1, 0).reshape(1, 256, 2048)
```

```python
def plan(shapes):
    off, at = {}, 0
    for name, n in shapes:
        off[name] = at
        at += n
    return off, at


PARAM_COLUMNS = [
    ("norm_mix_pre", 16), ("norm_mix_post", 16), ("norm_ffn_pre", 16), ("norm_ffn_post", 16),
    ("norm_mix_pre_2", 16), ("norm_mix_post_2", 16), ("norm_ffn_pre_2", 16), ("norm_ffn_post_2", 16),
    ("conv_a_w", 3 * 6), ("conv_b_w", 31 * 6), ("conv_b_bias", 6), ("ln_b_gain", 6), ("ln_b_bias", 6),
    ("pool_scale", 4), ("conv_ffn_w", 3 * 88), ("conv_ffn_bias", 88),
    ("conv_w_2", 4 * 16), ("conv_b_2", 16), ("mlstm_norm_2", 8), ("gate_bias", 2),
    ("pool_w", 4 * 128),
]
CONST_COLUMNS = [
    ("identity", 128), ("ones", 128), ("keep", 128), ("masked", 128), ("select", 4 * 128),
    ("pool_first", 4 * 16), ("inv_freq", 1), ("epsilon", 3), ("half_pi", 1), ("sign", 1),
]


def turn_parts():
    import math

    import numpy as np

    first = 6.28125
    second = math.floor((2 * math.pi - first) * 2.0 ** 20) / 2.0 ** 20
    return first, second, float(np.float32(2 * math.pi - first - second))


class Step:

    def __init__(self, base, i=None, rate=0, terms=()):
        self.base = base
        self.terms = tuple(terms) + (() if i is None else ((i, rate),))

    def plus(self, k):
        return Step(self.base + k, terms=self.terms)

    def times(self, k):
        return Step(self.base * k, terms=tuple((i, r * k) for i, r in self.terms))

    def along(self, i, rate):
        return Step(self.base, i, rate, self.terms)

    def value(self, k=0):
        out = self.base + k
        for i, rate in self.terms:
            out = i * rate + out
        return out

    def slot(self, slots):
        assert all(rate % slots == 0 for _, rate in self.terms)
        return self.base % slots

    def turn(self, slots):
        assert all(rate % slots == 0 for _, rate in self.terms)
        return Step(self.base // slots, terms=tuple((i, rate // slots) for i, rate in self.terms))


def build(nc, xT, params, consts, positions, w_in, w_out, w_up, w_down,
          w_in_2, w_branch_m_2, w_branch_a_2, w_out_2, w_up_2, w_down_2, outT):
    import math
    from contextlib import ExitStack

    import concourse.bass as bass
    from concourse import mybir

    f32, f32r, i32 = mybir.dt.float32, mybir.dt.float32r, mybir.dt.int32
    ALU, ACT, AX = mybir.AluOpType, mybir.ActivationFunctionType, mybir.AxisListType

    T = 256
    D = 2048
    KT = D // 128
    FF1, FF2 = 5632, 8192
    RAW_SLOTS, SPLIT_SLOTS = 4, 4
    PARAM, N_PARAM = plan(PARAM_COLUMNS)
    CONST, N_CONST = plan(CONST_COLUMNS)
    LO_CREDIT = 2 * RAW_SLOTS
    USED_CREDIT = SPLIT_SLOTS
    PAIR_CREDIT = 4

    ctx = ExitStack()
    with ctx:
        top = [(nc.sbuf_base + 31) // 32 * 32]

        def place(name, shape, dtype=f32, at=None):
            size = 4 * math.prod(shape[1:])
            if at is None:
                at = top[0]
                top[0] += (size + 31) // 32 * 32
            return nc.alloc_sbuf_tensor_at(name, shape, dtype, offset=at)

        cursor = [0]

        def put(name, shape):
            at = cursor[0]
            cursor[0] += (4 * math.prod(shape[1:]) + 31) // 32 * 32
            return place(name, shape, at=at)

        def region(size):
            at = top[0]
            top[0] += size
            return at


        raw = place("raw", [128, RAW_SLOTS, 2048])
        w_hi = place("w_hi", [128, SPLIT_SLOTS, 1024], f32r)
        w_lo = place("w_lo", [128, SPLIT_SLOTS, 1024], f32r)
        x = place("x", [128, KT, T])
        h_split = place("h_split", [128, KT, 2 * T], f32r)
        ACT_SPLIT = top[0]
        act_split = place("act_split", [128, KT, 2 * T], f32r)
        par = place("par", [128, N_PARAM])
        con = place("con", [128, N_CONST])
        low = place("low", [128, 2, 2, T])
        scaled = place("scaled", [128, 2, 2, T])
        squares = place("squares", [128, 2, 2, T])
        square_sum = place("square_sum", [128, 2, T])
        gate_pair = place("gate_pair", [128, 2, 2, T])
        root = place("root", [128, T])
        scale = place("scale", [128, T])
        pre_scale = place("pre_scale", [128, T])
        pos_i = place("pos_i", [128, T], i32)
        REGION = 32 * 1024 + 64
        C = region(REGION)
        assert top[0] <= nc.sbuf_top, (top[0], nc.sbuf_top)

        cursor[0] = C
        glu = put("glu", [128, 6, 30 + T])
        conv_b = put("conv_b", [128, 6, T])
        val_b = put("val_b", [128, 2, T])
        tanh_b = put("tanh_b", [128, 2, T])
        b_gate = put("b_gate", [128, 2, T])
        c_gate = put("c_gate", [128, 2, T])
        cv = put("cv", [128, 2, 2 + T])
        conv_a = put("conv_a", [128, 2, T])
        pool_in = put("pool_in", [128, 2, 16 + T])
        pool_sum = put("pool_sum", [128, 2, 16 + T])
        pooled = put("pooled", [128, 2, T])
        assert cursor[0] <= C + REGION, cursor[0] - C

        ln_squares = place("ln_squares", [128, 6, T], at=C)
        y = place("y", [128, KT, T], at=C)
        cursor[0] = C + KT * T * 4
        up_in = put("up_in", [128, 4, 2 + T])
        gate_conv = put("gate_conv", [128, 4, T])
        gate_tanh = put("gate_tanh", [128, 4, T])
        val_conv = put("val_conv", [128, 4, T])
        assert cursor[0] <= C + REGION, cursor[0] - C
        cursor[0] = C
        qk_in = put("qk_in", [128, 2, 3 + T])
        q_m = put("q_m", [128, 2, T])
        k_m = put("k_m", [128, 2, T])
        v_m = put("v_m", [128, 2, T])
        o_m = put("o_m", [128, 2, T])
        v_tok = put("v_tok", [128, 2, T])
        decay = put("decay", [128, 384])
        s_ts = put("s_ts", [128, 384])
        den_m = put("den_m", [128, 2, T])
        h_m = put("h_m", [128, 2, T])
        gcol = put("gcol", [128, 2, 4])
        row_g = put("row_g", [4, T])
        row_m = put("row_m", [4, T])
        row_n = put("row_n", [4, T])
        cos = put("cos", [128, T])
        sin = put("sin", [128, T])
        row_i = place("row_i", [4, T], at=cursor[0])
        row_f = place("row_f", [4, T], at=cursor[0] + 4 * T)
        a_q = put("a_q", [128, 2, T])
        a_k = put("a_k", [128, 2, T])
        a_v = put("a_v", [128, 2, T])
        prob_t = put("prob_t", [128, 384])
        a_stat = put("a_stat", [128, 8])
        assert cursor[0] <= C + REGION, cursor[0] - C
        merged = place("merged", [128, KT, 2 * T], f32r, at=C)
        y_2 = place("y_2", [128, KT, T], at=ACT_SPLIT)
        ps = ctx.enter_context(nc.psum_tensor("ps", [128, 8, 512], f32))

        def P(name, k=0, n=1):
            at = PARAM[name] + k
            return par[:, at:at + n] if isinstance(at, int) else par[:, bass.ds(at, n)]

        def K(name, k=0, n=1):
            return con[:, CONST[name] + k:CONST[name] + k + n]

        identity, ones = K("identity", 0, 128), K("ones", 0, 128)

        def bcast(row, tiles=2):
            return row.rearrange("p (a t) -> p a t", a=1).to_broadcast([128, tiles, T])

        def sem(name):
            return ctx.enter_context(nc.semaphore(name))

        raw_full = [sem(f"raw_full{i}") for i in range(RAW_SLOTS)]
        hi_ready = sem("hi_ready")
        lo_ready = sem("lo_ready")
        piece_used = sem("piece_used")
        low_ready = sem("low_ready")
        pair_combined = sem("pair_combined")
        x_loaded = [sem(f"x_loaded{i}") for i in range(4)]
        first_loaded = sem("first_loaded")
        gains_loaded, small_loaded, pos_loaded, forget_loaded, stored = (
            sem(n) for n in ("gains_loaded", "small_loaded", "pos_loaded", "forget_loaded", "stored"))
        cleared = sem("cleared")
        squares_ready = sem("squares_ready")
        squares_added = sem("squares_added")
        post_folded = sem("post_folded")
        ln_folded = sem("ln_folded")
        stat_summed = sem("stat_summed")
        mean_summed = sem("mean_summed")
        root_ready = sem("root_ready")
        scale_ready = sem("scale_ready")
        x_ready = sem("x_ready")
        y_gained = sem("y_gained")
        y_scaled = sem("y_scaled")
        pool_x_ready = sem("pool_x_ready")
        norm_hi = sem("norm_hi")
        h_ready = sem("h_ready")

        vector_step = sem("vector_step")
        tanh_ready = sem("tanh_ready")
        glu_ready = sem("glu_ready")
        taps_done = sem("taps_done")
        pool_step = sem("pool_step")
        tap_ready = sem("tap_ready")
        taps_added = sem("taps_added")
        conv_b_ready = sem("conv_b_ready")
        centered = sem("centered")
        ln_squared = sem("ln_squared")
        ln_scaled = sem("ln_scaled")
        ln_affine = sem("ln_affine")
        ln_tanh = sem("ln_tanh")
        ln_silu = sem("ln_silu")
        b_hi = sem("b_hi")
        b_split = sem("b_split")
        cv_ready = sem("cv_ready")
        conv_a_started = sem("conv_a_started")
        a_mixed = sem("a_mixed")
        a_hi = sem("a_hi")
        a_split = sem("a_split")
        pooled_ready = sem("pooled_ready")
        pool_summed = sem("pool_summed")
        c_hi = sem("c_hi")
        c_split = sem("c_split")
        conv_started = sem("conv_started")
        conv_done = sem("conv_done")
        gate_ready = sem("gate_ready")
        units_ready = sem("units_ready")
        unit_hi = sem("unit_hi")
        unit_split = sem("unit_split")
        y_summed = sem("y_summed")
        rows_split = sem("rows_split")
        row_step = sem("row_step")
        rows_ready = sem("rows_ready")
        columns_summed = sem("columns_summed")
        columns_ready = sem("columns_ready")
        angle_ready = sem("angle_ready")
        table_step = sem("table_step")
        qk_started = sem("qk_started")
        qk_convolved = sem("qk_convolved")
        qk_tanh = sem("qk_tanh")
        qk_ready = sem("qk_ready")
        o_ready = sem("o_ready")
        rows_bcast = sem("rows_bcast")
        m_scored = sem("m_scored")
        v_tok_ready = sem("v_tok_ready")
        decay_started = sem("decay_started")
        decay_ready = sem("decay_ready")
        s_ts_ready = sem("s_ts_ready")
        m_valued = sem("m_valued")
        den_ready = sem("den_ready")
        m_divided = sem("m_divided")
        m_squared = sem("m_squared")
        m_gated = sem("m_gated")
        m_hi = sem("m_hi")
        m_split = sem("m_split")
        rope_ready = sem("rope_ready")
        a_scored = sem("a_scored")
        a_v_ready = sem("a_v_ready")
        a_max_ready = sem("a_max_ready")
        a_exp_ready = sem("a_exp_ready")
        prob_ready = sem("prob_ready")
        prob_turned = sem("prob_turned")
        prob_t_ready = sem("prob_t_ready")
        a_valued = sem("a_valued")
        a_hi_2 = sem("a_hi_2")
        a_split_2 = sem("a_split_2")
        merge_tanh = sem("merge_tanh")
        merge_summed = sem("merge_summed")
        merge_hi = sem("merge_hi")
        merge_split = sem("merge_split")

        MERGE_FIRST = (0, 4, 8, 12, 16, 18, 20, 22)
        MERGE_LAST = (3, 7, 11, 15, 17, 19, 21, 23)

        (N_PRE1, N_LN, N_POST1, N_PREF1, N_POSTF1, N_PRE2, N_HEAD) = range(7)
        N_POST2, N_PREF2, N_POSTF2 = (N_HEAD + 4 + n for n in range(3))
        SUMMED = {e: n for n, e in enumerate(
            (N_PRE1, N_POST1, N_PREF1, N_POSTF1, N_PRE2, N_POST2, N_PREF2, N_POSTF2))}
        PRE = {e: n for n, e in enumerate((N_PRE1, N_PREF1, N_PRE2, N_PREF2))}
        POST = {e: n for n, e in enumerate((N_POST1, N_POSTF1, N_POST2, N_POSTF2))}
        NORM_BANK = {N_POSTF1: 0, N_POSTF2: 0}
        FIRST_TWO = [(n // 2 % 2, n // 4 * 2 + n % 2) for n in range(8)]

        SUMMED_BEFORE = {e: max((f + 1 for f in SUMMED if f < e), default=0) for e in SUMMED}
        ADDED_BEFORE = {e: sum(8 if f in PRE else 5 for f in SUMMED if f < e) for e in SUMMED}
        M_PE, M_ACT, M_DVE = (0, 5, 10), (3, 4, 8, 10, 13, 15), (3, 5, 9, 14, 16)
        A_PE = ((2, 6, 9), (4, 9, 12))
        A_ACT, A_DVE = ((5, 6, 9, 12), (7, 8, 12, 15)), ((5, 7, 13), (7, 9, 16))
        GATE_COLUMNS = 14
        BOUNDARY_SPLITS = {1: 3, 3: 4, 4: 5, 5: 6, 6: 7}
        POOL_PAIRS = 3
        MEAN_SUM, CENTER, SQUARE, VAR_SUM, VAR_ROOT, VAR_SCALE, LN_TANH, LN_SILU, LN_HI, LN_LO = (
            55, 58, 59, 61, 64, 65, 66, 67, 68, 69)
        TAP_PIECES = 39
        TAP_PIECES_3 = 21

        ROUND = 1.5 * 2.0 ** 23
        PI_BELOW = 3.1415925
        TURN_PARTS = turn_parts()

        def at_least(eng, s, value):
            if not isinstance(value, int) or value > 0:
                eng.wait_ge(s, value)

        NARROW, WIDE = 4, 8
        W1 = 0
        O1 = W1 + 17 * NARROW
        M1 = O1 + 4 * WIDE
        GROUPS1 = (4, 4, 3)
        up1, down1, at = [], [], M1
        for n in GROUPS1:
            up1.append(at)
            down1.append(at + n * 2 * WIDE)
            at += n * 2 * WIDE + 4 * (2 * n)
        W2 = at
        G2 = W2 + 2 * NARROW
        Y2 = W2 + 28 * NARROW + 2
        O2 = Y2 + 8 * 12
        M2 = O2 + 4 * WIDE
        END = M2 + 4 * 8 * WIDE
        qW1 = 0
        qO1 = qW1 + 17
        qup1, qdown1, at = [], [], qO1 + 8
        for n in GROUPS1:
            qup1.append(at)
            qdown1.append(at + 4 * n)
            at += 4 * n + 8
        qW2 = at
        qG2 = qW2 + 2
        qY2 = qW2 + 29
        qO2 = qY2 + 8 * 4
        qM2 = qO2 + 8

        def piece2(n):
            return W2 + n + (2 if n >= 2 * NARROW else 0)

        def pair2(c):
            return qW2 + c + (1 if c >= 2 else 0)

        def last_of(first, c):
            return first(NARROW * c + 3 + (2 if c == 0 else 0))

        def ends_1(n, end):
            for c in range(17):
                o = n - last_of(lambda m: m, c)
                if 4 <= o <= 8:
                    end(c, o)

        def ends_2(n, end):
            for c in range(28):
                o = n - {0: 3, 1: 5}.get(c, 4 * c + 3)
                if 4 <= o <= 8:
                    end(c, o)

        SHORT = [(0, 0), (0, 1), (0, 2), (0, 3), (1, 0), (1, 1), (1, 2), (1, 3), (0, 4), (0, 5), (1, 4), (1, 5)]

        def out_lasts(pieces):
            lasts = [pieces * (c + 1) - 1 for c in range(4)]
            if pieces == 6:
                lasts[0] = SHORT.index((0, 5))
            return lasts

        def out_ends(pieces, n):
            for c, last in enumerate(out_lasts(pieces)[:3]):
                if n - last in (4, 5):
                    return [(c, n - last - 4)]
            return []

        def merge_ends(n, end):
            for c in range(8):
                if 4 <= n - MERGE_LAST[c] <= 6:
                    end(c, n - MERGE_LAST[c])

        CHUNKS1 = [(kind, j) for j in range(3) for kind in ("val", "gate")]
        CHUNKS1 += [(kind, j) for j in range(3) for kind in ("b", "c", "v")]
        CHUNKS1 += [("pool", j) for j in range(2)]
        COLUMN1 = {"b": 0, "c": 768, "v": 1536, "val": 2304, "gate": 3072, "pool": 3840}
        COLUMN2 = {"q": 0, "k": 1024, "v": 2048, "o": 3072, "aq": 4104, "ak": 5128, "av": 6152,
                   "gm": 7176, "ga": 9224}
        CHUNKS2 = [(kind, h) for h in range(4) for kind in ("q", "k", "v", "o")]
        CHUNKS2 += [(kind, j) for j in range(4) for kind in ("aq", "ak", "av")]

        block = ctx.enter_context(nc.Block())

        @block.sync
        def _(sp):
            GAINS = PARAM["conv_a_w"]

            def load_x(quarter):
                tiles = slice(4 * quarter, 4 * quarter + 4)
                sp.dma_start(x[:, tiles, :], xT[:, tiles, :]).then_inc(x_loaded[quarter], 16)

            def load(n, w, row, col, deep):
                slot, cols = n.slot(RAW_SLOTS), 2048 // deep
                sp.wait_ge(lo_ready, n.times(2).value(2))
                sp.dma_start(raw[:, slot, :].rearrange("p (k n) -> p k n", k=deep),
                             w[row:row + 128 * deep, bass.ds(col, cols)].rearrange("(k p) n -> p k n", p=128)
                             ).then_inc(raw_full[slot], 16)

            def load_in(n, w, chunks, column, c, b):
                kind, j = chunks[c]
                load(Step(n), w, 1024 * b, column[kind] + 256 * j, 8)

            def load_first_two(i, w, chunks, column, first):
                load_in(first // 2 + i, w, chunks, column, i % 2, i // 2)

            load_x(0)
            sp.dma_start(par[:, 0:GAINS], params[:, 0:GAINS]).then_inc(gains_loaded, 16)
            columns = COLUMN1[CHUNKS1[0][0]]
            for half, loaded in enumerate((first_loaded, raw_full[0])):
                sp.dma_start(raw[:, 0, 1024 * half:1024 * half + 1024].rearrange("p (k n) -> p k n", k=4),
                             w_in[512 * half:512 * half + 512, columns:columns + 256
                                  ].rearrange("(k p) n -> p k n", p=128)).then_inc(loaded, 16)
            load_x(1)
            load_first_two(1, w_in, CHUNKS1, COLUMN1, W1)
            load_x(2)
            load_x(3)
            sp.dma_start(con[:, :], consts).then_inc(small_loaded, 16)
            sp.dma_start(par[:, GAINS:], params[:, GAINS:]).then_inc(small_loaded, 16)
            load_first_two(2, w_in, CHUNKS1, COLUMN1, W1)
            load_first_two(3, w_in, CHUNKS1, COLUMN1, W1)
            for c in range(2, 17):
                for b in range(2):
                    load_in(W1 // 2 + 2 * c + b, w_in, CHUNKS1, COLUMN1, c, b)
            with sp.Fori(1, 5) as i:
                for b in range(4):
                    load(Step(O1 // 2 + b - 4, i, 4), w_out, 512 * b, i * 512 - 512, 4)
            first = 0
            for g, n in enumerate(GROUPS1):
                with sp.Fori(1, n + 1) as i:
                    for half in range(2):
                        for b in range(4):
                            load(Step(up1[g] // 2 + 4 * half + b - 8, i, 8),
                                 w_up, 512 * b, i * 512 + (FF1 * half + 512 * (first - 1)), 4)
                order = [(i, b) for i in range(4) for b in range(n)]
                if n == 3:
                    order[:6] = [(c, p // 2) for c, p in SHORT[::2]]
                for m, (i, b) in enumerate(order):
                    load(Step(down1[g] // 2 + m), w_down, 512 * (first + b), i * 512, 4)
                first += n
            for i in range(4):
                load_first_two(i, w_in_2, CHUNKS2, COLUMN2, W2)
            n = Step(G2 // 2)
            slot = n.slot(RAW_SLOTS)
            sp.wait_ge(lo_ready, n.base * 2 + 2)
            gates = raw[:, slot, :].rearrange("p (k s n) -> p k s n", k=16, s=2)
            for half, s in enumerate((raw_full[slot], forget_loaded)):
                sp.dma_start(gates[:, :, half, :],
                             w_in_2[:, 4096 + 4 * half:4160 + 4 * half].rearrange("(k p) n -> p k n", p=128)
                             ).then_inc(s, 16)
            for c in range(2, 28):
                for b in range(2):
                    load_in(piece2(4 * c + 2 * b) // 2, w_in_2, CHUNKS2, COLUMN2, c, b)
            with sp.Fori(1, 5) as i:
                for half in range(2):
                    for b, kind in enumerate(("gm", "ga")):
                        for g in range(2):
                            load(Step(Y2 // 2 + 4 * half + 2 * b + g - 12, i, 12),
                                 w_in_2, 1024 * g, i * 512 + (COLUMN2[kind] + 256 * half - 512), 8)
                for half in range(2):
                    for g, w in enumerate((w_branch_m_2, w_branch_a_2)):
                        load(Step(Y2 // 2 + 8 + 2 * half + g - 12, i, 12), w, 0, i * 512 + (256 * half - 512), 8)
            with sp.Fori(1, 5) as i:
                for b in range(4):
                    load(Step(O2 // 2 + b - 4, i, 4), w_out_2, 512 * b, i * 512 - 512, 4)
            for g in range(4):
                with sp.Fori(1, 5) as i:
                    for b in range(4):
                        load(Step(M2 // 2 + 32 * g + b - 4, i, 4), w_up_2, 512 * b, i * 512 + (2048 * g - 512), 4)
                with sp.Fori(1, 5) as i:
                    for b in range(4):
                        load(Step(M2 // 2 + 32 * g + 16 + b - 4, i, 4), w_down_2, 2048 * g + 512 * b, i * 512 - 512, 4)
            for q in (3, 0, 4, 1, 5, 6, 2, 7):
                if q < POOL_PAIRS:
                    sp.wait_ge(pool_x_ready, q + 1)
                else:
                    sp.wait_ge(x_ready, 8 * POST[N_POSTF2] + q - POOL_PAIRS + 1)
                sp.dma_start(outT[:, 2 * q:2 * q + 2, :], x[:, 2 * q:2 * q + 2, :]).then_inc(stored, 16)
            sp.wait_ge(stored, 8 * 16)

        @block.tensor
        def _(pe):
            def piece(n, p, kn, banks, rhs, pieces, need=None):
                slot, across = n.slot(SPLIT_SLOTS), len(banks)
                pe.wait_ge(lo_ready, n.value(LO_CREDIT + 1))
                for kk in range(kn):
                    k = p * kn + kk
                    if need is not None and (k % 2 == 0 or kn == 1):
                        ready, value = need(k)
                        pe.wait_ge(ready, value)
                    for t, bank in enumerate(banks):
                        cols = slice((kk * across + t) * 128, (kk * across + t + 1) * 128)
                        nc.tensor.matmul(ps[:, bank, :], w_hi[:, slot, cols], rhs[:, k, :],
                                         start=(k == 0), stop=False)
                        last = nc.tensor.matmul(ps[:, bank, T:2 * T], w_lo[:, slot, cols], rhs[:, k, 0:T],
                                                start=False, stop=(k == pieces * kn - 1))
                last.then_inc(piece_used, 1)

            def narrow_chunk(n, q, bank, rhs, pieces=4, need=None, between=None, after=1):
                pe.wait_ge(pair_combined, q.value(PAIR_CREDIT - after))
                for p in range(pieces):
                    if between is not None:
                        between(p)
                    piece(n.plus(p), p, 4, (bank, bank + 1), rhs, pieces, need)

            def wide_chunk(n, q, bank, rhs, pieces=8, need=None, after=2, between=None):
                if after is not None:
                    pe.wait_ge(pair_combined, q.value(PAIR_CREDIT - after))
                for p in range(pieces):
                    if between is not None:
                        between(p)
                    piece(n.plus(p), p, 2, range(bank, bank + 4), rhs, pieces, need)

            def sum_channels(tiles, bank, summed):
                for i, tile in enumerate(tiles):
                    last = nc.tensor.matmul(ps[:, bank, 0:T], ones, tile, start=(i == 0), stop=(i == len(tiles) - 1))
                last.then_inc(summed, 1)

            def sum_norm(norm):
                if norm in POST:
                    pe.wait_ge(post_folded, POST[norm] + 1)
                else:
                    pe.wait_ge(squares_added, ADDED_BEFORE[norm] + 8)
                sum_channels([square_sum[:, 0, :]], NORM_BANK.get(norm, 7), stat_summed)

            def first_two(first, need, norm):
                for n, (c, p) in enumerate(FIRST_TWO):
                    if n == 6:
                        sum_norm(norm)
                    piece(Step(first + n), p, 4, (2 * c, 2 * c + 1), h_split, 4, need)

            def h_need(norm):
                return lambda k: (h_ready, 8 * PRE[norm] + k // 2 + 1)

            pe.sem_inc(piece_used, USED_CREDIT)
            first_two(W1, h_need(N_PRE1), N_PRE1)
            with pe.Fori(1, 6) as i:
                for c in range(2):
                    narrow_chunk(Step(W1 + 4 * c, i, 8), Step(qW1 + c, i, 2), 2 * c, h_split)

            def layer_norm(n):
                if n == MEAN_SUM:
                    pe.wait_ge(ln_folded, 1)
                    sum_channels([square_sum[:, 0, :]], 7, mean_summed)
                elif n == VAR_SUM:
                    pe.wait_ge(ln_folded, 2)
                    sum_channels([square_sum[:, 0, :]], 7, stat_summed)

            for c in range(12, 17):
                narrow_chunk(Step(W1 + 4 * c), Step(qW1 + c), 2 * (c % 2), h_split,
                             between=lambda p: layer_norm(4 * c + p))

            def pool_product(j):
                pe.wait_ge(pooled_ready, j + 1)
                for t in range(2):
                    last = nc.tensor.matmul(ps[:, 2 + j, T * t:T * t + T], P("pool_w", 128 * (2 * j + t), 128),
                                            pooled[:, t, :], start=True, stop=True)
                last.then_inc(pool_summed, 1)

            def mixed(k):
                if k < 6:
                    return a_split, k // 2 + 1
                return (b_split, (k - 6) // 2 + 1) if k < 12 else (c_split, (k - 12) // 2 + 1)

            def pools(p):
                if p == 1:
                    pool_product(0)
                elif p == 5:
                    pool_product(1)

            pe.wait_ge(root_ready, N_LN + 1)
            for c in range(4):
                wide_chunk(Step(O1 + 8 * c), Step(qO1 + 2 * c), 4 * ((c + 1) % 2), act_split,
                           need=mixed if c == 0 else None, after=2 if c else None, between=pools if c == 0 else None)
            sum_norm(N_POST1)

            def last_piece_sum(norm):
                return lambda p: sum_norm(norm) if p == 7 else None

            units = 0
            wide_chunk(Step(M1), Step(qup1[0]), 0, h_split, need=h_need(N_PREF1), between=last_piece_sum(N_PREF1))
            pe.wait_ge(root_ready, N_PREF1 + 1)
            wide_chunk(Step(M1 + 8), Step(qup1[0] + 2), 4, h_split)
            for g, n in enumerate(GROUPS1):
                with pe.Fori(0 if g else 1, n) as i:
                    for half in range(2):
                        wide_chunk(Step(up1[g] + 8 * half, i, 16), Step(qup1[g] + 2 * half, i, 4), 4 * half, h_split)
                need = lambda k: (unit_split, units + k // 2 + 1)
                if n == 3:
                    for m, (c, p) in enumerate(SHORT):
                        if p == 0:
                            pe.wait_ge(pair_combined, PAIR_CREDIT + qdown1[g] + 2 * c - 2)
                        piece(Step(down1[g] + m), p, 2, range(4 * c, 4 * c + 4), act_split, 6, need)
                with pe.Fori(1 if n == 3 else 0, 2) as i:
                    for c in range(2):
                        wide_chunk(Step(down1[g] + 2 * n * c, i, 4 * n), Step(qdown1[g] + 2 * c, i, 4), 4 * c,
                                   act_split, pieces=2 * n, need=need if c == 0 and n > 3 else None)
                units += 2 * n
            sum_norm(N_POSTF1)
            first_two(W2, h_need(N_PRE2), N_PRE2)
            for p in range(2):
                piece(Step(G2 + p), p, 8, (4,), h_split, 2)

            def gate_columns():
                pe.wait_ge(rows_ready, 1)
                for half in range(2):
                    last = nc.tensor.matmul(ps[:, 6, 4 * half:4 * half + 4], row_g[0:4, 128 * half:128 * half + 128],
                                            identity[0:4, 0:4], start=True, stop=True)
                last.then_inc(columns_summed, 1)

            def mlstm(h, stage):
                if stage == 0:
                    pe.wait_ge(qk_ready, 2 * h + 2)
                    pe.wait_ge(pair_combined, PAIR_CREDIT + pair2(4 * h + 2) + 1)
                    at_least(pe, m_split, h)
                    for r, row in enumerate((row_m, row_n)):
                        last = nc.tensor.matmul(ps[:, 7, T * r:T * r + T], K("select", 128 * h, 128)[0:4, :],
                                                row[0:4, :], start=True, stop=True)
                    last.then_inc(rows_bcast, 1)
                    for s in range(2):
                        out = ps[:, 4, 0:256] if s == 0 else ps[:, 4, 256:384]
                        for t in range(2):
                            nc.tensor.matmul(out, k_m[:, t, 128 * s:128 * s + 128], q_m[:, t, 128 * s:T],
                                             start=(t == 0), stop=(t == 1))
                    for s in range(2):
                        for t in range(2):
                            last = nc.tensor.transpose(ps[:, 5, T * s + 128 * t:T * s + 128 * t + 128],
                                                       v_m[:, t, 128 * s:128 * s + 128], identity)
                    last.then_inc(m_scored, 1)
                elif stage == 1:
                    pe.wait_ge(v_tok_ready, h + 1)
                    pe.wait_ge(s_ts_ready, h + 1)
                    for out, stationary in (((5, 0), lambda s: v_tok[:, s, 0:128]),
                                            ((5, T), lambda s: v_tok[:, s, 128:256]),
                                            ((6, 0), lambda s: ones)):
                        bank, col = out
                        nc.tensor.matmul(ps[:, bank, col:col + T], stationary(0), s_ts[:, 0:256],
                                         start=True, stop=False)
                        last = nc.tensor.matmul(ps[:, bank, col + 128:col + T], stationary(1), s_ts[:, 256:384],
                                                start=False, stop=True)
                    last.then_inc(m_valued, 1)
                elif stage == 2:
                    pe.wait_ge(m_squared, h + 1)
                    sum_channels([den_m[:, 0, :], den_m[:, 1, :]], 7, stat_summed)

            def attention(j, a, stage):
                t = 2 * j + a
                if stage == 0:
                    pe.wait_ge(rope_ready, 2 * j + 2)
                    pe.wait_ge(pair_combined, PAIR_CREDIT + pair2(16 + 3 * j + 2) + 1)
                    pe.wait_ge(m_divided, 4)
                    at_least(pe, a_max_ready, t)
                    at_least(pe, a_v_ready, t)
                    nc.tensor.matmul(ps[:, 4, 0:128], a_q[:, a, 0:128], a_k[:, a, 0:128], start=True, stop=True)
                    nc.tensor.matmul(ps[:, 4, 128:384], a_q[:, a, 128:256], a_k[:, a, :], start=True, stop=True)
                    for s in range(2):
                        last = nc.tensor.transpose(ps[:, 5, 128 * s:128 * s + 128],
                                                   a_v[:, a, 128 * s:128 * s + 128], identity)
                    last.then_inc(a_scored, 1)
                elif stage == 1:
                    pe.wait_ge(prob_ready, t + 1)
                    at_least(pe, prob_t_ready, t)
                    for s in range(3):
                        last = nc.tensor.transpose(ps[:, 6, 128 * s:128 * s + 128],
                                                   s_ts[:, 128 * s:128 * s + 128], identity)
                    last.then_inc(prob_turned, 1)
                else:
                    pe.wait_ge(prob_t_ready, t + 1)
                    at_least(pe, a_split_2, t)
                    nc.tensor.matmul(ps[:, 7, 0:256], v_tok[:, a, 0:128], prob_t[:, 0:256], start=True, stop=False)
                    nc.tensor.matmul(ps[:, 7, 128:256], v_tok[:, a, 128:256], prob_t[:, 256:384],
                                     start=False, stop=True).then_inc(a_valued, 1)

            def inner(piece_number):
                if piece_number == GATE_COLUMNS:
                    gate_columns()
                for h in range(4):
                    r = piece_number - 16 * (h + 1)
                    if r in M_PE:
                        mlstm(h, M_PE.index(r))
                for j in range(4):
                    r = piece_number - (64 + 12 * (j + 1))
                    for a in range(2):
                        if r in A_PE[a]:
                            attention(j, a, A_PE[a].index(r))

            for c in range(2, 28):
                narrow_chunk(Step(piece2(4 * c)), Step(pair2(c)), 2 * (c % 2), h_split,
                             between=lambda p: inner(4 * c + p), after=2 if c == 2 else 1)

            def merge_chunks(i, between=lambda n: None):
                for c, first in enumerate(MERGE_FIRST):
                    pieces = 4 if c < 4 else 2
                    branch = act_split[:, 8 * (c % 2):8 * (c % 2) + 8, :]
                    done = (a_split_2, 8) if c % 2 else (m_split, 4)
                    narrow_chunk(Step(Y2 + first, i, 24), Step(qY2 + c, i, 8), 2 * (c % 2),
                                 h_split if c < 4 else branch, pieces=pieces,
                                 between=lambda p: between(first + p), need=None if c < 4 else lambda k: done)

            merge_chunks(None, between=lambda n: inner(112 + n))
            with pe.Fori(1, 4) as i:
                merge_chunks(i)
            wide_chunk(Step(O2), Step(qO2), 4, merged, need=lambda k: (merge_split, k // 2 + 1), after=None)
            for c in range(1, 4):
                wide_chunk(Step(O2 + 8 * c), Step(qO2 + 2 * c), 4 * ((c + 1) % 2), merged)
            sum_norm(N_POST2)
            wide_chunk(Step(M2), Step(qM2), 0, h_split, need=h_need(N_PREF2), between=last_piece_sum(N_PREF2))
            pe.wait_ge(root_ready, N_PREF2 + 1)

            def group_2(g, up_from=0):
                for c in range(up_from, 4):
                    wide_chunk(Step(M2 + 8 * c).along(g, 64), Step(qM2 + 2 * c).along(g, 16), 4 * (c % 2), h_split)
                with pe.Fori(0, 2) as i:
                    for c in range(2):
                        wide_chunk(Step(M2 + 32 + 8 * c, i, 16).along(g, 64), Step(qM2 + 8 + 2 * c, i, 4).along(g, 16),
                                   4 * c, act_split,
                                   need=(lambda k: (unit_split, Step(22 + k // 2 + 1).along(g, 8).value()))
                                   if c == 0 else None)

            group_2(None, up_from=1)
            with pe.Fori(1, 4) as g:
                group_2(g)
            sum_norm(N_POSTF2)

        @block.scalar
        def _(act):
            def split(n, loaded=None):
                block_n = Step(n.base // 2, terms=tuple((i, r // 2) for i, r in n.terms))
                slot, half = block_n.slot(RAW_SLOTS), 1024 * (n.base % 2)
                if loaded or (loaded is None and not half):
                    act.wait_ge(raw_full[slot], block_n.turn(RAW_SLOTS).times(16).value(16))
                act.wait_ge(piece_used, n.value(1))
                nc.scalar.activation(w_hi[:, n.slot(SPLIT_SLOTS), :], raw[:, slot, half:half + 1024],
                                     ACT.Copy).then_inc(hi_ready, 1)

            def low_copy(q, bank, last, tiles=2):
                act.wait_ge(piece_used, last.value(USED_CREDIT + 1))
                act.wait_ge(pair_combined, q.value(PAIR_CREDIT - 1))
                nc.scalar.activation(low[:, q.slot(2), 0:tiles, :], ps[:, bank:bank + tiles, T:2 * T],
                                     ACT.Copy).then_inc(low_ready, 1)

            def combined(q):
                act.wait_ge(pair_combined, q.value(PAIR_CREDIT + 1))

            def square(norm, q, ready, value, source):
                s = 8 * SUMMED[norm] + q
                act.wait_ge(ready, value)
                if q < 2:
                    at_least(act, stat_summed, SUMMED_BEFORE[norm])
                    at_least(act, squares_added, ADDED_BEFORE[norm])
                else:
                    act.wait_ge(squares_added, ADDED_BEFORE[norm] + max(q - 2, 1))
                nc.scalar.activation(squares[:, s % 2, :, :], source[:, 2 * q:2 * q + 2, :],
                                     ACT.Square).then_inc(squares_ready, 1)

            def take_root(norm, channels, times=1):
                act.wait_ge(stat_summed, norm + 1)
                at_least(act, scale_ready, norm)
                eps = K("epsilon", {1: 0, 2: 2}[times] if norm != N_LN else 1)
                nc.scalar.activation(root[:, :], ps[:, NORM_BANK.get(norm, 7), 0:T], ACT.Sqrt, bias=eps,
                                     scale=times * times / channels).then_inc(root_ready, 1)

            def high_pair(norm, gain, q, ready, value):
                act.wait_ge(ready, value)
                for k in range(2 * q, 2 * q + 2):
                    nc.scalar.activation(h_split[:, k, 0:T], x[:, k, :], ACT.Copy, scale=P(gain, k)
                                         ).then_inc(norm_hi, 1)

            act.dma_start(pos_i[:, :], positions.partition_broadcast(128)).then_inc(pos_loaded, 16)
            act.wait_ge(gains_loaded, 16)
            for i in range(4):
                for q in (2 * i, 2 * i + 1):
                    high_pair(N_PRE1, "norm_mix_pre", q, x_loaded[i], 16)
                if i == 0:
                    act.wait_ge(first_loaded, 16)
                split(Step(W1 + i), loaded=i > 0)
                for q in (2 * i, 2 * i + 1):
                    square(N_PRE1, q, x_loaded[i], 16, x)
            split(Step(W1 + 4))
            act.wait_ge(small_loaded, 32)

            def finish_conv_b(j):
                if j == 2:
                    act.wait_ge(taps_added, 30)
                else:
                    act.wait_ge(taps_done, j + 1)
                for t in range(2 * j, 2 * j + 2):
                    nc.scalar.activation(conv_b[:, t, :], conv_b[:, t, :], ACT.Identity, scale=0.5,
                                         bias=P("conv_b_bias", t)).then_inc(conv_b_ready, 1)

            def tap_b(k):
                if k == 0:
                    act.wait_ge(glu_ready, 3)
                    act.wait_ge(cleared, 3)
                elif k > 2:
                    act.wait_ge(taps_added, k - 2)
                for t in range(2):
                    out = gate_pair[:, k % 2, t, :] if k else conv_b[:, 4 + t, :]
                    nc.scalar.activation(out, glu[:, 4 + t, k:k + T], ACT.Copy, scale=P("conv_b_w", 6 * k + 4 + t)
                                         ).then_inc(tap_ready, 1)

            def chunk_end_1(c, o):
                kind, j = CHUNKS1[c]
                q = Step(qW1 + c)
                if o == 4:
                    low_copy(q, 2 * (c % 2), Step(last_of(lambda n: W1 + n, c)))
                elif o == 5 and kind == "gate":
                    combined(q)
                    nc.scalar.activation(tanh_b[:, :, :], tanh_b[:, :, :], ACT.Tanh, scale=0.5).then_inc(tanh_ready, 1)
                elif o == 5 and kind == "v":
                    act.wait_ge(cv_ready, j + 1)
                    for t in range(2):
                        nc.scalar.activation(conv_a[:, t, :], cv[:, t, 2:2 + T], ACT.Copy,
                                             scale=P("conv_a_w", 12 + 2 * j + t)).then_inc(conv_a_started, 1)
                elif o == 7 and kind == "v":
                    act.wait_ge(a_mixed, j + 1)
                    nc.scalar.activation(act_split[:, 2 * j:2 * j + 2, 0:T], conv_a[:, :, :],
                                         ACT.Copy).then_inc(a_hi, 1)

            def layer_norm(n):
                if n == SQUARE:
                    for j in range(3):
                        act.wait_ge(centered, j + 1)
                        nc.scalar.activation(ln_squares[:, 2 * j:2 * j + 2, :], conv_b[:, 2 * j:2 * j + 2, :],
                                             ACT.Square).then_inc(ln_squared, 1)
                elif n == VAR_ROOT:
                    take_root(N_LN, 768)
                for j in range(3):
                    pair = slice(2 * j, 2 * j + 2)
                    if n == LN_TANH + j:
                        act.wait_ge(ln_scaled, j + 1)
                        for t in range(2 * j, 2 * j + 2):
                            nc.scalar.activation(conv_b[:, t, :], conv_b[:, t, :], ACT.Identity,
                                                 scale=P("ln_b_gain", t), bias=P("ln_b_bias", t)).then_inc(ln_affine, 1)
                        act.wait_ge(ln_affine, 2 * j + 2)
                        nc.scalar.activation(ln_squares[:, pair, :], conv_b[:, pair, :], ACT.Tanh, scale=0.5
                                             ).then_inc(ln_tanh, 1)
                    elif n == LN_HI + j:
                        act.wait_ge(ln_silu, j + 1)
                        nc.scalar.activation(act_split[:, 6 + 2 * j:8 + 2 * j, 0:T], conv_b[:, pair, :],
                                             ACT.Copy, scale=0.5).then_inc(b_hi, 1)

            def pool_end(j):
                act.wait_ge(pool_summed, j + 1)
                for t in range(2):
                    k = 2 * j + t
                    nc.scalar.activation(act_split[:, 12 + k, 0:T], ps[:, 2 + j, T * t:T * t + T], ACT.Copy,
                                         scale=P("pool_scale", k)).then_inc(c_hi, 1)

            def first_mixer(n):
                if n == 9:
                    take_root(N_PRE1, D)
                ends_1(n, chunk_end_1)
                if 30 <= n < 30 + TAP_PIECES_3:
                    for k in range(31 * (n - 30) // TAP_PIECES_3, 31 * (n - 29) // TAP_PIECES_3):
                        tap_b(k)
                if n == 15 + TAP_PIECES // 2:
                    finish_conv_b(0)
                elif n == 13 + TAP_PIECES:
                    finish_conv_b(2)
                    finish_conv_b(1)
                layer_norm(n)

            for n in range(4 * 17):
                if n > 4:
                    split(Step(W1 + n))
                first_mixer(n)

            def wide_end(q, bank, last, r):
                low_copy(q.plus(r), bank + 2 * r, last)

            def y_squares(norm, q0, q, y):
                square(norm, q, *y_pair_ready(norm, q0, q), y)
                if norm == N_POSTF2 and q < POOL_PAIRS:
                    act.wait_ge(squares_ready, 8 * SUMMED[norm] + q + 1)
                    for k in range(2 * q, 2 * q + 2):
                        nc.scalar.activation(y[:, k, :], y[:, k, :], ACT.Copy, scale=P("norm_ffn_post_2", k)
                                             ).then_inc(y_gained, 1)

            def y_pair_ready(norm, q0, q):
                if norm in (N_POST1, N_POST2):
                    return pair_combined, PAIR_CREDIT + q0 + q + 1
                groups = len(GROUPS1) - 1 if norm == N_POSTF1 else len(GROUPS1) - 1 + 3
                return y_summed, 8 * (groups - 1) + q + 1

            def out_product(n0, q0, pieces, norm, y, before, between=lambda n: None, flip=0):
                for n in range(4 * pieces):
                    split(Step(n0 + n))
                    between(n0 + n)
                    before(n)
                    for c, r in out_ends(pieces, n):
                        wide_end(Step(q0 + 2 * c), 4 * ((c + flip) % 2), Step(n0 + out_lasts(pieces)[c]), r)
                        if norm is not None:
                            y_squares(norm, q0, 2 * c + r, y)

            def last_chunk(n0, q0, pieces, norm, y, next_piece=None, flip=0):
                if next_piece is not None:
                    for p in range(3):
                        split(Step(next_piece + p))
                for r in range(2):
                    wide_end(Step(q0 + 6), 4 * (1 - flip), Step(n0 + 4 * pieces - 1), r)
                for r in range(2):
                    y_squares(norm, q0, 6 + r, y)

            def post_and_pre(post, pre, gain, next_piece):
                take_root(post, D)
                for q in range(8):
                    if q in BOUNDARY_SPLITS:
                        split(Step(next_piece + BOUNDARY_SPLITS[q]))
                    high_pair(pre, gain, q, x_ready, 8 * POST[post] + q + 1)
                    square(pre, q, x_ready, 8 * POST[post] + q + 1, x)

            def first_pools(n):
                first_mixer(n)
                if n == O1 + 4:
                    pool_end(0)
                elif n == O1 + 8:
                    pool_end(1)

            out_product(O1, qO1, 8, N_POST1, y, before=lambda p: None, between=first_pools, flip=1)
            last_chunk(O1, qO1, 8, N_POST1, y, M1, flip=1)
            post_and_pre(N_POST1, N_PREF1, "norm_ffn_pre", M1)

            def start_conv(chunk, r, half, out):
                for t in range(2):
                    k = chunk.times(4).value(44 * half + 2 * r + t)
                    nc.scalar.activation(out[:, 2 * r + t, :], up_in[:, 2 * r + t, 2:2 + T], ACT.Identity,
                                         scale=P("conv_ffn_w", 2 * 88 + k), bias=P("conv_ffn_bias", k)
                                         ).then_inc(conv_started, 1)

            def gate_end(n0, q0, chunk, p):
                if p in (3, 4):
                    r = p - 3
                    low_copy(q0.plus(r), 2 * r, n0.plus(7))
                if p in (4, 5):
                    r = p - 4
                    combined(q0.plus(r))
                    start_conv(chunk, r, 0, gate_conv)
                if p in (6, 7):
                    r = p - 6
                    act.wait_ge(conv_done, chunk.times(2).value(r + 1))
                    pair = slice(2 * r, 2 * r + 2)
                    nc.scalar.activation(gate_tanh[:, pair, :], gate_conv[:, pair, :], ACT.Tanh,
                                         scale=0.5).then_inc(gate_ready, 1)

            def val_end(n0, q0, chunk, first, p):
                if p in (3, 4):
                    r = p - 3
                    low_copy(q0.plus(2 + r), 4 + 2 * r, n0.plus(15))
                if p in (4, 5):
                    r = p - 4
                    combined(q0.plus(2 + r))
                    start_conv(chunk, r, 1, val_conv)
                if p in (6, 7):
                    r = p - 6
                    act.wait_ge(units_ready, chunk.times(2).value(r + 1))
                    k = chunk.times(4).value(2 * r - 4 * first)
                    nc.scalar.activation(act_split[:, at2(k), 0:T], gate_conv[:, 2 * r:2 * r + 2, :], ACT.Copy,
                                         scale=0.5).then_inc(unit_hi, 1)

            def at2(k):
                return slice(k, k + 2) if isinstance(k, int) else bass.ds(k, 2)

            def up_chunks(g, first, i, before, skip=0):
                n0, q0 = Step(up1[g], i, 16), Step(qup1[g], i, 4)
                chunk = Step(first, i, 1)
                for p in range(16):
                    if p >= skip:
                        split(n0.plus(p))
                    if skip and p == 9:
                        take_root(N_PREF1, D)
                    before(p)
                    gate_end(n0, q0, chunk, p - 8)

            def down_end(q0, last):
                def before(p):
                    if p in (3, 4):
                        wide_end(Step(q0 + 6), 4, Step(last), p - 3)
                return before

            first = 0
            for g, n in enumerate(GROUPS1):
                if g == 0:
                    up_chunks(0, 0, None, lambda p: None, skip=8)
                else:
                    up_chunks(g, first, None, down_end(qdown1[g - 1], down1[g - 1] + 8 * GROUPS1[g - 1] - 1))
                with act.Fori(1, n) as i:
                    up_chunks(g, first, i, lambda p: val_end(
                        Step(up1[g] - 16, i, 16), Step(qup1[g] - 4, i, 4), Step(first - 1, i, 1), first, p))
                last = g == len(GROUPS1) - 1
                out_product(down1[g], qdown1[g], 2 * n, N_POSTF1 if last else None, y, before=lambda p: val_end(
                    Step(up1[g] + 16 * (n - 1)), Step(qup1[g] + 4 * (n - 1)), Step(first + n - 1), first, p))
                first += n
            last_chunk(down1[-1], qdown1[-1], 2 * n, N_POSTF1, y, W2)
            post_and_pre(N_POSTF1, N_PRE2, "norm_mix_pre_2", W2)

            def gate_rows(n):
                if n == 11:
                    low_copy(Step(qG2), 4, Step(G2 + 1), tiles=1)
                elif n == 12:
                    act.wait_ge(rows_split, 1)
                    nc.scalar.activation(row_g[0:4, :], row_f[0:4, :], ACT.Abs).then_inc(row_step, 1)
                    act.wait_ge(row_step, 1)
                    nc.scalar.activation(row_g[0:4, :], row_g[0:4, :], ACT.Exp, scale=-1.0).then_inc(row_step, 1)
                    act.wait_ge(row_step, 2)
                    nc.scalar.activation(row_g[0:4, :], row_g[0:4, :], ACT.Ln, bias=ones[0:4, 0:1]
                                         ).then_inc(row_step, 1)

            def rope_tables():
                act.wait_ge(angle_ready, 1)
                nc.scalar.activation(sin[:, :], cos[:, :], ACT.Sin, scale=K("sign")).then_inc(table_step, 1)
                act.wait_ge(table_step, 1)
                nc.scalar.activation(cos[:, :], cos[:, :], ACT.Abs).then_inc(table_step, 1)
                act.wait_ge(table_step, 2)
                nc.scalar.activation(cos[:, :], cos[:, :], ACT.Sin, scale=-1.0, bias=K("half_pi")
                                     ).then_inc(table_step, 1)

            def chunk_end_2(c, o):
                kind, h = CHUNKS2[c]
                q = Step(pair2(c))
                if o == 4:
                    low_copy(q, 2 * (c % 2), Step(last_of(piece2, c)))
                elif o == 5 and kind in ("q", "k"):
                    is_k = int(kind == "k")
                    out = (q_m, k_m)[is_k]
                    combined(q)
                    at_least(act, m_scored, h)
                    for t in range(2):
                        k = 8 * is_k + 2 * h + t
                        nc.scalar.activation(out[:, t, :], qk_in[:, t, 3:3 + T], ACT.Identity,
                                             scale=P("conv_w_2", 48 + k), bias=P("conv_b_2", k)
                                             ).then_inc(qk_started, 1)
                elif o == 7 and kind in ("q", "k"):
                    is_k = int(kind == "k")
                    act.wait_ge(qk_convolved, 2 * h + is_k + 1)
                    nc.scalar.activation(squares[:, is_k, :, :], (q_m, k_m)[is_k][:, :, :], ACT.Tanh, scale=0.5
                                         ).then_inc(qk_tanh, 1)
                elif o == 5 and kind == "o":
                    combined(q)
                    nc.scalar.activation(o_m[:, :, :], o_m[:, :, :], ACT.Tanh, scale=0.5).then_inc(o_ready, 1)

            def mlstm(h, stage):
                if stage == 0:
                    act.wait_ge(m_scored, h + 1)
                    at_least(act, m_valued, h)
                    nc.scalar.activation(v_tok[:, :, :].rearrange("p a t -> p (a t)"), ps[:, 5, :],
                                         ACT.Copy).then_inc(v_tok_ready, 1)
                elif stage == 1:
                    act.wait_ge(decay_started, h + 1)
                    nc.scalar.activation(decay[:, :], decay[:, :], ACT.Exp, scale=-1.0).then_inc(decay_ready, 1)
                elif stage == 2:
                    act.wait_ge(m_valued, h + 1)
                    nc.scalar.activation(den_m[:, 0, :], ps[:, 6, 0:T], ACT.Abs).then_inc(den_ready, 1)
                    nc.scalar.activation(den_m[:, 1, :], ps[:, 7, T:2 * T], ACT.Exp).then_inc(den_ready, 1)
                elif stage == 3:
                    act.wait_ge(m_divided, h + 1)
                    nc.scalar.activation(den_m[:, :, :], h_m[:, :, :], ACT.Square).then_inc(m_squared, 1)
                elif stage == 4:
                    take_root(N_HEAD + h, 256, times=2)
                else:
                    act.wait_ge(m_gated, h + 1)
                    for t in range(2):
                        nc.scalar.activation(act_split[:, 2 * h + t, 0:T], h_m[:, t, :], ACT.Copy,
                                             scale=P("mlstm_norm_2", 2 * h + t)).then_inc(m_hi, 1)

            def attention(t, stage):
                if stage == 0:
                    act.wait_ge(a_scored, t + 1)
                    act.wait_ge(m_valued, 4)
                    at_least(act, a_valued, t - 1)
                    nc.scalar.activation(v_tok[:, t % 2, :], ps[:, 5, 0:T], ACT.Copy).then_inc(a_v_ready, 1)
                elif stage == 1:
                    act.wait_ge(a_max_ready, t + 1)
                    for half, cols in enumerate((slice(0, 128), slice(128, 384))):
                        nc.scalar.activation(decay[:, cols], decay[:, cols], ACT.Exp,
                                             bias=a_stat[:, 2 + half:3 + half],
                                             accum_out=a_stat[:, 4 + half:5 + half]).then_inc(a_exp_ready, 1)
                elif stage == 2:
                    act.wait_ge(prob_turned, t + 1)
                    at_least(act, a_valued, t)
                    nc.scalar.activation(prob_t[:, :], ps[:, 6, 0:384], ACT.Copy).then_inc(prob_t_ready, 1)
                else:
                    act.wait_ge(a_valued, t + 1)
                    nc.scalar.activation(act_split[:, 8 + t, 0:T], ps[:, 7, 0:T], ACT.Copy).then_inc(a_hi_2, 1)

            def second_mixer(n):
                ends_2(n, chunk_end_2)
                gate_rows(n)
                if n == 15:
                    rope_tables()
                for h in range(4):
                    r = n - 16 * (h + 1)
                    if r in M_ACT:
                        mlstm(h, M_ACT.index(r))
                for j in range(4):
                    r = n - (64 + 12 * (j + 1))
                    for a in range(2):
                        if r in A_ACT[a]:
                            attention(2 * j + a, A_ACT[a].index(r))

            for n in range(7, 4 * 28):
                if n > 7:
                    split(Step(piece2(n)))
                else:
                    act.wait_ge(forget_loaded, 16)
                    for p in range(2):
                        split(Step(G2 + p))
                    take_root(N_PRE2, D)
                second_mixer(n)

            def merge_end(c, turn, o):
                q = turn.times(8).plus(qY2 + c)
                if o == 4:
                    low_copy(q, 2 * (c % 2), turn.times(24).plus(Y2 + MERGE_LAST[c]))
                elif o == 5 and c < 4:
                    gate = (gate_pair, squares)[c // 2][:, c % 2, :, :]
                    combined(q)
                    nc.scalar.activation(gate, gate, ACT.Tanh, scale=0.5).then_inc(merge_tanh, 1)
                elif o == 5 and c % 2:
                    j = turn.times(2).plus(c // 2 - 2)
                    act.wait_ge(merge_summed, j.value(1))
                    nc.scalar.activation(merged[:, at2(j.times(2).value()), 0:T], scaled[:, 0, :, :],
                                         ACT.Copy, scale=0.5).then_inc(merge_hi, 1)

            def merge_turn(i, before):
                for n in range(24):
                    split(Step(Y2 + n, i, 24))
                    before(n)
                    merge_ends(n, lambda c, o: merge_end(c, Step(0, i, 1), o))

            merge_turn(None, lambda n: second_mixer(112 + n))
            with act.Fori(1, 4) as i:
                merge_turn(i, lambda n: merge_ends(24 + n, lambda c, o: merge_end(c, Step(-1, i, 1), o)))
            out_product(O2, qO2, 8, N_POST2, y_2, flip=1,
                        before=lambda p: merge_ends(24 + p, lambda c, o: merge_end(c, Step(3), o)))
            last_chunk(O2, qO2, 8, N_POST2, y_2, M2, flip=1)
            post_and_pre(N_POST2, N_PREF2, "norm_ffn_pre_2", M2)

            def relu_end(g, c, p):
                n, q = M2 + 64 * g + 8 * c, qM2 + 16 * g + 2 * c
                if p in (4, 5):
                    r = p - 4
                    act.wait_ge(units_ready, 22 + 8 * g + 2 * c + r + 1)
                    nc.scalar.activation(act_split[:, 4 * c + 2 * r:4 * c + 2 * r + 2, 0:T],
                                         gate_conv[:, 2 * r:2 * r + 2, :], ACT.Copy).then_inc(unit_hi, 1)
                if p in (3, 4):
                    low_copy(Step(q + p - 3), 4 * (c % 2) + 2 * (p - 3), Step(n + 7))

            for g in range(4):
                for c in range(4):
                    for p in range(8):
                        if g or c or p > 7:
                            split(Step(M2 + 64 * g + 8 * c + p))
                        if (g, c, p) == (0, 1, 1):
                            take_root(N_PREF2, D)
                        if c:
                            relu_end(g, c - 1, p)
                        elif g and p in (3, 4):
                            wide_end(Step(qM2 + 16 * g - 2), 4, Step(M2 + 64 * g - 1), p - 3)
                out_product(M2 + 64 * g + 32, qM2 + 16 * g + 8, 8, N_POSTF2 if g == 3 else None, y,
                            before=lambda p: relu_end(g, 3, p))
            last_chunk(M2 + 64 * 3 + 32, qM2 + 16 * 3 + 8, 8, N_POSTF2, y)
            take_root(N_POSTF2, D)

        @block.gpsimd
        def _(pool):
            nc.gpsimd.memset(glu[:, :, 0:30], 0.0).then_inc(cleared, 1)
            nc.gpsimd.memset(cv[:, :, 0:2], 0.0).then_inc(cleared, 1)
            nc.gpsimd.memset(pool_in[:, :, 0:16], 0.0).then_inc(cleared, 1)

            def sum_squares(norm):
                at_least(pool, stat_summed, SUMMED_BEFORE[norm])
                for q in range(1, 8 if norm in PRE else 6):
                    pool.wait_ge(squares_ready, 8 * SUMMED[norm] + q + 1)
                    if q > 1:
                        pool.wait_ge(squares_added, ADDED_BEFORE[norm] + q - 1)
                    nc.gpsimd.tensor_tensor(square_sum[:, :, :],
                                            square_sum[:, :, :] if q > 1 else squares[:, 0, :, :],
                                            squares[:, q % 2, :, :], ALU.add).then_inc(squares_added, 1)
                if norm in PRE:
                    pool.wait_ge(squares_added, ADDED_BEFORE[norm] + 7)
                    nc.gpsimd.tensor_tensor(square_sum[:, 0, :], square_sum[:, 0, :], square_sum[:, 1, :], ALU.add
                                            ).then_inc(squares_added, 1)

            def fold_six(tiles, fold):
                nc.gpsimd.tensor_tensor(square_sum[:, :, :], tiles[:, 0:2, :], tiles[:, 2:4, :], ALU.add
                                        ).then_inc(pool_step, 1)
                pool.wait_ge(pool_step, 2 * fold + 1)
                nc.gpsimd.tensor_tensor(square_sum[:, :, :], square_sum[:, :, :], tiles[:, 4:6, :], ALU.add
                                        ).then_inc(pool_step, 1)
                pool.wait_ge(pool_step, 2 * fold + 2)
                nc.gpsimd.tensor_tensor(square_sum[:, 0, :], square_sum[:, 0, :], square_sum[:, 1, :], ALU.add
                                        ).then_inc(ln_folded, 1)

            def long_convolution():
                for k in range(1, 31):
                    pool.wait_ge(tap_ready, 2 * k + 2)
                    at_least(pool, taps_added, k - 1)
                    nc.gpsimd.tensor_tensor(conv_b[:, 4:6, :], conv_b[:, 4:6, :], gate_pair[:, k % 2, :, :], ALU.add
                                            ).then_inc(taps_added, 1)

            for norm in SUMMED:
                sum_squares(norm)
                if norm == N_PRE1:
                    long_convolution()
                    pool.wait_ge(stat_summed, 1)
                    pool.wait_ge(conv_b_ready, 6)
                    fold_six(conv_b, 0)
                    pool.wait_ge(mean_summed, 1)
                    pool.wait_ge(ln_squared, 3)
                    fold_six(ln_squares, 1)
                elif norm == N_POST1:
                    nc.gpsimd.memset(up_in[:, :, 0:2], 0.0).then_inc(cleared, 1)
                elif norm == N_PRE2:
                    nc.gpsimd.memset(qk_in[:, :, 0:3], 0.0).then_inc(cleared, 1)
            pool.wait_ge(scale_ready, N_POSTF2 + 1)
            for q in range(POOL_PAIRS):
                pair = slice(2 * q, 2 * q + 2)
                pool.wait_ge(y_gained, 2 * q + 2)
                nc.gpsimd.tensor_tensor(y[:, pair, :], y[:, pair, :], bcast(scale[:, :]), ALU.mult
                                        ).then_inc(y_scaled, 1)
                pool.wait_ge(y_scaled, q + 1)
                nc.gpsimd.tensor_tensor(x[:, pair, :], x[:, pair, :], y[:, pair, :], ALU.add
                                        ).then_inc(pool_x_ready, 1)

        @block.vector
        def _(dve):
            class Taken:

                def __init__(self):
                    self.count = Step(0)

                def one(self):
                    self.count = self.count.plus(1)
                    return 1

                def all(self, but=0):
                    return self.count.value(-but)

                def enter(self, i, start, rate):
                    self.outside, self.rate, self.start = self.count, rate, start
                    self.count = self.inside = self.count.plus(-start * rate).along(i, rate)

                def leave(self, end):
                    assert self.count.base - self.inside.base == self.rate, self.count.base - self.inside.base
                    self.count = self.outside.plus((end - self.start) * self.rate)

            steps = Taken()

            def tt(out, a, b, op):
                return nc.vector.tensor_tensor(out, a, b, op)

            def stt(out, a, scalar, b, op0, op1):
                return nc.vector.scalar_tensor_tensor(out=out, in0=a, scalar=scalar, in1=b, op0=op0, op1=op1)

            def split(n):
                block_n = Step(n.base // 2, terms=tuple((i, r // 2) for i, r in n.terms))
                slot, half = block_n.slot(RAW_SLOTS), 1024 * (n.base % 2)
                dve.wait_ge(hi_ready, n.value(1))
                tt(w_lo[:, n.slot(SPLIT_SLOTS), :], raw[:, slot, half:half + 1024],
                   w_hi[:, n.slot(SPLIT_SLOTS), :].bitcast(f32), ALU.subtract).then_inc(lo_ready, 1)

            def combine(q, bank, out, tiles=2, by=None):
                dve.wait_ge(low_ready, q.value(1))
                ins = tt(out, ps[:, bank:bank + tiles, 0:T], low[:, q.slot(2), 0:tiles, :], ALU.add)
                if by is not None:
                    ins.then_inc(vector_step, steps.one())
                    dve.wait_ge(vector_step, steps.all())
                    ins = tt(out, out, bcast(by[:, :], tiles), ALU.mult)
                ins.then_inc(pair_combined, 1)

            def combined(q):
                dve.wait_ge(pair_combined, q.value(PAIR_CREDIT + 1))

            def low_half(out, value, scale, high):
                return stt(out, value, scale, high.bitcast(f32), ALU.mult, ALU.subtract)

            def make_scale(norm, out=scale):
                dve.wait_ge(root_ready, norm + 1)
                nc.vector.reciprocal(out[:, :], root[:, :]).then_inc(scale_ready, 1)
                dve.wait_ge(scale_ready, norm + 1)

            def fold_post(norm):
                for q in (6, 7):
                    if q == 6:
                        dve.wait_ge(squares_added, ADDED_BEFORE[norm] + 5)
                    else:
                        dve.wait_ge(vector_step, steps.all())
                    dve.wait_ge(squares_ready, 8 * SUMMED[norm] + q + 1)
                    tt(square_sum[:, :, :], square_sum[:, :, :], squares[:, q % 2, :, :], ALU.add
                       ).then_inc(vector_step, steps.one())
                dve.wait_ge(vector_step, steps.all())
                tt(square_sum[:, 0, :], square_sum[:, 0, :], square_sum[:, 1, :], ALU.add).then_inc(post_folded, 1)

            def scale_pair(y, q):
                tt(y[:, 2 * q:2 * q + 2, :], y[:, 2 * q:2 * q + 2, :], bcast(scale[:, :]), ALU.mult
                   ).then_inc(vector_step, steps.one())

            def add_pair(y, gain, q, before):
                dve.wait_ge(vector_step, steps.all(but=before))
                for k in range(2 * q, 2 * q + 2):
                    last = stt(x[:, k, :], y[:, k, :], P(gain, k), x[:, k, :], ALU.mult, ALU.add)
                last.then_inc(x_ready, 1)

            def pre_pair(norm, gain, q):
                dve.wait_ge(norm_hi, 2 * (8 * PRE[norm] + q + 1))
                for k in range(2 * q, 2 * q + 2):
                    last = low_half(h_split[:, k, T:2 * T], x[:, k, :], P(gain, k), h_split[:, k, 0:T])
                last.then_inc(h_ready, 1)

            dve.sem_inc(lo_ready, LO_CREDIT)
            dve.sem_inc(pair_combined, PAIR_CREDIT)
            dve.wait_ge(gains_loaded, 16)
            for q in range(8):
                if q % 2 == 0:
                    dve.wait_ge(x_loaded[q // 2], 16)
                pre_pair(N_PRE1, "norm_mix_pre", q)
                if q % 2:
                    split(Step(W1 + q // 2))
            split(Step(W1 + 4))
            dve.wait_ge(small_loaded, 32)

            def tap_b(j, k):
                if k == 0:
                    dve.wait_ge(glu_ready, j + 1)
                    dve.wait_ge(cleared, 3)
                for t in range(2 * j, 2 * j + 2):
                    weight = P("conv_b_w", 6 * k + t)
                    window = glu[:, t, k:k + T]
                    if k == 0:
                        ins = nc.vector.tensor_scalar(conv_b[:, t, :], window, weight, None, ALU.mult)
                    else:
                        dve.wait_ge(vector_step, steps.all(but=1))
                        ins = stt(conv_b[:, t, :], window, weight, conv_b[:, t, :], ALU.mult, ALU.add)
                    if (k, t) == (30, 2 * j + 1):
                        ins.then_inc(taps_done, 1)
                    else:
                        ins.then_inc(vector_step, steps.one())

            def chunk_end_1(c, o):
                kind, j = CHUNKS1[c]
                q, bank = Step(qW1 + c), 2 * (c % 2)
                if o == 4:
                    out = {"val": val_b, "gate": tanh_b, "b": b_gate, "c": c_gate, "v": conv_a}.get(kind)
                    if kind == "pool":
                        at_least(dve, pooled_ready, j)
                        out = pool_in[:, :, 16:16 + T]
                    else:
                        out = out[:, :, :]
                    combine(q, bank, out, by=pre_scale)
                if kind == "gate" and o == 6:
                    dve.wait_ge(tanh_ready, j + 1)
                    stt(glu[:, 2 * j:2 * j + 2, 30:30 + T], tanh_b[:, :, :], 1.0, val_b[:, :, :], ALU.add, ALU.mult
                        ).then_inc(glu_ready, 1)
                elif kind == "v" and o == 4:
                    combined(q)
                    tt(cv[:, :, 2:2 + T], c_gate[:, :, :], conv_a[:, :, :], ALU.mult).then_inc(cv_ready, 1)
                elif kind == "v" and o == 6:
                    for k in (1, 0):
                        for t in range(2):
                            dve.wait_ge(conv_a_started, 2 * j + t + 1)
                            if k == 0:
                                dve.wait_ge(vector_step, steps.all(but=1))
                            stt(conv_a[:, t, :], cv[:, t, k:k + T], P("conv_a_w", 6 * k + 2 * j + t),
                                conv_a[:, t, :], ALU.mult, ALU.add).then_inc(vector_step, steps.one())
                    dve.wait_ge(vector_step, steps.all())
                    tt(conv_a[:, :, :], conv_a[:, :, :], b_gate[:, :, :], ALU.mult).then_inc(a_mixed, 1)
                elif kind == "v" and o == 8:
                    dve.wait_ge(a_hi, j + 1)
                    tt(act_split[:, 2 * j:2 * j + 2, T:2 * T], conv_a[:, :, :],
                       act_split[:, 2 * j:2 * j + 2, 0:T].bitcast(f32), ALU.subtract).then_inc(a_split, 1)
                elif kind == "pool" and o in (4, 5):
                    if o == 4:
                        combined(q)
                        at_least(dve, pool_summed, j)
                    pool_tile(j, o - 4)

            def pool_tile(j, t):
                g = 2 * j + t
                source = pool_in[:, t, :]
                for s in range(g + 1):
                    w, out = 1 << s, pool_sum[:, s % 2, :]
                    dve.wait_ge(vector_step, steps.all())
                    tt(out[:, 2 * w - 1:16 + T], source[:, 2 * w - 1:16 + T],
                       source[:, w - 1:16 + T - w], ALU.add).then_inc(vector_step, steps.one())
                    source = out
                dve.wait_ge(vector_step, steps.all())
                w = 2 << g
                tt(pooled[:, t, 0:16], source[:, 16:32], K("pool_first", 16 * g, 16), ALU.mult
                   ).then_inc(vector_step, steps.one())
                stt(pooled[:, t, 16:T], source[:, 32:16 + T], 1 / w, pool_in[:, t, 32:16 + T],
                    ALU.mult, ALU.subtract).then_inc(vector_step, steps.one())
                dve.wait_ge(vector_step, steps.all(but=1))
                last = tt(pooled[:, t, 0:16], pooled[:, t, 0:16], pool_in[:, t, 16:32], ALU.subtract)
                if t:
                    last.then_inc(pooled_ready, 1)
                else:
                    last.then_inc(vector_step, steps.one())

            def layer_norm(n):
                if n == CENTER:
                    dve.wait_ge(mean_summed, 1)
                    for j in range(3):
                        pair = conv_b[:, 2 * j:2 * j + 2, :]
                        stt(pair, bcast(ps[:, 7, 0:T]), -1 / 768, pair, ALU.mult, ALU.add).then_inc(centered, 1)
                elif n == VAR_SCALE:
                    make_scale(N_LN)
                for j in range(3):
                    pair = conv_b[:, 2 * j:2 * j + 2, :]
                    if n == VAR_SCALE + j:
                        dve.wait_ge(ln_squared, j + 1)
                        tt(pair, pair, bcast(scale[:, :]), ALU.mult).then_inc(ln_scaled, 1)
                    if n == LN_SILU + j:
                        dve.wait_ge(ln_tanh, j + 1)
                        stt(pair, ln_squares[:, 2 * j:2 * j + 2, :], 1.0, pair, ALU.add, ALU.mult
                            ).then_inc(ln_silu, 1)
                    if n == LN_LO + j:
                        dve.wait_ge(b_hi, j + 1)
                        low_half(act_split[:, 6 + 2 * j:8 + 2 * j, T:2 * T], pair, 0.5,
                                 act_split[:, 6 + 2 * j:8 + 2 * j, 0:T]).then_inc(b_split, 1)

            def pool_end(j):
                dve.wait_ge(c_hi, 2 * j + 2)
                for t in range(2):
                    k = 2 * j + t
                    last = low_half(act_split[:, 12 + k, T:2 * T], ps[:, 2 + j, T * t:T * t + T], P("pool_scale", k),
                                    act_split[:, 12 + k, 0:T])
                last.then_inc(c_split, 1)

            def first_mixer(n):
                if n == 9:
                    make_scale(N_PRE1, pre_scale)
                ends_1(n, chunk_end_1)
                if 13 <= n < 13 + TAP_PIECES:
                    for m in range(62 * (n - 13) // TAP_PIECES, 62 * (n - 12) // TAP_PIECES):
                        tap_b(m // 31, m % 31)
                layer_norm(n)

            for n in range(4 * 17):
                if n > 4:
                    split(Step(W1 + n))
                first_mixer(n)

            def y_pair(g, q, bank, y, n):
                if g == 0:
                    combine(q, bank, y[:, 2 * n:2 * n + 2, :])
                    return
                combine(q, bank, scaled[:, n % 2, :, :])
                combined(q)
                tt(y[:, 2 * n:2 * n + 2, :], y[:, 2 * n:2 * n + 2, :], scaled[:, n % 2, :, :], ALU.add
                   ).then_inc(y_summed, 1)

            def out_product(n0, q0, pieces, g, y, before, between=lambda n: None, flip=0):
                for n in range(4 * pieces):
                    split(Step(n0 + n))
                    between(n0 + n)
                    before(n)
                    for c, r in out_ends(pieces, n):
                        y_pair(g, Step(q0 + 2 * c + r), 4 * ((c + flip) % 2) + 2 * r, y, 2 * c + r)

            def last_chunk(q0, g, y, next_piece=None, flip=0):
                if next_piece is not None:
                    for p in range(3):
                        split(Step(next_piece + p))
                for r in range(2):
                    y_pair(g, Step(q0 + 6 + r), 4 * (1 - flip) + 2 * r, y, 6 + r)

            def post_and_pre(post, y, post_gain, pre, pre_gain, next_piece):
                fold_post(post)
                make_scale(post)
                scale_pair(y, 0)
                for q in range(8):
                    add_pair(y, post_gain, q, before=0)
                    if q < 7:
                        scale_pair(y, q + 1)
                    if q in BOUNDARY_SPLITS:
                        split(Step(next_piece + BOUNDARY_SPLITS[q]))
                    pre_pair(pre, pre_gain, q)

            def first_pools(n):
                first_mixer(n)
                if n == O1 + 5:
                    pool_end(0)
                elif n == O1 + 9:
                    pool_end(1)

            out_product(O1, qO1, 8, 0, y, before=lambda p: None, between=first_pools, flip=1)
            last_chunk(qO1, 0, y, M1, flip=1)
            post_and_pre(N_POST1, y, "norm_mix_post", N_PREF1, "norm_ffn_pre", M1)

            def taps_ffn(chunk, r, half, out, last_signal):
                for k in (1, 0):
                    for t in range(2 * r, 2 * r + 2):
                        weight = P("conv_ffn_w", chunk.times(4).value(88 * k + 44 * half + t))
                        if k:
                            dve.wait_ge(conv_started, chunk.times(8).value(4 * half + t + 1))
                        else:
                            dve.wait_ge(vector_step, steps.all(but=1))
                        ins = stt(out[:, t, :], up_in[:, t, k:k + T], weight, out[:, t, :], ALU.mult, ALU.add)
                        if last_signal is not None and (k, t) == (0, 2 * r + 1):
                            ins.then_inc(last_signal, 1)
                        else:
                            ins.then_inc(vector_step, steps.one())

            def gate_end(q0, chunk, p):
                if p in (3, 4):
                    r = p - 3
                    combine(q0.plus(r), 2 * r, up_in[:, 2 * r:2 * r + 2, 2:2 + T], by=pre_scale)
                if p in (5, 6):
                    taps_ffn(chunk, p - 5, 0, gate_conv, conv_done)

            def at2(k):
                return slice(k, k + 2) if isinstance(k, int) else bass.ds(k, 2)

            def split_hidden(u, r, k, scale):
                dve.wait_ge(unit_hi, u + 1)
                low_half(act_split[:, at2(k), T:2 * T], gate_conv[:, 2 * r:2 * r + 2, :], scale,
                         act_split[:, at2(k), 0:T]).then_inc(unit_split, 1)

            def val_end(q0, chunk, first, p):
                if p in (3, 4):
                    r = p - 3
                    combine(q0.plus(2 + r), 4 + 2 * r, up_in[:, 2 * r:2 * r + 2, 2:2 + T], by=pre_scale)
                if p in (5, 6):
                    r = p - 5
                    taps_ffn(chunk, r, 1, val_conv, None)
                    dve.wait_ge(gate_ready, chunk.times(2).value(r + 1))
                    pair = slice(2 * r, 2 * r + 2)
                    stt(gate_conv[:, pair, :], gate_tanh[:, pair, :], 1.0, gate_conv[:, pair, :], ALU.add, ALU.mult
                        ).then_inc(vector_step, steps.one())
                    dve.wait_ge(vector_step, steps.all())
                    tt(gate_conv[:, pair, :], gate_conv[:, pair, :], val_conv[:, pair, :], ALU.mult
                       ).then_inc(units_ready, 1)
                if p in (7, 8):
                    r = p - 7
                    split_hidden(chunk.times(2).value(r), r, chunk.times(4).value(2 * r - 4 * first), 0.5)

            def up_chunks(g, first, i, before, skip=0):
                q0 = Step(qup1[g], i, 4)
                chunk = Step(first, i, 1)
                for p in range(16):
                    if p >= skip:
                        split(Step(up1[g] + p, i, 16))
                    if skip and p == 9:
                        make_scale(N_PREF1, pre_scale)
                    before(p)
                    gate_end(q0, chunk, p - 8)

            def down_end(g):
                def before(p):
                    if p in (3, 4):
                        y_pair(g, Step(qdown1[g] + 6 + p - 3), 4 + 2 * (p - 3), y, 6 + p - 3)
                return before

            dve.wait_ge(cleared, 4)
            first = 0
            for g, n in enumerate(GROUPS1):
                if g == 0:
                    up_chunks(0, 0, None, lambda p: None, skip=8)
                else:
                    up_chunks(g, first, None, down_end(g - 1))
                with dve.Fori(1, n) as i:
                    steps.enter(i, 1, 20)
                    up_chunks(g, first, i, lambda p: val_end(
                        Step(qup1[g] - 4, i, 4), Step(first - 1, i, 1), first, p))
                    steps.leave(n)
                out_product(down1[g], qdown1[g], 2 * n, g, y, before=lambda p: val_end(
                    Step(qup1[g] + 4 * (n - 1)), Step(first + n - 1), first, p))
                first += n
            last_chunk(qdown1[-1], 2, y, W2)
            post_and_pre(N_POSTF1, y, "norm_ffn_post", N_PRE2, "norm_mix_pre_2", W2)

            def gate_rows():
                combine(Step(qG2), 4, scaled[:, 0, 0:1, :], tiles=1, by=pre_scale)
                combined(Step(qG2))
                nc.vector.tensor_scalar(row_i[0:4, :], scaled[0:4, 0, 0, :], P("gate_bias", 0)[0:4, :], None, ALU.add
                                        ).then_inc(vector_step, steps.one())
                nc.vector.tensor_scalar(row_f[0:4, :], scaled[64:68, 0, 0, :], P("gate_bias", 1)[64:68, :], None,
                                        ALU.add).then_inc(rows_split, 1)
                dve.wait_ge(rows_split, 1)
                nc.vector.tensor_scalar(row_m[0:4, :], row_f[0:4, :], 0.0, None, ALU.min
                                        ).then_inc(vector_step, steps.one())

            def gate_sums():
                dve.wait_ge(row_step, 3)
                dve.wait_ge(vector_step, steps.all())
                tt(row_m[0:4, :], row_m[0:4, :], row_g[0:4, :], ALU.subtract).then_inc(vector_step, steps.one())
                dve.wait_ge(vector_step, steps.all())
                one = ones[0:4, 0:1].to_broadcast([4, T])
                nc.vector.tensor_tensor_scan(row_n[0:4, :], one, row_m[0:4, :], 0.0, ALU.mult, ALU.add
                                             ).then_inc(vector_step, steps.one())
                dve.wait_ge(vector_step, steps.all())
                tt(row_g[0:4, :], row_i[0:4, :], row_n[0:4, :], ALU.subtract).then_inc(vector_step, steps.one())
                dve.wait_ge(vector_step, steps.all())
                nc.vector.tensor_tensor_scan(row_m[0:4, :], one, row_g[0:4, :], 0.0, ALU.mult, ALU.max
                                             ).then_inc(vector_step, steps.one())
                dve.wait_ge(vector_step, steps.all())
                stt(row_n[0:4, :], row_n[0:4, :], -1.0, row_m[0:4, :], ALU.mult, ALU.subtract
                    ).then_inc(rows_ready, 1)

            def angles():
                turns, angle = scaled[:, 1, 0, :], cos[:, :]
                dve.wait_ge(pos_loaded, 16)
                nc.vector.tensor_copy(angle, pos_i[:, :]).then_inc(vector_step, steps.one())
                dve.wait_ge(vector_step, steps.all())
                nc.vector.tensor_scalar(angle, angle, K("inv_freq"), None, ALU.mult).then_inc(vector_step, steps.one())
                dve.wait_ge(vector_step, steps.all())
                nc.vector.tensor_scalar(turns, angle, 1 / (2 * math.pi), ROUND, ALU.mult, ALU.add
                                        ).then_inc(vector_step, steps.one())
                dve.wait_ge(vector_step, steps.all())
                nc.vector.tensor_scalar(turns, turns, ROUND, None, ALU.subtract).then_inc(vector_step, steps.one())
                for part in TURN_PARTS:
                    dve.wait_ge(vector_step, steps.all())
                    stt(angle, turns, -part, angle, ALU.mult, ALU.add).then_inc(vector_step, steps.one())
                dve.wait_ge(vector_step, steps.all())
                nc.vector.tensor_scalar(angle, angle, PI_BELOW, -PI_BELOW, ALU.min, ALU.max).then_inc(angle_ready, 1)

            def columns():
                dve.wait_ge(columns_summed, 1)
                nc.vector.tensor_copy(gcol[:, :, :].rearrange("p a t -> p (a t)"), ps[:, 6, 0:8]
                                      ).then_inc(columns_ready, 1)
                dve.wait_ge(columns_ready, 1)

            def chunk_end_2(c, o):
                kind, h = CHUNKS2[c]
                q, bank = Step(pair2(c)), 2 * (c % 2)
                is_k = int(kind in ("k", "ak"))
                if o == 4:
                    if kind in ("q", "k"):
                        at_least(dve, qk_convolved, 2 * h + is_k)
                        combine(q, bank, qk_in[:, :, 3:3 + T], by=pre_scale)
                    elif kind == "v":
                        at_least(dve, m_scored, h)
                        combine(q, bank, v_m[:, :, :], by=pre_scale)
                    elif kind == "o":
                        combine(q, bank, o_m[:, :, :], by=pre_scale)
                    else:
                        at_least(dve, a_scored, 2 * h)
                        combine(q, bank, {"aq": a_q, "ak": a_k, "av": a_v}[kind][:, :, :], by=pre_scale)
                elif o == 6 and kind in ("q", "k"):
                    out = (q_m, k_m)[is_k]
                    for k in (2, 1, 0):
                        for t in range(2):
                            if k == 2:
                                dve.wait_ge(qk_started, 4 * h + 2 * is_k + t + 1)
                            else:
                                dve.wait_ge(vector_step, steps.all(but=1))
                            ins = stt(out[:, t, :], qk_in[:, t, k:k + T], P("conv_w_2", 16 * k + 8 * is_k + 2 * h + t),
                                      out[:, t, :], ALU.mult, ALU.add)
                            if (k, t) == (0, 1):
                                ins.then_inc(qk_convolved, 1)
                            else:
                                ins.then_inc(vector_step, steps.one())
                elif o == 8 and kind in ("q", "k"):
                    out = (q_m, k_m)[is_k]
                    dve.wait_ge(qk_tanh, 2 * h + is_k + 1)
                    stt(out[:, :, :], squares[:, is_k, :, :], 1.0, out[:, :, :], ALU.add, ALU.mult
                        ).then_inc(qk_ready, 1)
                elif o == 5 and kind in ("aq", "ak"):
                    a = (a_q, a_k)[is_k]
                    combined(q)
                    dve.wait_ge(table_step, 3)
                    at_least(dve, rope_ready, 2 * h + is_k)
                    for lo_, hi_ in ((0, 64), (64, 0)):
                        for t in range(2):
                            tt(scaled[lo_:lo_ + 64, 0, t, :], a[hi_:hi_ + 64, t, :],
                               sin[hi_:hi_ + 64, :], ALU.mult).then_inc(vector_step, steps.one())
                    dve.wait_ge(vector_step, steps.all())
                    tt(a[:, :, :], a[:, :, :], bcast(cos[:, :]), ALU.mult).then_inc(vector_step, steps.one())
                    dve.wait_ge(vector_step, steps.all())
                    tt(a[:, :, :], a[:, :, :], scaled[:, 0, :, :], ALU.add).then_inc(rope_ready, 1)

            def mlstm(h, stage):
                if stage == 0:
                    if h == 0:
                        columns()
                    dve.wait_ge(rows_bcast, h + 1)
                    for s, cols, queries in ((0, slice(0, 256), slice(0, 256)), (1, slice(256, 384), slice(128, 256))):
                        last = nc.vector.tensor_scalar(decay[:, cols], ps[:, 7, queries], gcol[:, s, h:h + 1], 0.0,
                                                       ALU.subtract, ALU.max)
                    last.then_inc(decay_started, 1)
                elif stage == 1:
                    dve.wait_ge(decay_ready, h + 1)
                    for cols in (slice(0, 128), slice(256, 384)):
                        tt(decay[:, cols], decay[:, cols], K("keep", 0, 128), ALU.mult
                           ).then_inc(vector_step, steps.one())
                    dve.wait_ge(vector_step, steps.all())
                    dve.wait_ge(m_scored, h + 1)
                    at_least(dve, m_valued, h)
                    stt(s_ts[:, :], ps[:, 4, 0:384], 1 / 64, decay[:, :], ALU.mult, ALU.mult).then_inc(s_ts_ready, 1)
                elif stage == 2:
                    dve.wait_ge(den_ready, 2 * h + 2)
                    tt(den_m[:, 0, :], den_m[:, 0, :], den_m[:, 1, :], ALU.max).then_inc(vector_step, steps.one())
                    dve.wait_ge(vector_step, steps.all())
                    nc.vector.reciprocal(den_m[:, 0, :], den_m[:, 0, :]).then_inc(vector_step, steps.one())
                    dve.wait_ge(vector_step, steps.all())
                    tt(h_m[:, :, :], ps[:, 5, :].rearrange("p (a t) -> p a t", a=2), bcast(den_m[:, 0, :]), ALU.mult
                       ).then_inc(m_divided, 1)
                elif stage == 3:
                    make_scale(N_HEAD + h)
                    dve.wait_ge(m_squared, h + 1)
                    tt(h_m[:, :, :], h_m[:, :, :], bcast(scale[:, :]), ALU.mult).then_inc(vector_step, steps.one())
                    dve.wait_ge(o_ready, h + 1)
                    dve.wait_ge(vector_step, steps.all())
                    stt(h_m[:, :, :], o_m[:, :, :], 1.0, h_m[:, :, :], ALU.add, ALU.mult).then_inc(m_gated, 1)
                else:
                    dve.wait_ge(m_hi, 2 * h + 2)
                    for t in range(2):
                        last = low_half(act_split[:, 2 * h + t, T:2 * T], h_m[:, t, :], P("mlstm_norm_2", 2 * h + t),
                                        act_split[:, 2 * h + t, 0:T])
                    last.then_inc(m_split, 1)

            def attention(t, stage):
                if stage == 0:
                    factor = 128 ** -0.5
                    dve.wait_ge(a_scored, t + 1)
                    at_least(dve, prob_ready, t)
                    for cols in (slice(0, 128), slice(256, 384)):
                        stt(decay[:, cols], ps[:, 4, cols], factor, K("masked", 0, 128), ALU.mult, ALU.add
                            ).then_inc(vector_step, steps.one())
                    nc.vector.tensor_scalar(decay[:, 128:256], ps[:, 4, 128:256], factor, None, ALU.mult
                                            ).then_inc(vector_step, steps.one())
                    dve.wait_ge(vector_step, steps.all())
                    for half, cols in enumerate((slice(0, 128), slice(128, 384))):
                        nc.vector.reduce_max(a_stat[:, half:half + 1], decay[:, cols], AX.X
                                             ).then_inc(vector_step, steps.one())
                    dve.wait_ge(vector_step, steps.all())
                    nc.vector.tensor_scalar(a_stat[:, 2:4], a_stat[:, 0:2], -1.0, None, ALU.mult
                                            ).then_inc(a_max_ready, 1)
                elif stage == 1:
                    dve.wait_ge(a_exp_ready, 2 * t + 2)
                    at_least(dve, prob_turned, t)
                    nc.vector.reciprocal(a_stat[:, 6:8], a_stat[:, 4:6]).then_inc(vector_step, steps.one())
                    dve.wait_ge(vector_step, steps.all())
                    for half, cols in enumerate((slice(0, 128), slice(128, 384))):
                        last = nc.vector.tensor_scalar(s_ts[:, cols], decay[:, cols], a_stat[:, 6 + half:7 + half],
                                                       None, ALU.mult)
                    last.then_inc(prob_ready, 1)
                else:
                    dve.wait_ge(a_hi_2, t + 1)
                    tt(act_split[:, 8 + t, T:2 * T], ps[:, 7, 0:T], act_split[:, 8 + t, 0:T].bitcast(f32),
                       ALU.subtract).then_inc(a_split_2, 1)

            def second_mixer(n):
                ends_2(n, chunk_end_2)
                if n == 11:
                    gate_rows()
                elif n == 13:
                    gate_sums()
                elif n == 14:
                    angles()
                for h in range(4):
                    r = n - 16 * (h + 1)
                    if r in M_DVE:
                        mlstm(h, M_DVE.index(r))
                for j in range(4):
                    r = n - (64 + 12 * (j + 1))
                    for a in range(2):
                        if r in A_DVE[a]:
                            attention(2 * j + a, A_DVE[a].index(r))

            dve.wait_ge(cleared, 5)
            for n in range(7, 4 * 28):
                if n > 7:
                    split(Step(piece2(n)))
                else:
                    for p in range(2):
                        split(Step(G2 + p))
                    make_scale(N_PRE2, pre_scale)
                second_mixer(n)

            def merge_end(c, turn, o):
                q = turn.times(8).plus(qY2 + c)
                bank = 2 * (c % 2)
                if c < 4:
                    if o == 4:
                        combine(q, bank, (gate_pair, squares)[c // 2][:, c % 2, :, :], by=pre_scale)
                    return
                half, branch = c // 2 - 2, c % 2
                if o == 4:
                    out = scaled[:, branch, :, :]
                    if c == 6:
                        dve.wait_ge(merge_split, turn.times(2).value(1))
                    combine(q, bank, out)
                    combined(q)
                    dve.wait_ge(merge_tanh, turn.times(4).value(4))
                    stt(out, (gate_pair, squares)[half][:, branch, :, :], 1.0, out, ALU.add, ALU.mult
                        ).then_inc(vector_step, steps.one())
                    if branch:
                        dve.wait_ge(vector_step, steps.all())
                        tt(scaled[:, 0, :, :], scaled[:, 0, :, :], out, ALU.add).then_inc(merge_summed, 1)
                elif o == 6 and branch:
                    j = turn.times(2).plus(half)
                    dve.wait_ge(merge_hi, j.value(1))
                    low_half(merged[:, at2(j.times(2).value()), T:2 * T], scaled[:, 0, :, :], 0.5,
                             merged[:, at2(j.times(2).value()), 0:T]).then_inc(merge_split, 1)

            def merge_turn(i, before):
                for n in range(24):
                    split(Step(Y2 + n, i, 24))
                    before(n)
                    merge_ends(n, lambda c, o: merge_end(c, Step(0, i, 1), o))

            merge_turn(None, lambda n: second_mixer(112 + n))
            with dve.Fori(1, 4) as i:
                steps.enter(i, 1, 8)
                merge_turn(i, lambda n: merge_ends(24 + n, lambda c, o: merge_end(c, Step(-1, i, 1), o)))
                steps.leave(4)
            out_product(O2, qO2, 8, 0, y_2, flip=1,
                        before=lambda p: merge_ends(24 + p, lambda c, o: merge_end(c, Step(3), o)))
            last_chunk(qO2, 0, y_2, M2, flip=1)
            post_and_pre(N_POST2, y_2, "norm_mix_post_2", N_PREF2, "norm_ffn_pre_2", M2)

            def relu_end(g, c, p):
                if p in (4, 5):
                    split_hidden(22 + 8 * g + 2 * c + p - 4, p - 4, 4 * c + 2 * (p - 4), 1.0)
                if p in (3, 4):
                    r = p - 3
                    combine(Step(qM2 + 16 * g + 2 * c + r), 4 * (c % 2) + 2 * r, squares[:, r, :, :], by=pre_scale)
                    combined(Step(qM2 + 16 * g + 2 * c + r))
                    stt(gate_conv[:, 2 * r:2 * r + 2, :], squares[:, r, :, :], 0.0, squares[:, r, :, :],
                        ALU.max, ALU.mult).then_inc(units_ready, 1)

            for g in range(4):
                for c in range(4):
                    for p in range(8):
                        if g or c or p > 7:
                            split(Step(M2 + 64 * g + 8 * c + p))
                        if (g, c, p) == (0, 1, 1):
                            make_scale(N_PREF2, pre_scale)
                        if c:
                            relu_end(g, c - 1, p)
                        elif g and p in (3, 4):
                            y_pair(g - 1, Step(qM2 + 16 * g - 2 + p - 3), 4 + 2 * (p - 3), y, 6 + p - 3)
                out_product(M2 + 64 * g + 32, qM2 + 16 * g + 8, 8, g, y, before=lambda p: relu_end(g, 3, p))
            last_chunk(qM2 + 16 * 3 + 8, 3, y)
            fold_post(N_POSTF2)
            make_scale(N_POSTF2)
            scale_pair(y, POOL_PAIRS)
            for q in range(POOL_PAIRS, 8):
                if q < 7:
                    scale_pair(y, q + 1)
                add_pair(y, "norm_ffn_post_2", q, before=int(q < 7))


_WEIGHTS = ["w_in", "w_out", "w_up", "w_down", "w_in_2", "w_branch_m_2", "w_branch_a_2", "w_out_2",
            "w_up_2", "w_down_2"]


def pack_params(inputs):
    import numpy as np

    def columns(name):
        if name == "gate_bias":
            out = np.zeros((128, 2), np.float32)
            out[0:4, 0] = inputs["i_bias_2"][0]
            out[64:68, 1] = inputs["f_bias_2"][0]
            return out
        a = np.asarray(inputs[name][0])
        if name == "pool_w":
            return a.transpose(1, 0, 2).reshape(128, -1)
        return a.reshape(-1, 128).T

    return np.ascontiguousarray(np.concatenate([columns(name) for name, _ in PARAM_COLUMNS], 1), np.float32)


def constants():
    import numpy as np

    p, one = np.arange(128), np.ones((128, 128), np.float32)
    select = np.zeros((128, 4, 128), np.float32)
    for h in range(4):
        select[h, h] = 1
    first = np.array([[1 / min(t + 1, w) for t in range(16)] for w in (2, 4, 8, 16)], np.float32).reshape(1, 64)
    column = {
        "identity": np.eye(128), "ones": one,
        "keep": np.triu(one),
        "masked": np.triu(one, 1) * np.float32(-1e38),
        "select": select.reshape(128, -1),
        "pool_first": np.repeat(first, 128, 0),
        "inv_freq": (np.float32(1) / np.float32(10000) ** ((2 * (p % 64)).astype(np.float32) / np.float32(128))
                     )[:, None],
        "epsilon": np.repeat(np.array([[1e-6, 1e-5, 4e-6]]), 128, 0),
        "half_pi": np.full((128, 1), np.pi / 2), "sign": np.where(p < 64, 1, -1)[:, None],
    }
    return np.ascontiguousarray(np.concatenate([column[n] for n, _ in CONST_COLUMNS], 1), np.float32)


def kernel(**inputs):
    import concourse.bacc as bacc
    import numpy as np
    from concourse import mybir
    from concourse.bass_utils import run_bass_kernel_spmd

    nc = bacc.Bacc("TRN2", target_bir_lowering=False, num_devices=1)
    arrays = {
        "xT": np.ascontiguousarray(np.asarray(inputs["x"])[0].reshape(256, 16, 128).transpose(2, 1, 0)),
        "params": pack_params(inputs), "consts": constants(),
        "positions": np.ascontiguousarray(inputs["positions_2"]).astype(np.int32),
    }
    for name in _WEIGHTS:
        arrays[name] = np.ascontiguousarray(inputs[name][0])
    aps = [nc.dram_tensor(name, a.shape, mybir.dt.from_np(a.dtype), kind="ExternalInput").ap()
           for name, a in arrays.items()]
    out = nc.dram_tensor("outT", (128, 16, 256), mybir.dt.float32, kind="ExternalOutput").ap()
    build(nc, *aps, out)
    result = run_bass_kernel_spmd(nc, [arrays], core_ids=[0]).results[0]["outT"]
    return result.transpose(2, 1, 0).reshape(1, 256, 2048)
```
